# Optimizing a Trainium2 kernel written in Bass

```python
import math
import jax, jax.numpy as jnp
from jax import lax
import numpy as np

D_MODEL = 1024
BATCH = 1
SEQ = 256
DEPTH = 2

N_EVEN = (DEPTH + 1) // 2
N_ODD = DEPTH // 2
GROUP_WIDTH = D_MODEL // 2

RET_HEADS = 4
RET_HEAD_DIM = GROUP_WIDTH // RET_HEADS
RET_W = RET_HEADS * RET_HEAD_DIM
RET_THETA = 10000.0
DIFF_HEADS = 4
DIFF_HEAD_DIM = GROUP_WIDTH // (2 * DIFF_HEADS)
DIFF_V_DIM = 2 * DIFF_HEAD_DIM
DIFF_QK_W = 2 * DIFF_HEADS * DIFF_HEAD_DIM
DIFF_V_W = DIFF_HEADS * DIFF_V_DIM
ROPE_THETA = 500000.0
DIFF_ROT_DIM = DIFF_HEAD_DIM // 4
MLA_HEADS = 4
MLA_Q_RANK = 256
MLA_KV_RANK = 128
MLA_NOPE = 64
MLA_ROPE = 32
MLA_V = GROUP_WIDTH // MLA_HEADS
GLA_HEADS = 4
GLA_K_DIM = GROUP_WIDTH // 2 // GLA_HEADS
GLA_V_DIM = GROUP_WIDTH // GLA_HEADS
GLA_K_W = GLA_HEADS * GLA_K_DIM
GLA_V_W = GLA_HEADS * GLA_V_DIM
GLA_GATE_RANK = 16
GLA_TAU = 16.0
CHUNK = 64
Q_BLOCK = 128
N_GROUPS = 4
EXPERTS_PER_GROUP = 8
N_EXPERTS = N_GROUPS * EXPERTS_PER_GROUP
TOP_K_IN_GROUP = 2
D_EXPERT = 512
MOE_BLOCK = 128
ALPHA = (2.0 * DEPTH) ** 0.25
BETA = (8.0 * DEPTH) ** -0.25
LN_EPS = 1e-5

EVEN_SPLITS = (RET_W, RET_W, RET_W, RET_W, DIFF_QK_W, DIFF_QK_W, DIFF_V_W)
EVEN_VALUE_BLOCKS = (2, 6)
EVEN_IN = sum(EVEN_SPLITS)
ODD_SPLITS = (MLA_Q_RANK, MLA_KV_RANK, MLA_ROPE, GLA_K_W, GLA_K_W, GLA_V_W, GLA_V_W, GLA_GATE_RANK, GLA_GATE_RANK)
ODD_VALUE_BLOCKS = (5,)
ODD_IN = sum(ODD_SPLITS)


F32 = jnp.float32

def _split(z, sizes):
    return jnp.split(z, np.cumsum(sizes)[:-1].tolist(), axis=-1)

def _heads(z, h):
    b, t, _ = z.shape
    return z.reshape(b, t, h, -1).transpose(0, 2, 1, 3)

def _merge(z):
    b, h, t, d = z.shape
    return z.transpose(0, 2, 1, 3).reshape(b, t, h * d)

def _layer_norm(x, g, b):
    xf = x.astype(F32)
    mu = jnp.mean(xf, -1, keepdims=True)
    var = jnp.mean(jnp.square(xf - mu), -1, keepdims=True)
    return ((xf - mu) * lax.rsqrt(var + LN_EPS) * g + b).astype(x.dtype)

def _group_norm(z):
    zf = z.astype(F32)
    mu = jnp.mean(zf, -1, keepdims=True)
    var = jnp.mean(jnp.square(zf - mu), -1, keepdims=True)
    return ((zf - mu) * lax.rsqrt(var + LN_EPS)).astype(z.dtype)

def _rms_norm(z, g):
    zf = z.astype(F32)
    return (zf * lax.rsqrt(jnp.mean(jnp.square(zf), -1, keepdims=True) + 1e-6) * g).astype(z.dtype)

def _rotary(x, rot_dim, theta):
    t = x.shape[2]
    half = rot_dim // 2
    pos = jnp.arange(t, dtype=F32)
    inv = jnp.power(jnp.float32(theta), -jnp.arange(0, rot_dim, 2, dtype=F32) / rot_dim)
    ang = pos[:, None] * inv[None, :]
    cos, sin = jnp.cos(ang), jnp.sin(ang)
    xr = x[..., :rot_dim].astype(F32)
    x1, x2 = xr[..., :half], xr[..., half:]
    rot = jnp.concatenate([x1 * cos - x2 * sin, x2 * cos + x1 * sin], -1).astype(x.dtype)
    return jnp.concatenate([rot, x[..., rot_dim:]], -1)

def _chunk_scan(q, k, v, log_a, strict):
    b, h, t, dk = q.shape
    dv = v.shape[-1]
    n = t // CHUNK

    def chunks(z):
        return z.reshape(b, h, n, CHUNK, z.shape[-1]).transpose(2, 0, 1, 3, 4)

    cum = jnp.cumsum(chunks(log_a.astype(F32)), axis=3)
    mask = jnp.tril(jnp.ones((CHUNK, CHUNK), bool), -1 if strict else 0)[None, None, :, :, None]

    def step(state, inp):
        qi, ki, vi, bi = inp
        qi, ki, vi = qi.astype(F32), ki.astype(F32), vi.astype(F32)
        o_inter = jnp.einsum('bhck,bhkv->bhcv', qi * jnp.exp(bi), state)
        diff = bi[:, :, :, None, :] - bi[:, :, None, :, :]
        decay = jnp.where(mask, jnp.exp(jnp.where(mask, diff, 0.0)), 0.0)
        scores = jnp.sum(qi[:, :, :, None, :] * ki[:, :, None, :, :] * decay, axis=-1)
        o_intra = jnp.einsum('bhij,bhjv->bhiv', scores, vi)
        b_last = bi[:, :, -1:, :]
        state = jnp.exp(b_last[:, :, 0, :, None]) * state + jnp.einsum('bhck,bhcv->bhkv', ki * jnp.exp(b_last - bi), vi)
        return state, o_inter + o_intra

    state0 = jnp.zeros((b, h, dk, dv), F32)
    _, o = lax.scan(step, state0, (chunks(q), chunks(k), chunks(v), cum))
    return o.transpose(1, 2, 0, 3, 4).reshape(b, h, t, dv).astype(v.dtype)

def _bidirectional_scan(q, k, v, log_a_fwd, log_a_bwd):
    rev = lambda z: jnp.flip(z, axis=2)
    fwd = _chunk_scan(q, k, v, log_a_fwd, strict=False)
    bwd = rev(_chunk_scan(rev(q), rev(k), rev(v), rev(log_a_bwd), strict=True))
    return fwd + bwd

def _query_blocks(z):
    b, h, t, d = z.shape
    return z.reshape(b, h, t // Q_BLOCK, Q_BLOCK, d).transpose(2, 0, 1, 3, 4)

def _unblock(o):
    nb, b, h, qb, d = o.shape
    return o.transpose(1, 2, 0, 3, 4).reshape(b, h, nb * qb, d)

def _blocked_attention(q, k, v, scale):
    def one(qi):
        s = jnp.einsum('bhqd,bhkd->bhqk', qi, k).astype(F32) * scale
        p = jax.nn.softmax(s, axis=-1)
        return jnp.einsum('bhqk,bhkd->bhqd', p.astype(v.dtype), v)
    return _unblock(lax.map(one, _query_blocks(q)))

def _blocked_diff_attention(q1, q2, k1, k2, v, lam, scale):
    def one(qs):
        qa, qb = qs
        p1 = jax.nn.softmax(jnp.einsum('bhqd,bhkd->bhqk', qa, k1).astype(F32) * scale, axis=-1)
        p2 = jax.nn.softmax(jnp.einsum('bhqd,bhkd->bhqk', qb, k2).astype(F32) * scale, axis=-1)
        return jnp.einsum('bhqk,bhkd->bhqd', (p1 - lam * p2).astype(v.dtype), v)
    return _unblock(lax.map(one, (_query_blocks(q1), _query_blocks(q2))))

def _retention_diff_mixer(x, w_in, ret_decay_f, ret_decay_b, lq1, lk1, lq2, lk2, subln, w_out, layer_idx):
    rq, rk, rv, rg, dq, dk, dv = _split(x @ w_in, EVEN_SPLITS)
    b, t, _ = x.shape
    q = _rotary(_heads(rq, RET_HEADS), RET_HEAD_DIM, RET_THETA)
    k = _rotary(_heads(rk, RET_HEADS), RET_HEAD_DIM, RET_THETA) * (RET_HEAD_DIM ** -0.5)
    v = _heads(rv, RET_HEADS)
    la_f = jnp.broadcast_to((-jnp.exp(ret_decay_f.astype(F32)))[None, :, None, None], (b, RET_HEADS, t, 1))
    la_b = jnp.broadcast_to((-jnp.exp(ret_decay_b.astype(F32)))[None, :, None, None], (b, RET_HEADS, t, 1))
    ret = _merge(_group_norm(_bidirectional_scan(q, k, v, la_f, la_b))) * jax.nn.silu(rg)
    def pair(z):
        z = z.reshape(b, t, DIFF_HEADS, 2, DIFF_HEAD_DIM).transpose(0, 2, 3, 1, 4)
        return (_rotary(z[:, :, 0], DIFF_ROT_DIM, ROPE_THETA), _rotary(z[:, :, 1], DIFF_ROT_DIM, ROPE_THETA))
    q1, q2 = pair(dq)
    k1, k2 = pair(dk)
    vv = _heads(dv, DIFF_HEADS)
    lam_init = 0.8 - 0.6 * math.exp(-0.3 * layer_idx)
    lam = (jnp.exp(jnp.sum(lq1 * lk1)) - jnp.exp(jnp.sum(lq2 * lk2))).astype(F32) + lam_init
    o = _blocked_diff_attention(q1, q2, k1, k2, vv, lam, DIFF_HEAD_DIM ** -0.5)
    diff = _merge(_rms_norm(o, subln) * (1.0 - lam_init))
    return jnp.concatenate([ret, diff], axis=-1) @ w_out

def _mla_gla_mixer(x, w_in, q_norm, w_uq, kv_norm, w_ukv, gla_w2_f, gla_b_f, gla_w2_b, gla_b_b, gla_norm, w_out):
    cq, ckv, krope, gq, gk, gv, gg, lr_f, lr_b = _split(x @ w_in, ODD_SPLITS)
    qh = _heads(_rms_norm(cq, q_norm) @ w_uq, MLA_HEADS)
    q = jnp.concatenate([qh[..., :MLA_NOPE], _rotary(qh[..., MLA_NOPE:], MLA_ROPE, ROPE_THETA)], -1)
    kvh = _heads(_rms_norm(ckv, kv_norm) @ w_ukv, MLA_HEADS)
    k_nope, v = kvh[..., :MLA_NOPE], kvh[..., MLA_NOPE:]
    k_rope = _rotary(krope[:, None], MLA_ROPE, ROPE_THETA)
    k = jnp.concatenate([k_nope, jnp.broadcast_to(k_rope, k_nope.shape[:-1] + (MLA_ROPE,))], -1)
    mla = _merge(_blocked_attention(q, k, v, (MLA_NOPE + MLA_ROPE) ** -0.5))
    def log_gate(lr, w2, bias):
        return _heads(jax.nn.log_sigmoid((lr @ w2 + bias).astype(F32)) / GLA_TAU, GLA_HEADS)
    gq_h = _heads(gq, GLA_HEADS) * (GLA_K_DIM ** -0.5)
    o = _bidirectional_scan(gq_h, _heads(gk, GLA_HEADS), _heads(gv, GLA_HEADS), log_gate(lr_f, gla_w2_f, gla_b_f), log_gate(lr_b, gla_w2_b, gla_b_b))
    gla = _merge(_rms_norm(o, gla_norm)) * jax.nn.silu(gg)
    return jnp.concatenate([mla, gla], axis=-1) @ w_out

def _hier_moe(x, w_grp, b_grp, w_exp, b_exp, w_gate, w_up, w_down):
    b, t, d = x.shape
    n = b * t
    xf = x.reshape(n, d)
    grp_logits = (xf @ w_grp + b_grp).astype(F32)
    g_idx = jnp.argmax(grp_logits, axis=-1).astype(jnp.int32)
    p_grp = jnp.take_along_axis(jax.nn.softmax(grp_logits, -1), g_idx[:, None], axis=1)[:, 0]
    exp_logits = (xf @ w_exp + b_exp).astype(F32).reshape(n, N_GROUPS, EXPERTS_PER_GROUP)
    in_grp = jnp.take_along_axis(exp_logits, g_idx[:, None, None], axis=1)[:, 0]
    top_l, top_e = lax.top_k(in_grp, TOP_K_IN_GROUP)
    gate = p_grp[:, None] * jax.nn.softmax(top_l, axis=-1)
    eid = (g_idx[:, None] * EXPERTS_PER_GROUP + top_e).reshape(-1).astype(jnp.int32)
    tok = jnp.repeat(jnp.arange(n, dtype=jnp.int32), TOP_K_IN_GROUP)
    gw = gate.reshape(-1)
    a = eid.shape[0]
    order = jnp.argsort(eid)
    eid_s, tok_s, gw_s = eid[order], tok[order], gw[order]
    counts = jnp.bincount(eid, length=N_EXPERTS).astype(jnp.int32)
    padded = (counts + MOE_BLOCK - 1) // MOE_BLOCK * MOE_BLOCK
    start = jnp.cumsum(counts) - counts
    pend = jnp.cumsum(padded)
    pstart = pend - padded
    dest = pstart[eid_s] + (jnp.arange(a, dtype=jnp.int32) - start[eid_s])
    cap = a + N_EXPERTS * MOE_BLOCK
    nb = cap // MOE_BLOCK
    buf_tok = jnp.full((cap,), n, jnp.int32).at[dest].set(tok_s)
    buf_w = jnp.zeros((cap,), F32).at[dest].set(gw_s)
    blk_e = jnp.minimum(jnp.searchsorted(pend, jnp.arange(nb, dtype=jnp.int32) * MOE_BLOCK, side='right'), N_EXPERTS - 1).astype(jnp.int32)
    x_pad = jnp.concatenate([xf, jnp.zeros((1, d), xf.dtype)], axis=0)

    def expert_block(args):
        idx, e = args
        xb = x_pad[idx]
        hdn = jax.nn.silu(xb @ w_gate[e]) * (xb @ w_up[e])
        return hdn @ w_down[e]

    y = lax.map(expert_block, (buf_tok.reshape(nb, MOE_BLOCK), blk_e)).reshape(cap, d)
    out = jnp.zeros((n + 1, d), x.dtype).at[buf_tok].add(y * buf_w[:, None].astype(y.dtype))
    return out[:n].reshape(b, t, d)

def first_inputs(seed: int = 0) -> dict:
    key = jax.random.key(seed)
    ks = iter(jax.random.split(key, 40))

    def nrm(shape, scale):
        return jax.random.normal(next(ks), shape, jnp.float32) * scale

    def gain(shape):
        return 1.0 + nrm(shape, 0.02)

    ev_col = np.concatenate([np.full((w,), BETA if i in EVEN_VALUE_BLOCKS else 1.0, np.float32) for i, w in enumerate(EVEN_SPLITS)])
    od_col = np.concatenate([np.full((w,), BETA if i in ODD_VALUE_BLOCKS else 1.0, np.float32) for i, w in enumerate(ODD_SPLITS)])
    ukv_col = np.tile(np.concatenate([np.ones((MLA_NOPE,), np.float32), np.full((MLA_V,), BETA, np.float32)]), MLA_HEADS)
    gam = 1.0 - 2.0 ** (-5.0 - np.arange(RET_HEADS))
    ret_base = jnp.asarray(np.log(-np.log(gam)), jnp.float32)
    return {
        'x': nrm((BATCH, SEQ, D_MODEL), 1.0),
        'ev_w_in': nrm((N_EVEN, D_MODEL, EVEN_IN), D_MODEL ** -0.5) * jnp.asarray(ev_col),
        'ev_ret_decay_f': ret_base + nrm((N_EVEN, RET_HEADS), 0.05),
        'ev_ret_decay_b': ret_base + nrm((N_EVEN, RET_HEADS), 0.05),
        'ev_lq1': nrm((N_EVEN, DIFF_HEAD_DIM), 0.1),
        'ev_lk1': nrm((N_EVEN, DIFF_HEAD_DIM), 0.1),
        'ev_lq2': nrm((N_EVEN, DIFF_HEAD_DIM), 0.1),
        'ev_lk2': nrm((N_EVEN, DIFF_HEAD_DIM), 0.1),
        'ev_subln': gain((N_EVEN, DIFF_V_DIM)),
        'ev_w_out': nrm((N_EVEN, D_MODEL, D_MODEL), D_MODEL ** -0.5 * BETA),
        'od_w_in': nrm((N_ODD, D_MODEL, ODD_IN), D_MODEL ** -0.5) * jnp.asarray(od_col),
        'od_q_norm': gain((N_ODD, MLA_Q_RANK)),
        'od_w_uq': nrm((N_ODD, MLA_Q_RANK, MLA_HEADS * (MLA_NOPE + MLA_ROPE)), MLA_Q_RANK ** -0.5),
        'od_kv_norm': gain((N_ODD, MLA_KV_RANK)),
        'od_w_ukv': nrm((N_ODD, MLA_KV_RANK, MLA_HEADS * (MLA_NOPE + MLA_V)), MLA_KV_RANK ** -0.5) * jnp.asarray(ukv_col),
        'od_gla_w2_f': nrm((N_ODD, GLA_GATE_RANK, GLA_K_W), GLA_GATE_RANK ** -0.5),
        'od_gla_b_f': nrm((N_ODD, GLA_K_W), 0.5),
        'od_gla_w2_b': nrm((N_ODD, GLA_GATE_RANK, GLA_K_W), GLA_GATE_RANK ** -0.5),
        'od_gla_b_b': nrm((N_ODD, GLA_K_W), 0.5),
        'od_gla_norm': gain((N_ODD, GLA_V_DIM)),
        'od_w_out': nrm((N_ODD, D_MODEL, D_MODEL), D_MODEL ** -0.5 * BETA),
        'ln1_g': gain((DEPTH, D_MODEL)),
        'ln1_b': nrm((DEPTH, D_MODEL), 0.02),
        'ln2_g': gain((DEPTH, D_MODEL)),
        'ln2_b': nrm((DEPTH, D_MODEL), 0.02),
        'moe_w_grp': nrm((DEPTH, D_MODEL, N_GROUPS), D_MODEL ** -0.5),
        'moe_b_grp': nrm((DEPTH, N_GROUPS), 0.01),
        'moe_w_exp': nrm((DEPTH, D_MODEL, N_EXPERTS), D_MODEL ** -0.5),
        'moe_b_exp': nrm((DEPTH, N_EXPERTS), 0.01),
        'moe_w_gate': nrm((DEPTH, N_EXPERTS, D_MODEL, D_EXPERT), D_MODEL ** -0.5),
        'moe_w_up': nrm((DEPTH, N_EXPERTS, D_MODEL, D_EXPERT), D_MODEL ** -0.5 * BETA),
        'moe_w_down': nrm((DEPTH, N_EXPERTS, D_EXPERT, D_MODEL), D_EXPERT ** -0.5 * BETA),
    }

def first_block(x, ev_w_in, ev_ret_decay_f, ev_ret_decay_b, ev_lq1, ev_lk1, ev_lq2, ev_lk2, ev_subln, ev_w_out,
              od_w_in, od_q_norm, od_w_uq, od_kv_norm, od_w_ukv, od_gla_w2_f, od_gla_b_f, od_gla_w2_b, od_gla_b_b, od_gla_norm, od_w_out,
              ln1_g, ln1_b, ln2_g, ln2_b,
              moe_w_grp, moe_b_grp, moe_w_exp, moe_b_exp, moe_w_gate, moe_w_up, moe_w_down):
    for i in range(DEPTH):
        j = i // 2
        if i % 2 == 0:
            mix = _retention_diff_mixer(x, ev_w_in[j], ev_ret_decay_f[j], ev_ret_decay_b[j], ev_lq1[j], ev_lk1[j], ev_lq2[j], ev_lk2[j], ev_subln[j], ev_w_out[j], i)
        else:
            mix = _mla_gla_mixer(x, od_w_in[j], od_q_norm[j], od_w_uq[j], od_kv_norm[j], od_w_ukv[j], od_gla_w2_f[j], od_gla_b_f[j], od_gla_w2_b[j], od_gla_b_b[j], od_gla_norm[j], od_w_out[j])
        x = _layer_norm(ALPHA * x + mix, ln1_g[i], ln1_b[i])
        ffn = _hier_moe(x, moe_w_grp[i], moe_b_grp[i], moe_w_exp[i], moe_b_exp[i], moe_w_gate[i], moe_w_up[i], moe_w_down[i])
        x = _layer_norm(ALPHA * x + ffn, ln2_g[i], ln2_b[i])
    return x


D_MIX = D_MODEL
D_POOL = D_MIX // 2
D_HGRN = D_MIX - D_POOL
POOL_WINDOWS = (2, 4, 8, 16)
N_POOL_GROUPS = len(POOL_WINDOWS)
POOL_GROUP_DIM = D_POOL // N_POOL_GROUPS
HGRN_HEADS = 4
HGRN_HEAD_DIM = D_HGRN // HGRN_HEADS
D_IN = D_POOL + 4 * D_HGRN
D_FF = ((8 * D_MODEL // 3 + 127) // 128) * 128
ALPHA_2 = (2.0 * DEPTH) ** 0.25
BETA_2 = (8.0 * DEPTH) ** -0.25
RMS_EPS = 1e-6


def layer_norm(x, g, b):
    x32 = x.astype(jnp.float32)
    mu = jnp.mean(x32, axis=-1, keepdims=True)
    var = jnp.mean(jnp.square(x32 - mu), axis=-1, keepdims=True)
    y = (x32 - mu) * lax.rsqrt(var + LN_EPS) * g.astype(jnp.float32) + b.astype(jnp.float32)
    return y.astype(x.dtype)

def swiglu(x, w_gate, w_up, w_down):
    return (jax.nn.silu(x @ w_gate) * (x @ w_up)) @ w_down

def multiscale_pool(u, pool_w, pool_scale):
    B, S, _ = u.shape
    u32 = u.astype(jnp.float32).reshape(B, S, N_POOL_GROUPS, POOL_GROUP_DIM)
    c = jnp.cumsum(u32, axis=1)
    pos = jnp.arange(S)
    means = []
    for g, w in enumerate(POOL_WINDOWS):
        cg = c[:, :, g]
        lag = jnp.pad(cg, ((0, 0), (w, 0), (0, 0)))[:, :S]
        cnt = jnp.minimum(pos + 1, w).astype(jnp.float32)[None, :, None]
        means.append((cg - lag) / cnt)
    pooled = jnp.stack(means, axis=2) - u32
    y = jnp.einsum('bsgc,gcd->bsgd', pooled.astype(u.dtype), pool_w)
    return y.reshape(B, S, D_POOL) * pool_scale

def hgrn2_recurrence(q, f_raw, v, lb):
    B, S, _ = q.shape
    n = S // CHUNK
    log_f = jnp.logaddexp(jnp.log(lb), jnp.log1p(-lb) + jax.nn.log_sigmoid(f_raw))
    k = (1.0 - lb) * jax.nn.sigmoid(-f_raw)
    q = q * (HGRN_HEAD_DIM ** -0.5)

    def heads(t):
        return t.reshape(B, n, CHUNK, HGRN_HEADS, HGRN_HEAD_DIM).transpose(1, 0, 3, 2, 4)

    causal = jnp.tril(jnp.ones((CHUNK, CHUNK), dtype=bool))[:, :, None]

    def step(state, inp):
        q_c, k_c, v_c, g_c = inp
        b = jnp.cumsum(g_c, axis=2)
        o_inter = jnp.einsum('bhtd,bhdv->bhtv', q_c * jnp.exp(b), state)
        rel = b[:, :, :, None, :] - b[:, :, None, :, :]
        decay = jnp.exp(jnp.where(causal, rel, -jnp.inf))
        scores = jnp.einsum('bhtd,bhsd,bhtsd->bhts', q_c, k_c, decay)
        o_intra = jnp.einsum('bhts,bhsv->bhtv', scores, v_c)
        b_last = b[:, :, -1:, :]
        k_dec = k_c * jnp.exp(b_last - b)
        new_state = jnp.exp(b_last[:, :, 0, :])[..., None] * state + jnp.einsum('bhsd,bhsv->bhdv', k_dec, v_c)
        return new_state, o_inter + o_intra

    s0 = jnp.zeros((B, HGRN_HEADS, HGRN_HEAD_DIM, HGRN_HEAD_DIM), jnp.float32)
    _, o = lax.scan(step, s0, (heads(q), heads(k), heads(v), heads(log_f)))
    return o.transpose(1, 0, 3, 2, 4).reshape(B, S, D_HGRN)

def head_rms_norm(o, g):
    B, S, _ = o.shape
    o = o.reshape(B, S, HGRN_HEADS, HGRN_HEAD_DIM)
    o = o * lax.rsqrt(jnp.mean(jnp.square(o), axis=-1, keepdims=True) + RMS_EPS) * g.astype(jnp.float32)
    return o.reshape(B, S, D_HGRN)

def second_inputs(seed: int = 0) -> dict:
    key = jax.random.key(seed)
    ks = jax.random.split(key, 16)
    nrm = jax.random.normal
    f32 = jnp.float32
    x = nrm(ks[0], (BATCH, SEQ, D_MODEL), f32)
    w_in = nrm(ks[1], (DEPTH, D_MODEL, D_IN), f32) * D_MODEL ** -0.5
    pool_w = nrm(ks[2], (DEPTH, N_POOL_GROUPS, POOL_GROUP_DIM, POOL_GROUP_DIM), f32) * POOL_GROUP_DIM ** -0.5
    pool_scale = 1.0 + 0.02 * nrm(ks[3], (DEPTH, D_POOL), f32)
    lb_param = 0.5 * nrm(ks[4], (DEPTH, D_HGRN), f32)
    hgrn_norm_g = 1.0 + 0.02 * nrm(ks[5], (DEPTH, HGRN_HEAD_DIM), f32)
    w_out = nrm(ks[6], (DEPTH, D_MIX, D_MODEL), f32) * (D_MIX ** -0.5 * BETA_2)
    ffn1_gate = nrm(ks[7], (DEPTH, D_MODEL, D_FF), f32) * D_MODEL ** -0.5
    ffn1_up = nrm(ks[8], (DEPTH, D_MODEL, D_FF), f32) * D_MODEL ** -0.5
    ffn1_down = nrm(ks[9], (DEPTH, D_FF, D_MODEL), f32) * (D_FF ** -0.5 * BETA_2)
    ffn2_gate = nrm(ks[10], (DEPTH, D_MODEL, D_FF), f32) * D_MODEL ** -0.5
    ffn2_up = nrm(ks[11], (DEPTH, D_MODEL, D_FF), f32) * D_MODEL ** -0.5
    ffn2_down = nrm(ks[12], (DEPTH, D_FF, D_MODEL), f32) * (D_FF ** -0.5 * BETA_2)
    ln_g = 1.0 + 0.02 * nrm(ks[13], (DEPTH, 3, D_MODEL), f32)
    ln_b = 0.02 * nrm(ks[14], (DEPTH, 3, D_MODEL), f32)
    return {"x": x, "w_in": w_in, "pool_w": pool_w, "pool_scale": pool_scale, "lb_param": lb_param,
            "hgrn_norm_g": hgrn_norm_g, "w_out": w_out, "ffn1_gate": ffn1_gate, "ffn1_up": ffn1_up,
            "ffn1_down": ffn1_down, "ffn2_gate": ffn2_gate, "ffn2_up": ffn2_up, "ffn2_down": ffn2_down,
            "ln_g": ln_g, "ln_b": ln_b}

def second_block(x, w_in, pool_w, pool_scale, lb_param, hgrn_norm_g, w_out, ffn1_gate, ffn1_up, ffn1_down,
              ffn2_gate, ffn2_up, ffn2_down, ln_g, ln_b):
    f32 = jnp.float32
    lb_all = jnp.cumsum(jax.nn.softmax(lb_param.astype(f32), axis=0), axis=0)
    lb_all = lb_all - lb_all[0:1]
    for l in range(DEPTH):
        x = layer_norm(ALPHA_2 * x + 0.5 * swiglu(x, ffn1_gate[l], ffn1_up[l], ffn1_down[l]), ln_g[l, 0], ln_b[l, 0])
        h = x @ w_in[l]
        u = h[..., :D_POOL]
        q, f_raw, v, g = jnp.split(h[..., D_POOL:], 4, axis=-1)
        y_pool = multiscale_pool(u, pool_w[l], pool_scale[l])
        o = hgrn2_recurrence(q.astype(f32), f_raw.astype(f32), v.astype(f32), lb_all[l])
        y_hgrn = head_rms_norm(o, hgrn_norm_g[l]) * jax.nn.silu(g.astype(f32))
        mix = jnp.concatenate([y_pool.astype(x.dtype), y_hgrn.astype(x.dtype)], axis=-1) @ w_out[l]
        x = layer_norm(ALPHA_2 * x + mix, ln_g[l, 1], ln_b[l, 1])
        x = layer_norm(ALPHA_2 * x + 0.5 * swiglu(x, ffn2_gate[l], ffn2_up[l], ffn2_down[l]), ln_g[l, 2], ln_b[l, 2])
    return x


def setup_inputs(seed=0):
    out = dict(first_inputs(seed))
    for name, value in second_inputs(seed + 1).items():
        if name != "x":
            out[name + "_2"] = value
    return out


def reference(
    x, ev_w_in, ev_ret_decay_f, ev_ret_decay_b, ev_lq1, ev_lk1, ev_lq2, ev_lk2, ev_subln,
    ev_w_out, od_w_in, od_q_norm, od_w_uq, od_kv_norm, od_w_ukv, od_gla_w2_f, od_gla_b_f,
    od_gla_w2_b, od_gla_b_b, od_gla_norm, od_w_out, ln1_g, ln1_b, ln2_g, ln2_b, moe_w_grp,
    moe_b_grp, moe_w_exp, moe_b_exp, moe_w_gate, moe_w_up, moe_w_down, w_in_2, pool_w_2,
    pool_scale_2, lb_param_2, hgrn_norm_g_2, w_out_2, ffn1_gate_2, ffn1_up_2, ffn1_down_2,
    ffn2_gate_2, ffn2_up_2, ffn2_down_2, ln_g_2, ln_b_2,
):
    x = first_block(
        x, ev_w_in, ev_ret_decay_f, ev_ret_decay_b, ev_lq1, ev_lk1, ev_lq2, ev_lk2, ev_subln,
        ev_w_out, od_w_in, od_q_norm, od_w_uq, od_kv_norm, od_w_ukv, od_gla_w2_f, od_gla_b_f,
        od_gla_w2_b, od_gla_b_b, od_gla_norm, od_w_out, ln1_g, ln1_b, ln2_g, ln2_b, moe_w_grp,
        moe_b_grp, moe_w_exp, moe_b_exp, moe_w_gate, moe_w_up, moe_w_down,
    )
    return second_block(
        x, w_in_2, pool_w_2, pool_scale_2, lb_param_2, hgrn_norm_g_2, w_out_2, ffn1_gate_2,
        ffn1_up_2, ffn1_down_2, ffn2_gate_2, ffn2_up_2, ffn2_down_2, ln_g_2, ln_b_2,
    )


_drawn_inputs = setup_inputs


def setup_inputs(seed=0):
    import zlib

    import numpy as np

    out = dict(_drawn_inputs(seed))
    spreads = {}
    factors = {'ev_lk1': 6.237,
     'ev_lq2': 6.317,
     'ev_lk2': 2.933,
     'ev_subln': 8.0,
     'od_q_norm': 8.0,
     'od_w_uq': 3.669,
     'od_kv_norm': 8.0,
     'od_gla_w2_f': 4.565,
     'od_gla_w2_b': 4.024,
     'od_gla_norm': 8.0,
     'moe_b_grp': 8.0,
     'moe_b_exp': 8.0,
     'pool_scale_2': 8.0,
     'hgrn_norm_g_2': 8.0}
    for name, (base, spread) in spreads.items():
        noise = np.random.default_rng([zlib.crc32(name.encode()), seed]).standard_normal(out[name].shape)
        drawn = base * np.exp(spread * noise) if base else spread * noise
        out[name] = __import__('jax').numpy.asarray(drawn.astype(out[name].dtype))
    for name, factor in factors.items():
        out[name] = (out[name] * factor).astype(out[name].dtype)
    return out
```

```python
from contextlib import ExitStack

import concourse.bass as bass
import numpy as np
from concourse import mybir

F32 = mybir.dt.float32
I32 = mybir.dt.int32
U8 = mybir.dt.uint8
ALU = mybir.AluOpType
ACT = mybir.ActivationFunctionType
AXX = mybir.AxisListType.X

P = 128
T = 256
NB = T // P
D = 1024
KT = D // P
BANK = 512
HEADS = 4
HD = 128
DIFF_D = 64
MLA_NOPE, MLA_ROPE, MLA_QR, MLA_KVR = 64, 32, 256, 128
MLA_QD = MLA_NOPE + MLA_ROPE
GATE_RANK = 16
GLA_TAU = 16.0
CHUNK = 64
N_GROUPS, PER_GROUP, N_EXPERTS = 4, 8, 32
D_EXPERT = 512
FT_E = D_EXPERT // P
D_FF = 2816
FT = D_FF // P
DEPTH = 2
ALPHA = (2.0 * DEPTH) ** 0.25
LN_EPS = 1e-5
RMS_EPS = 1e-6
LAM_INIT = 0.2
SLOT = 2048
RING = 9
CAP = 64
PAIR = 2
BIG = 1e30
WINDOWS = (2, 4, 8, 16)


def rotary_tables(rows, half, theta, width):
    pos = np.arange(T, dtype=np.float32)
    inv = np.power(np.float32(theta), -np.arange(0, 2 * half, 2, dtype=np.float32) / np.float32(2 * half)).astype(np.float32)
    ang = (pos[:, None] * inv[None, :]).astype(np.float32)
    cos = np.ones((rows, T), np.float32)
    sin = np.zeros((rows, T), np.float32)
    swap = np.zeros((rows, rows), np.float32)
    for r in range(rows):
        i = r % width
        if i < 2 * half:
            cos[r] = np.cos(ang[:, i % half])
            sin[r] = np.sin(ang[:, i % half]) * (-1.0 if i < half else 1.0)
            swap[r + half if i < half else r - half, r] = 1.0
    return cos, sin, swap


def constant_tables():
    parts = {}
    parts["ident"] = np.eye(P, dtype=np.float32)
    parts["ones"] = np.ones((P, P), np.float32)
    parts["earlier"] = np.triu(np.ones((P, P), np.float32), 1)
    parts["slot_no"] = np.tile(np.arange(CAP, dtype=np.float32), (P, 1))
    parts["desc_grp"] = np.tile(np.arange(N_GROUPS, 0, -1, dtype=np.float32), (P, 1))
    parts["desc_exp"] = np.tile(np.arange(N_EXPERTS, 0, -1, dtype=np.float32), (P, 1))
    parts["neg_half"] = np.full((P, 16), -0.5, np.float32)
    for name, half, theta, width in (("ret", 64, 10000.0, 128), ("dif", 8, 500000.0, 64)):
        c, s, w = rotary_tables(P, half, theta, width)
        parts[name + "_cos"], parts[name + "_sin"], parts[name + "_swap"] = c, s, w
    c, s, w = rotary_tables(MLA_ROPE, MLA_ROPE // 2, 500000.0, MLA_ROPE)
    at = slice(MLA_NOPE, MLA_QD)
    for key, v in (("mla_cos", c), ("mla_sin", s), ("mla_swap", w)):
        full = np.zeros((P, v.shape[1]), np.float32)
        full[at] = v
        parts[key] = full
    scan = np.ones((P, HEADS * T), np.float32)
    scan[:, ::CHUNK] = 0.0
    parts["scan"] = scan
    cols, at = {}, 0
    for key, v in parts.items():
        cols[key] = (at, v.shape[1])
        at += v.shape[1]
    return np.concatenate(list(parts.values()), axis=1), cols


def distance_tables():
    s = np.arange(P)[:, None, None] + P * np.arange(NB)[None, :, None]
    t = np.arange(T)[None, None, :]
    return np.stack([np.maximum(t - s, 0), np.maximum(s - t, 0)], axis=1).astype(np.float32)


def pool_tables():
    out = np.zeros((T, len(WINDOWS), T), np.float32)
    for g, w in enumerate(WINDOWS):
        for t in range(T):
            n = min(t + 1, w)
            out[t - n + 1:t + 1, g, t] = np.float32(1.0) / np.float32(n)
            out[t, g, t] -= 1.0
    return np.ascontiguousarray(out.reshape(NB, P, len(WINDOWS), T).transpose(1, 0, 2, 3))


LEVELS = tuple(range(7, 0, -1))


def level_masks():
    s, t = np.arange(P)[:, None], np.arange(P)[None, :]
    out = []
    for flip in (False, True):
        a, b = (t, s) if flip else (s, t)
        for m in LEVELS:
            n = 1 << m
            out.append((a // n == b // n) & (a % n < n // 2) & (b % n >= n // 2))
    out.append(s == t)
    return np.stack(out, axis=1).astype(np.float32)


class Step:

    def __init__(self, sem, count):
        self.sem, self.count = sem, count


class Queue:

    def __init__(self, sem):
        self.sem, self.count, self.met, self.items = sem, 0, {}, []

    def wait(self, step):
        if self.met.get(id(step.sem), 0) < step.count:
            self.met[id(step.sem)] = step.count
            self.items.append(("wait", step.sem, step.count))

    def do(self, emit, after=(), chain=True):
        for step in after:
            self.wait(step)
        if chain and self.count:
            self.wait(Step(self.sem, self.count))
        self.count += 1
        self.items.append(("run", emit, self.sem, 1))
        return Step(self.sem, self.count)

    def dma(self, out, in_, sem, count, after=()):
        for step in after:
            self.wait(step)
        self.items.append(("run", lambda e: e.dma_start(out, in_), sem, 16))
        return Step(sem, count)

    def play(self, engine):
        for kind, what, *rest in self.items:
            if kind == "wait":
                engine.wait_ge(what, rest[0])
            else:
                what(engine).then_inc(rest[0], rest[1])
        self.items = []


class Tiles:
    pass


class Bank:

    def __init__(self, tile):
        self.tile, self.free = tile, []


class Banks:

    def __init__(self, banks):
        self.banks, self.n = banks, 0

    def take(self):
        self.n += 1
        return self.banks[(self.n - 1) % len(self.banks)]


class Ring:

    def __init__(self, slots, sems, plan, queue):
        self.slots, self.sems, self.plan, self.queue = slots, sems, plan, queue
        self.asked, self.loaded, self.released = 0, 0, [None] * len(plan)

    def next(self, key):
        n = self.asked
        self.asked += 1
        assert self.plan[n][0] == key, (self.plan[n][0], key)
        src = self.plan[n][1]
        a, b = src.shape[1:]
        k = n % len(self.slots)
        view = self.slots[k][:, 0:a * b].rearrange("p (a b) -> p a b", a=a)
        return n, view, Step(self.sems[k], 16 * (n // len(self.slots) + 1))

    def release(self, n, step):
        self.released[n] = step

    def load(self):
        k = len(self.slots)
        while self.loaded < len(self.plan):
            n = self.loaded
            if n >= k and self.released[n - k] is None:
                break
            src = self.plan[n][1]
            a, b = src.shape[1:]
            dst = self.slots[n % k][:, 0:a * b].rearrange("p (a b) -> p a b", a=a)
            self.queue.dma(dst, src, self.sems[n % k], 16 * (n // k + 1), after=[self.released[n - k]] if n >= k else [])
            self.loaded += 1


class Engines:

    def __init__(self, new_sem, name):
        self.sems = []

        def sem(what):
            self.sems.append(new_sem(f"{name}_{what}"))
            return self.sems[-1]

        self.sem = sem
        self.pe, self.act, self.dve, self.pool, self.sp = (Queue(sem(w)) for w in ("pe_done", "act_done", "dve_done", "pool_done", "sp_done"))

    def play(self, nc, rings):
        for ring in rings:
            ring.load()
        with nc.Block(no_gpsimd_drain=True) as block:
            block.sync(self.sp.play)
            block.tensor(self.pe.play)
            block.scalar(self.act.play)
            block.vector(self.dve.play)
            block.gpsimd(self.pool.play)


class Arena:

    def __init__(self, tile, words):
        self.tile, self.words, self.at = tile, words, 0

    def restart(self):
        self.at = 0

    def take(self, *shape):
        n = int(np.prod(shape))
        assert self.at + n <= self.words, (self.at, n, self.words)
        v = self.tile[:, self.at:self.at + n]
        self.at += n
        if len(shape) == 2:
            v = v.rearrange("p (a b) -> p a b", a=shape[0])
        elif len(shape) == 3:
            v = v.rearrange("p (a b c) -> p a b c", a=shape[0], b=shape[1])
        return v


def product(q, bank, groups, after=()):

    def emit(e):
        for out, parts in groups:
            for i, (lhs, rhs) in enumerate(parts):
                ins = e.matmul(out, lhs, rhs, start=i == 0, stop=i == len(parts) - 1)
        return ins

    return q.pe.do(emit, after=list(bank.free) + list(after), chain=False)


def transposes(q, bank, ident, pairs, after=()):
    def emit(e):
        for out, in_ in pairs:
            ins = e.transpose(out, in_, ident)
        return ins

    return q.pe.do(emit, after=list(bank.free) + list(after), chain=False)


def bcast(ap, n):
    return ap.unsqueeze(ap.ndim).to_broadcast(list(ap.shape) + [n])


def mid_bcast(ap, n):
    return ap.unsqueeze(1).to_broadcast([ap.shape[0], n] + list(ap.shape[1:]))


def rows(w, k=KT):
    return w.rearrange("(p k) n -> p k n", k=k)


def tiled_rows(w):
    return w.rearrange("(k p) n -> p k n", p=P)


def moe_plan(A, layer):
    out = []
    for g in range(N_EXPERTS // PAIR):
        for name, per in (("gate", KT // 2), ("up", KT // 2), ("down", FT_E // 2)):
            w = A["moe_w_" + name]
            for half in range(2):
                for j in range(PAIR):
                    k = KT if name != "down" else FT_E
                    src = rows(w[layer, PAIR * g + j], k)[:, half * per:(half + 1) * per, :]
                    out.append(((name, g, half, j), src))
    return out


def weight_plan(A):
    plan = [(("ev_in", c), rows(A["ev_w_in"][0])[:, :, 256 * c:256 * c + 256]) for c in range(14)]
    plan += [(("ev_out", c), tiled_rows(A["ev_w_out"][0])[:, :, 256 * c:256 * c + 256]) for c in range(4)]
    plan += moe_plan(A, 0)
    for c, (a, b) in enumerate(OD_COLUMNS):
        plan.append((("od_in", c), rows(A["od_w_in"][0])[:, :, a:b]))
    plan += [(("od_out", c), tiled_rows(A["od_w_out"][0])[:, :, 256 * c:256 * c + 256]) for c in range(4)]
    plan += moe_plan(A, 1)
    for layer in range(DEPTH):
        plan += ffn_plan(A, layer, 1)
        plan += [(("in2", c), rows(A["w_in_2"][layer])[:, :, 256 * c:256 * c + 256]) for c in range(10)]
        plan += [(("out2", c), tiled_rows(A["w_out_2"][layer])[:, :, 256 * c:256 * c + 256]) for c in range(4)]
        plan += ffn_plan(A, layer, 2)
    return plan


def ffn_plan(A, layer, which):
    out = []
    lag = FFN_LAG // 2
    for c in range(FT // 2 + lag):
        if c < FT // 2:
            for name in ("gate", "up"):
                src = rows(A[f"ffn{which}_{name}_2"][layer])[:, :, 256 * c:256 * c + 256]
                out.append(((name, c), src))
        if c >= lag:
            d = c - lag
            out.append((("down", d), tiled_rows(A[f"ffn{which}_down_2"][layer])[:, 2 * d:2 * d + 2, :]))
    return out


FFN_LAG = 2
OD_COLUMNS = ((0, 256), (256, 416), (1952, 1984), (416, 672), (672, 928), (928, 1184), (1184, 1440), (1440, 1696), (1696, 1952))


def to_feature_major(k, q, after_block):
    done = []
    for tb in range(NB):
        for half in range(2):
            bank = k.banks.take()
            view = bank.tile[:, :].rearrange("p (k t) -> p k t", k=4)
            pairs = [(view[:, i, :], k.x_tok[:, tb, (4 * half + i)::KT]) for i in range(4)]
            step = transposes(q, bank, k.ident, pairs, after=[after_block[tb]] + k.xT_free)
            dst = k.xT[:, 4 * half:4 * half + 4, tb * P:(tb + 1) * P]
            if half == 0:
                got = q.act.do(lambda e, dst=dst, view=view: e.copy(dst, view), after=[step], chain=False)
            else:
                got = q.dve.do(lambda e, dst=dst, view=view: e.tensor_copy(dst, view), after=[step], chain=False)
            bank.free = [got]
            done.append(got)
    k.xT_ready = done
    k.xT_free = []


def load_norm(k, q, n):
    sem, free = k.norm_sem[n % 2], k.norm_free[n % 2]
    for i, row in enumerate(k.norm_rows[n]):
        q.pool.dma(k.norm_gb[n % 2][:, i, :], row.partition_broadcast(P), sem, 32 * (n // 2 + 1), after=free)


def layer_norm(k, q, after_block):
    n = k.norm_no
    k.norm_no += 1
    gb = k.norm_gb[n % 2]
    gb_here = Step(k.norm_sem[n % 2], 32 * (n // 2 + 1))
    block_done = []
    for tb in range(NB):
        for h in range(2):
            q.dve.do(lambda e, tb=tb, h=h: e.bn_stats(k.bn[:, tb, 6 * h:6 * h + 6], k.acc[:, tb, 512 * h:512 * h + 512]),
                     after=after_block[tb], chain=False)
        q.dve.do(lambda e, tb=tb: e.bn_aggr(k.mv[:, tb, :], k.bn[:, tb, :]))
        var = q.dve.do(lambda e, tb=tb: e.tensor_scalar(k.ve[:, tb:tb + 1], k.mv[:, tb, 1:2], LN_EPS, None, ALU.add))
        rstd = q.pool.do(lambda e, tb=tb: e.tensor_tensor(k.rstd[:, tb:tb + 1], k.ve[:, tb:tb + 1], k.neg_half[:, 0:1], ALU.pow),
                         after=[var])
        q.dve.do(lambda e, tb=tb: e.tensor_scalar(k.x_tok[:, tb, :], k.acc[:, tb, :], k.mv[:, tb, 0:1], k.rstd[:, tb:tb + 1],
                                                  ALU.subtract, ALU.mult), after=[rstd] + k.x_free)
        q.dve.do(lambda e, tb=tb: e.tensor_tensor(k.x_tok[:, tb, :], k.x_tok[:, tb, :], gb[:, 0, :], ALU.mult), after=[gb_here])
        block_done.append(q.dve.do(lambda e, tb=tb: e.tensor_tensor(k.x_tok[:, tb, :], k.x_tok[:, tb, :], gb[:, 1, :], ALU.add)))
    k.x_free = []
    k.norm_free[n % 2] = [block_done[-1]]
    if n + 2 < len(k.norm_rows):
        load_norm(k, q, n + 2)
    k.x_ready = block_done
    to_feature_major(k, q, block_done)


def project(k, q, key, parts):
    n, w, here = k.ring.next(key)
    bank = k.banks.take()
    groups = []
    for kind, c0, c1, *at in parts:
        if kind == "tok":
            for tb in range(NB):
                out = bank.tile[:, at[0] + tb * (c1 - c0):at[0] + (tb + 1) * (c1 - c0)]
                groups.append((out, [(k.xT[:, i, tb * P:(tb + 1) * P], w[:, i, c0:c1]) for i in range(KT)]))
        else:
            out = bank.tile[at[0]:at[0] + c1 - c0, at[1]:at[1] + T]
            groups.append((out, [(w[:, i, c0:c1], k.xT[:, i, :]) for i in range(KT)]))
    step = product(q, bank, groups, after=[here] + k.xT_ready)
    k.ring.release(n, step)
    return bank, step


FEAT2 = [("feat", 0, 128, 0, 0), ("feat", 128, 256, 0, T)]
TOK = [("tok", 0, 256, 0)]


def evacuate(k, q, bank, step, dst, src=None, scale=None, func=None, engine="act"):
    src = bank.tile[:, :] if src is None else src
    if func is None:
        func = ACT.Copy
    if engine == "act":
        got = q.act.do(lambda e, src=src, func=func: e.activation(dst, src, func, scale=1.0 if scale is None else scale), after=[step], chain=False)
    elif scale is None:
        got = q.dve.do(lambda e, src=src: e.tensor_copy(dst, src), after=[step], chain=False)
    else:
        got = q.dve.do(lambda e, src=src: e.tensor_scalar(dst, src, scale, None, ALU.mult), after=[step], chain=False)
    bank.free = [got]
    return got


def token_major(k, q, key, dst, func=None):
    bank, step = project(k, q, key, TOK)
    return evacuate(k, q, bank, step, dst, bank.tile[:, :].rearrange("p (a b) -> p a b", a=NB), func=func)


def rotate(k, q, raw, out, cos, sin, swap, after, at=slice(0, P)):
    bank = k.banks.take()
    view = bank.tile[at, :].rearrange("p (a b) -> p a b", a=2)
    swapped = product(q, bank, [(view[:, i, :], [(swap, raw[:, i, :])]) for i in range(2)], after=after)
    q.dve.do(lambda e: e.tensor_tensor(out, raw, mid_bcast(cos, 2), ALU.mult), after=after)
    tmp = k.rot_tmp[at, :].rearrange("p (a b) -> p a b", a=2)
    got = q.dve.do(lambda e: e.tensor_tensor(tmp, view, mid_bcast(sin, 2), ALU.mult), after=[swapped])
    bank.free = [got]
    return q.dve.do(lambda e: e.tensor_tensor(out, out, tmp, ALU.add))


def out_projection(k, q, name, mix_ready):
    done = []
    for c in range(4):
        n, w, here = k.ring.next((name, c))
        bank = k.banks.take()
        view = bank.tile[:, :].rearrange("p (a b) -> p a b", a=NB)
        groups = [(view[:, tb, :], [(k.mixT[:, i, tb * P:(tb + 1) * P], w[:, i, :]) for i in range(KT)]) for tb in range(NB)]
        step = product(q, bank, groups, after=[here] + mix_ready)
        k.ring.release(n, step)
        cols = slice(256 * c, 256 * c + 256)
        got = q.dve.do(lambda e, cols=cols, view=view: e.scalar_tensor_tensor(
            out=k.acc[:, :, cols], in0=k.x_tok[:, :, cols], scalar=ALPHA, in1=view, op0=ALU.mult, op1=ALU.add),
            after=[step] + k.x_ready, chain=False)
        bank.free = [got]
        done.append(got)
    return [done, done]


def mix_transposes(k, q, src, base, after):
    done = []
    for half in range(2):
        bank = k.banks.take()
        view = bank.tile[:, :].rearrange("p (i t) -> p i t", i=2)
        pairs = [(view[:, i, tb * P:(tb + 1) * P], src[:, tb, (2 * half + i) * P:(2 * half + i + 1) * P])
                 for i in range(2) for tb in range(NB)]
        step = transposes(q, bank, k.ident, pairs, after=after)
        dst = k.mixT[:, base + 2 * half:base + 2 * half + 2, :]
        done.append(evacuate(k, q, bank, step, dst, view, engine="act" if half else "dve"))
    return done


def sums_of_squares(k, q, banks, steps, groups, width, out):
    for b, (bank, step) in enumerate(zip(banks, steps)):
        for g in range(groups):
            got = q.act.do(lambda e, bank=bank, b=b, g=g: e.activation(
                k.junk[:, 0:width], bank[:, g * width:(g + 1) * width], ACT.Square,
                accum_out=out[:, b * groups + g:b * groups + g + 1]), after=[step])
    return got


def rms_scale(k, q, sums, n, width, eps, after):
    a = q.dve.do(lambda e: e.tensor_scalar(sums[:, 0:n], sums[:, 0:n], 1.0 / width, eps, ALU.mult, ALU.add), after=[after])
    return q.pool.do(lambda e: e.tensor_tensor(sums[:, 0:n], sums[:, 0:n], k.neg_half[:, 0:n], ALU.pow), after=[a])


def softmax_rows(k, q, bank, step, e_out, scale, tag):
    view = bank.tile[:, :].rearrange("p (a b) -> p a b", a=NB)
    q.dve.do(lambda e: e.tensor_reduce(tag[:, 0:2], view, AXX, ALU.max), after=[step] + k.soft_free)
    neg = q.dve.do(lambda e: e.tensor_scalar(tag[:, 2:4], tag[:, 0:2], -scale, None, ALU.mult))
    for b in range(NB):
        got = q.act.do(lambda e, b=b: e.activation(e_out[:, b, :], view[:, b, :], ACT.Exp, bias=tag[:, 2 + b:3 + b], scale=scale,
                                                   accum_out=tag[:, 4 + b:5 + b]), after=[neg] + k.soft_free)
    bank.free = [got]
    return got


def retention_diff_mixer(k, q):
    A = k.arena
    A.restart()
    qk_raw, qk = A.take(2, T), {}
    for name in ("rq", "rk"):
        qk[name] = A.take(HEADS, T)
    v, gate = A.take(NB, 512), A.take(NB, 512)
    decay, scores = A.take(NB, T), A.take(NB, T)
    raw_free = []

    def rotated(c0, name, which):
        nonlocal raw_free
        for pair in range(2):
            bank, step = project(k, q, ("ev_in", c0 + pair), FEAT2)
            q.act.wait(step)
            for s in raw_free:
                q.act.wait(s)
            got = evacuate(k, q, bank, step, qk_raw, bank.tile[:, :].rearrange("p (a b) -> p a b", a=2))
            done = rotate(k, q, qk_raw, qk[name][:, 2 * pair:2 * pair + 2, :], k.tab(which + "_cos"), k.tab(which + "_sin"),
                          k.tab(which + "_swap"), [got])
            raw_free = [done]
        return done

    q.act.do(lambda e: e.activation(k.neg_rate[:, :], k.ret_decay[:, :], ACT.Exp), after=[k.params])
    rates = q.dve.do(lambda e: e.tensor_scalar(k.neg_rate[:, :], k.neg_rate[:, :], -1.0, None, ALU.mult),
                     after=[Step(q.act.sem, q.act.count)])
    rq = rotated(0, "rq", "ret")
    rk = rotated(2, "rk", "ret")
    for c in range(2):
        rv = token_major(k, q, ("ev_in", 4 + c), v[:, :, 256 * c:256 * c + 256])
    for c in range(2):
        rg = token_major(k, q, ("ev_in", 6 + c), gate[:, :, 256 * c:256 * c + 256], func=ACT.Silu)

    o_banks = [k.banks.take() for _ in range(NB)]
    o_step = [None] * NB
    scores_free = []
    for h in range(HEADS):
        q.dve.do(lambda e, h=h: e.tensor_scalar(decay, k.distance[:, 0, :, :], k.neg_rate[:, h:h + 1], None, ALU.mult),
                 after=[rates, k.distance_here])
        arg = q.dve.do(lambda e, h=h: e.scalar_tensor_tensor(out=decay, in0=k.distance[:, 1, :, :], scalar=k.neg_rate[:, HEADS + h:HEADS + h + 1],
                                                             in1=decay, op0=ALU.mult, op1=ALU.add))
        dec = q.act.do(lambda e: e.activation(decay, decay, ACT.Exp), after=[arg])
        bank = k.banks_b.take()
        view = bank.tile[:, :].rearrange("p (a b) -> p a b", a=NB)
        step = product(q, bank, [(view[:, sb, :], [(qk["rk"][:, h, sb * P:(sb + 1) * P], qk["rq"][:, h, :])]) for sb in range(NB)],
                       after=[rq, rk])
        got = q.dve.do(lambda e, view=view: e.scalar_tensor_tensor(out=scores, in0=view, scalar=HD ** -0.5, in1=decay,
                                                                   op0=ALU.mult, op1=ALU.mult), after=[step, dec] + scores_free)
        bank.free = [got]
        for tb in range(NB):
            out = o_banks[tb].tile[:, h * HD:(h + 1) * HD]
            o_step[tb] = product(q, o_banks[tb], [(out, [(scores[:, sb, tb * P:(tb + 1) * P], v[:, sb, h * HD:(h + 1) * HD])
                                                        for sb in range(NB)])], after=[got, rv])
        scores_free = [o_step[1]]
    y = k.acc
    for tb in range(NB):
        for h in range(HEADS):
            i = tb * HEADS + h
            q.dve.do(lambda e, tb=tb, h=h, i=i, o_banks=o_banks: e.bn_stats(k.hbn[:, i, :], o_banks[tb].tile[:, h * HD:(h + 1) * HD]), after=[o_step[tb]])
            q.dve.do(lambda e, i=i: e.bn_aggr(k.hmv[:, i, :], k.hbn[:, i, :]))
    var = q.dve.do(lambda e: e.tensor_scalar(k.hrs[:, 0:8], k.hmv[:, :, 1], LN_EPS, None, ALU.add))
    rs = q.pool.do(lambda e: e.tensor_tensor(k.hrs[:, 0:8], k.hrs[:, 0:8], k.neg_half[:, 0:8], ALU.pow), after=[var])
    for tb in range(NB):
        for h in range(HEADS):
            i = tb * HEADS + h
            got = q.dve.do(lambda e, tb=tb, h=h, i=i, o_banks=o_banks: e.tensor_scalar(
                y[:, tb, h * HD:(h + 1) * HD], o_banks[tb].tile[:, h * HD:(h + 1) * HD], k.hmv[:, i, 0:1], k.hrs[:, i:i + 1],
                ALU.subtract, ALU.mult), after=[rs])
        o_banks[tb].free = [got]
    got = q.dve.do(lambda e: e.tensor_tensor(y[:, :, 0:512], y[:, :, 0:512], gate, ALU.mult), after=[rg])
    mix_a = mix_transposes(k, q, y, 0, [got])

    A.at = qk_words = 2 * T
    for name in ("dq", "dk"):
        qk[name] = A.take(HEADS, T)
    dv = A.take(NB, 512)
    e1, e2, pt = A.take(NB, T), A.take(NB, T), A.take(NB, T)
    dq = rotated(8, "dq", "dif")
    dk = rotated(10, "dk", "dif")
    for c in range(2):
        vr = token_major(k, q, ("ev_in", 12 + c), dv[:, :, 256 * c:256 * c + 256])
    lam = k.lam
    for i in range(2):
        q.dve.do(lambda e, i=i: e.tensor_tensor(k.lqk[:, 2 * i, :], k.lqk[:, 2 * i, :], k.lqk[:, 2 * i + 1, :], ALU.mult), after=[k.params])
        s = q.dve.do(lambda e, i=i: e.tensor_reduce(lam[:, i:i + 1], k.lqk[:, 2 * i, :], AXX, ALU.add))
    s = q.act.do(lambda e: e.activation(lam[:, 0:2], lam[:, 0:2], ACT.Exp), after=[s])
    q.dve.do(lambda e: e.tensor_tensor(lam[:, 2:3], lam[:, 1:2], lam[:, 0:1], ALU.subtract), after=[s])
    neg_lam = q.dve.do(lambda e: e.tensor_scalar(lam[:, 2:3], lam[:, 2:3], -LAM_INIT, None, ALU.add))
    q.dve.do(lambda e: e.tensor_scalar(k.subln[:, :], k.subln[:, :], 1.0 - LAM_INIT, None, ALU.mult), after=[k.params])
    o_banks = [k.banks.take() for _ in range(NB)]
    k.soft_free = []
    pt_free = []
    scale = DIFF_D ** -0.5
    tags = k.tags
    for h in range(HEADS):
        ex = []
        for m, e_out in enumerate((e1, e2)):
            r = slice(m * DIFF_D, (m + 1) * DIFF_D)
            bank = k.banks_b.take()
            view = bank.tile[:, :].rearrange("p (a b) -> p a b", a=NB)
            step = product(q, bank, [(view[:, b, :], [(qk["dq"][r, h, b * P:(b + 1) * P], qk["dk"][r, h, :])]) for b in range(NB)],
                           after=[dq, dk])
            ex.append(softmax_rows(k, q, bank, step, e_out, scale, tags[:, m, :]))
        q.dve.do(lambda e: e.reciprocal(tags[:, :, 6:8], tags[:, :, 4:6]), after=ex)
        q.dve.do(lambda e: e.tensor_scalar(tags[:, 1, 6:8], tags[:, 1, 6:8], lam[:, 2:3], None, ALU.mult), after=[neg_lam])
        for b in range(NB):
            q.dve.do(lambda e, b=b: e.tensor_scalar(e2[:, b, :], e2[:, b, :], tags[:, 1, 6 + b:7 + b], None, ALU.mult))
            p = q.dve.do(lambda e, b=b: e.scalar_tensor_tensor(out=e1[:, b, :], in0=e1[:, b, :], scalar=tags[:, 0, 6 + b:7 + b],
                                                               in1=e2[:, b, :], op0=ALU.mult, op1=ALU.add))
        o_step = probabilities_times_v(k, q, e1, pt, p, pt_free, dv, h, vr, o_banks)
        pt_free = [o_step[1]]
        k.soft_free = [o_step[1]]
    ss = sums_of_squares(k, q, [b.tile for b in o_banks], o_step, HEADS, HD, k.hrs)
    rs = rms_scale(k, q, k.hrs, 8, HD, RMS_EPS, ss)
    for tb in range(NB):
        for h in range(HEADS):
            i = tb * HEADS + h
            got = q.dve.do(lambda e, tb=tb, h=h, i=i, o_banks=o_banks: e.scalar_tensor_tensor(
                out=y[:, tb, 512 + h * HD:512 + (h + 1) * HD], in0=o_banks[tb].tile[:, h * HD:(h + 1) * HD], scalar=k.hrs[:, i:i + 1],
                in1=k.subln[:, :], op0=ALU.mult, op1=ALU.mult), after=[rs])
        o_banks[tb].free = [got]
    mix_b = mix_transposes(k, q, y[:, :, 512:1024], 4, [got])
    return out_projection(k, q, "ev_out", mix_a + mix_b)


def probabilities_times_v(k, q, p, pt, p_ready, pt_free, v, h, v_ready, o_banks):
    bank = k.banks_b.take()
    view = bank.tile[:, :].rearrange("p (a b) -> p a b", a=NB)
    step = transposes(q, bank, k.ident, [(view[:, kb, b * P:(b + 1) * P], p[:, b, kb * P:(kb + 1) * P])
                                         for kb in range(NB) for b in range(NB)], after=[p_ready])
    for s in pt_free:
        q.act.wait(s)
    got = evacuate(k, q, bank, step, pt, view)
    out = []
    for tb in range(NB):
        out.append(product(q, o_banks[tb], [(o_banks[tb].tile[:, h * HD:(h + 1) * HD],
                                             [(pt[:, kb, tb * P:(tb + 1) * P], v[:, kb, h * HD:(h + 1) * HD]) for kb in range(NB)])],
                           after=[got, v_ready]))
    return out


def decayed_scores(k, q, la, qT, kT, heads_on, diag, cross, ready, forward, first, work):
    n = la.shape[1]
    b, f, qf, kf = work
    flat = lambda a: a.rearrange("p a b -> p (a b)")
    refs = k.refs
    if forward:
        got = q.dve.do(lambda e: e.tensor_tensor_scan(flat(b), k.tab("scan")[:, 0:n * T], flat(la), 0.0, ALU.mult, ALU.add), after=ready)
        tot = b[:, :, CHUNK - 1::CHUNK]
    else:
        q.dve.do(lambda e: e.tensor_tensor(flat(f)[:, 1:n * T], flat(la)[:, 0:n * T - 1], k.tab("scan")[:, 1:n * T], ALU.mult), after=ready)
        q.dve.do(lambda e: e.memset(flat(f)[:, 0:1], 0.0))
        q.dve.do(lambda e: e.tensor_tensor_scan(flat(b), k.tab("scan")[:, 0:n * T], flat(f), 0.0, ALU.mult, ALU.add))
        got = q.dve.do(lambda e: e.tensor_tensor(refs[:, 3, 0:n, :], b[:, :, CHUNK - 1::CHUNK], la[:, :, CHUNK - 1::CHUNK], ALU.add))
        tot = refs[:, 3, 0:n, :]
    q.dve.do(lambda e: e.memset(refs[:, 0:2, :, :], 0.0))
    q.dve.do(lambda e, tot=tot: e.tensor_copy(refs[:, 0, 0:n, 0::2], tot[:, :, 0::2]))
    q.dve.do(lambda e, tot=tot: e.tensor_copy(refs[:, 1, 0:n, 1:2], tot[:, :, 1:2]))
    q.dve.do(lambda e, tot=tot: e.tensor_tensor(refs[:, 1, 0:n, 0:1], tot[:, :, 0:1], tot[:, :, 1:2], ALU.add))
    q.dve.do(lambda e, tot=tot: e.tensor_scalar(refs[:, 1, 0:n, 3:4], tot[:, :, 2:3], -1.0, None, ALU.mult))
    mask_base = 0 if forward else len(LEVELS)
    work_free = []
    for m in (8,) + LEVELS:
        size = 1 << m
        if m >= 7:
            mid = refs[:, m - 7, 0:n, :].rearrange("p a b -> p (a b)")
            width = CHUNK
        else:
            at = size // 2 - (1 if forward else 0)
            mid = flat(b)[:, at::size]
            width = size
        bv, fv = (flat(a).rearrange("p (a b) -> p a b", b=width) for a in (b, f))
        q.dve.do(lambda e, fv=fv, bv=bv, mid=mid, width=width: e.tensor_tensor(fv, bv, bcast(mid, width), ALU.subtract))
        d = q.dve.do(lambda e: e.scalar_tensor_tensor(out=flat(f), in0=flat(f), scalar=-1.0, in1=flat(f), op0=ALU.mult, op1=ALU.min))
        ex = q.act.do(lambda e: e.activation(flat(f), flat(f), ACT.Exp), after=[d])
        q.dve.do(lambda e: e.tensor_tensor(flat(qf), flat(f), flat(qT), ALU.mult), after=[ex] + work_free)
        fac = q.dve.do(lambda e: e.tensor_tensor(flat(kf), flat(f), flat(kT), ALU.mult))
        work_free = []
        for side in range(2):
            bank = k.banks_b.take()
            if m == 8:
                sb, tb = (0, 1) if forward else (1, 0)
                view = bank.tile[:, 0:2 * P].rearrange("p (a b) -> p a b", a=2)
                groups = []
                for i in range(2):
                    r, j = heads_on(side, i)
                    groups.append((view[:, i, :], [(kf[r, j, sb * P:(sb + 1) * P], qf[r, j, tb * P:(tb + 1) * P])]))
                step = product(q, bank, groups, after=[fac])
                got = evacuate(k, q, bank, step, cross[:, side, :, :], view)
            else:
                view = bank.tile[:, :].rearrange("p (a b) -> p a b", a=4)
                groups = []
                for i in range(2):
                    r, j = heads_on(side, i)
                    for blk in range(NB):
                        ts = slice(blk * P, (blk + 1) * P)
                        groups.append((view[:, 2 * i + blk, :], [(kf[r, j, ts], qf[r, j, ts])]))
                step = product(q, bank, groups, after=[fac])
                mask = k.masks[:, mask_base + LEVELS.index(m), :]
                got = q.dve.do(lambda e, side=side, view=view, mask=mask: e.copy_predicated(diag[:, side, :, :], mid_bcast(mask, 4), view),
                               after=[step] + first)
                bank.free = [got]
            work_free.append(step)
    if forward:
        for side in range(2):
            bank = k.banks_b.take()
            view = bank.tile[:, :].rearrange("p (a b) -> p a b", a=4)
            groups = []
            for i in range(2):
                r, j = heads_on(side, i)
                for blk in range(NB):
                    ts = slice(blk * P, (blk + 1) * P)
                    groups.append((view[:, 2 * i + blk, :], [(kT[r, j, ts], qT[r, j, ts])]))
            step = product(q, bank, groups, after=ready)
            mask = k.masks[:, 2 * len(LEVELS), :]
            got = q.dve.do(lambda e, side=side, view=view, mask=mask: e.copy_predicated(diag[:, side, :, :], mid_bcast(mask, 4), view),
                           after=[step])
            bank.free = [got]
    k.work_free = work_free
    return [got, Step(q.act.sem, q.act.count), Step(q.dve.sem, q.dve.count)]


def decayed_values(k, q, diag, crosses, head_of, v, ready):
    o_banks = [k.banks.take() for _ in range(NB)]
    steps = []
    for tb in range(NB):
        groups = []
        for side in range(2):
            for i in range(2):
                h = head_of(side, i)
                vs = slice(h * HD, (h + 1) * HD)
                parts = [(diag[:, side, 2 * i + tb, :], v[:, tb, vs])]
                if crosses[tb] is not None:
                    parts.append((crosses[tb][:, side, i, :], v[:, 1 - tb, vs]))
                groups.append((o_banks[tb].tile[:, vs], parts))
        steps.append(product(q, o_banks[tb], groups, after=ready))
    return o_banks, steps


def gated_rms(k, q, o_banks, steps, gain, gate, gate_ready, y):
    ss = sums_of_squares(k, q, [b.tile for b in o_banks], steps, HEADS, HD, k.hrs)
    rs = rms_scale(k, q, k.hrs, 8, HD, RMS_EPS, ss)
    for tb in range(NB):
        for h in range(HEADS):
            i = tb * HEADS + h
            got = q.dve.do(lambda e, tb=tb, h=h, i=i: e.scalar_tensor_tensor(
                out=y[:, tb, h * HD:(h + 1) * HD], in0=o_banks[tb].tile[:, h * HD:(h + 1) * HD], scalar=k.hrs[:, i:i + 1],
                in1=gain, op0=ALU.mult, op1=ALU.mult), after=[rs, k.params])
        o_banks[tb].free = [got]
    return q.dve.do(lambda e: e.tensor_tensor(y[:, :, 0:512], y[:, :, 0:512], gate, ALU.mult), after=[gate_ready])


def log_sigmoid(k, q, z, tmp, ready):
    a = q.dve.do(lambda e: e.scalar_tensor_tensor(out=tmp, in0=z, scalar=-1.0, in1=z, op0=ALU.mult, op1=ALU.min), after=ready)
    q.act.do(lambda e: e.activation(tmp, tmp, ACT.Exp), after=[a])
    return q.act.do(lambda e: e.activation(tmp, tmp, ACT.Ln, bias=1.0))


def mla_gla_mixer(k, q):
    A = k.arena
    A.restart()
    y = k.acc
    cq, ckv = A.take(NB, MLA_QR), A.take(NB, MLA_KVR)
    cqT, ckvT = A.take(2, T), A.take(1, T)
    qh, kh = A.take(HEADS, T), A.take(HEADS, T)
    v = A.take(NB, 512)
    e1, pt = A.take(NB, T), A.take(NB, T)
    tmp = A.take(HEADS, T)
    lr_at = A.words - 2 * T
    A.at = lr_at
    lr = A.take(2, T)
    bank, step = project(k, q, ("od_in", 0), TOK)
    sq = sums_of_squares(k, q, [bank.tile[:, b * 256:(b + 1) * 256] for b in range(NB)], [step, step], 1, MLA_QR, k.hrs)
    bank2, step2 = project(k, q, ("od_in", 1), [("tok", 0, MLA_KVR, 0), ("feat", MLA_KVR, MLA_KVR + MLA_ROPE, MLA_NOPE, T)])
    sk = sums_of_squares(k, q, [bank2.tile[:, b * P:(b + 1) * P] for b in range(NB)], [step2, step2], 1, MLA_KVR, k.hrs[:, 8:10])
    rs = rms_scale(k, q, k.hrs, 2, MLA_QR, RMS_EPS, sq)
    rk = rms_scale(k, q, k.hrs[:, 8:10], 2, MLA_KVR, RMS_EPS, sk)
    for b in range(NB):
        a = q.dve.do(lambda e, b=b, bank=bank: e.tensor_scalar(cq[:, b, :], bank.tile[:, b * 256:(b + 1) * 256], k.hrs[:, b:b + 1], None, ALU.mult), after=[rs])
    bank.free = [a]
    for b in range(NB):
        c = q.dve.do(lambda e, b=b: e.tensor_scalar(ckv[:, b, :], bank2.tile[:, b * P:(b + 1) * P], k.hrs[:, 8 + b:9 + b], None, ALU.mult), after=[rk])
    ropes = slice(MLA_NOPE, MLA_QD)
    kr_raw = tmp[ropes, 0:1, :]
    kr = q.dve.do(lambda e: e.tensor_copy(kr_raw[:, 0, :], bank2.tile[ropes, T:2 * T]))
    bank2.free = [kr]
    tb_bank = k.banks.take()
    view = tb_bank.tile[:, :].rearrange("p (a b) -> p a b", a=2)
    step = transposes(q, tb_bank, k.ident, [(view[:, j, b * P:(b + 1) * P], cq[:, b, j * P:(j + 1) * P]) for j in range(2) for b in range(NB)], after=[a])
    for j in range(2):
        cq_done = q.dve.do(lambda e, j=j, view=view: e.tensor_scalar(cqT[:, j, :], view[:, j, :], k.q_norm[:, j:j + 1], None, ALU.mult), after=[step, k.params])
    tb_bank.free = [cq_done]
    tb2 = k.banks.take()
    step = transposes(q, tb2, k.ident, [(tb2.tile[:, b * P:(b + 1) * P], ckv[:, b, :]) for b in range(NB)], after=[c])
    ckv_done = q.dve.do(lambda e: e.tensor_scalar(ckvT[:, 0, :], tb2.tile[:, 0:T], k.kv_norm[:, 0:1], None, ALU.mult), after=[step])
    tb2.free = [ckv_done]
    for pair in range(2):
        bank = k.banks.take()
        groups = [(bank.tile[0:MLA_QD, i * T:(i + 1) * T],
                   [(k.w_uq[:, j, (2 * pair + i) * MLA_QD:(2 * pair + i + 1) * MLA_QD], cqT[:, j, :]) for j in range(2)]) for i in range(2)]
        step = product(q, bank, groups, after=[cq_done, k.params])
        src = bank.tile[0:MLA_QD, :].rearrange("p (a b) -> p a b", a=2)
        q_raw = evacuate(k, q, bank, step, qh[0:MLA_QD, 2 * pair:2 * pair + 2, :], src)
        bank = k.banks.take()
        groups = [(bank.tile[0:MLA_NOPE, i * T:(i + 1) * T], [(k.w_ukv[:, (2 * pair + i) * 192:(2 * pair + i) * 192 + MLA_NOPE], ckvT[:, 0, :])])
                  for i in range(2)]
        step = product(q, bank, groups, after=[ckv_done])
        src = bank.tile[0:MLA_NOPE, :].rearrange("p (a b) -> p a b", a=2)
        k_raw = evacuate(k, q, bank, step, kh[0:MLA_NOPE, 2 * pair:2 * pair + 2, :], src)
        bank = k.banks.take()
        groups = [(bank.tile[:, (b * 2 + i) * HD:(b * 2 + i + 1) * HD],
                   [(ckvT[:, 0, b * P:(b + 1) * P], k.w_ukv[:, (2 * pair + i) * 192 + MLA_NOPE:(2 * pair + i + 1) * 192])])
                  for b in range(NB) for i in range(2)]
        step = product(q, bank, groups, after=[ckv_done])
        v_done = evacuate(k, q, bank, step, v[:, :, 256 * pair:256 * pair + 256], bank.tile[:, :].rearrange("p (a b) -> p a b", a=2), engine="dve")
    cos, sin, swap = (k.tab(n)[ropes, :] for n in ("mla_cos", "mla_sin", "mla_swap"))
    for pair in range(2):
        part = qh[ropes, 2 * pair:2 * pair + 2, :]
        bank = k.banks.take()
        view = bank.tile[ropes, :].rearrange("p (a b) -> p a b", a=2)
        step = product(q, bank, [(view[:, i, :], [(swap, part[:, i, :])]) for i in range(2)], after=[q_raw])
        t2 = k.rot_tmp[ropes, :].rearrange("p (a b) -> p a b", a=2)
        g = q.dve.do(lambda e, view=view, t2=t2: e.tensor_tensor(t2, view, mid_bcast(sin, 2), ALU.mult), after=[step])
        bank.free = [g]
        q.dve.do(lambda e, part=part: e.tensor_tensor(part, part, mid_bcast(cos, 2), ALU.mult))
        q_done = q.dve.do(lambda e, part=part, t2=t2: e.tensor_tensor(part, part, t2, ALU.add))
    bank = k.banks.take()
    step = product(q, bank, [(bank.tile[ropes, 0:T], [(swap, kr_raw[:, 0, :])])], after=[kr])
    g = q.dve.do(lambda e, bank=bank: e.tensor_tensor(k.rot_tmp[ropes, 0:T], bank.tile[ropes, 0:T], sin, ALU.mult), after=[step])
    bank.free = [g]
    q.dve.do(lambda e: e.tensor_tensor(kr_raw[:, 0, :], kr_raw[:, 0, :], cos, ALU.mult))
    k_done = q.dve.do(lambda e: e.tensor_tensor(kh[ropes, :, :], mid_bcast(kr_raw[:, 0, :], HEADS), mid_bcast(k.rot_tmp[ropes, 0:T], HEADS), ALU.add))
    lr_bank, step = project(k, q, ("od_in", 2), [("feat", 0, GATE_RANK, 0, 0), ("feat", GATE_RANK, 2 * GATE_RANK, 0, T)])
    lr_done = evacuate(k, q, lr_bank, step, lr[0:GATE_RANK, :, :], lr_bank.tile[0:GATE_RANK, :].rearrange("p (a b) -> p a b", a=2))
    k.soft_free, pt_free = [], []
    mixed = []
    for pair in range(2):
        out_bank = k.banks.take()
        for i in range(2):
            h = 2 * pair + i
            bank = k.banks_b.take()
            view = bank.tile[:, :].rearrange("p (a b) -> p a b", a=NB)
            step = product(q, bank, [(view[:, b, :], [(qh[0:MLA_QD, h, b * P:(b + 1) * P], kh[0:MLA_QD, h, :])]) for b in range(NB)],
                           after=[q_done, k_done, k_raw])
            ex = softmax_rows(k, q, bank, step, e1, MLA_QD ** -0.5, k.tags[:, 0, :])
            q.dve.do(lambda e: e.reciprocal(k.tags[:, 0, 6:8], k.tags[:, 0, 4:6]), after=[ex])
            for b in range(NB):
                p = q.dve.do(lambda e, b=b: e.tensor_scalar(e1[:, b, :], e1[:, b, :], k.tags[:, 0, 6 + b:7 + b], None, ALU.mult))
            bank = k.banks_b.take()
            view = bank.tile[:, :].rearrange("p (a b) -> p a b", a=NB)
            step = transposes(q, bank, k.ident, [(view[:, kb, b * P:(b + 1) * P], e1[:, b, kb * P:(kb + 1) * P])
                                                 for kb in range(NB) for b in range(NB)], after=[p])
            k.soft_free = [step]
            for s in pt_free:
                q.act.wait(s)
            got = evacuate(k, q, bank, step, pt, view)
            step = product(q, out_bank, [(out_bank.tile[:, i * T:(i + 1) * T],
                                          [(v[:, kb, h * HD:(h + 1) * HD], pt[:, kb, :]) for kb in range(NB)])], after=[got, v_done])
            pt_free = [step]
        mixed.append(evacuate(k, q, out_bank, step, k.mixT[:, 2 * pair:2 * pair + 2, :], out_bank.tile[:, :].rearrange("p (a b) -> p a b", a=2)))

    A.restart()
    v, gate = A.take(NB, 512), A.take(NB, 512)
    gq, gk = A.take(2, T), A.take(2, T)
    diag = A.take(2, 4, P)
    cross_f, cross_b = A.take(2, 2, P), A.take(2, 2, P)
    la = [A.take(2, T), A.take(2, T)]
    work = [A.take(2, T) for _ in range(4)]
    zt = A.take(2, T)
    assert A.at <= lr_at
    for s in pt_free + [mixed[-1], p]:
        q.act.wait(s)
        q.dve.wait(s)
    q_ready = []
    bank, step = project(k, q, ("od_in", 3), FEAT2)
    q_ready.append(evacuate(k, q, bank, step, gq, bank.tile[:, :].rearrange("p (a b) -> p a b", a=2), scale=64 ** -0.5))
    bank, step = project(k, q, ("od_in", 4), FEAT2)
    q_ready.append(evacuate(k, q, bank, step, gk, bank.tile[:, :].rearrange("p (a b) -> p a b", a=2)))
    for c in range(2):
        v_done = token_major(k, q, ("od_in", 5 + c), v[:, :, 256 * c:256 * c + 256])
    for c in range(2):
        g_done = token_major(k, q, ("od_in", 7 + c), gate[:, :, 256 * c:256 * c + 256], func=ACT.Silu)
    clear = q.dve.do(lambda e: e.memset(diag.rearrange("p a b c -> p (a b c)"), 0.0))
    rows_of = lambda side, i: (slice(64 * side, 64 * side + 64), i)
    steps = []
    for way in range(2):
        bank = k.banks.take()
        view = bank.tile[:, :].rearrange("p (a b) -> p a b", a=2)
        step = product(q, bank, [(view[:, j, :], [(k.gla_w2[0:GATE_RANK, way, j * P:(j + 1) * P], lr[0:GATE_RANK, way, :])]) for j in range(2)],
                       after=[lr_done, k.params])
        for j in range(2):
            z = q.dve.do(lambda e, way=way, j=j, view=view: e.tensor_scalar(zt[:, j, :], view[:, j, :], k.gla_b[:, way, j:j + 1], None, ALU.add), after=[step])
        bank.free = [z]
        ln = log_sigmoid(k, q, zt, la[way], [z])
        q.dve.do(lambda e, way=way: e.scalar_tensor_tensor(out=la[way], in0=zt, scalar=0.0, in1=la[way], op0=ALU.min, op1=ALU.subtract), after=[ln])
        steps.append(q.dve.do(lambda e, way=way: e.tensor_scalar(la[way], la[way], 1.0 / GLA_TAU, None, ALU.mult)))
    k.work_free = []
    for way, cross in enumerate((cross_f, cross_b)):
        for s in k.work_free:
            q.dve.wait(s)
        done = decayed_scores(k, q, la[way], gq, gk, rows_of, diag, cross, q_ready + [steps[way]], way == 0, [clear], work)
    o_banks, o_steps = decayed_values(k, q, diag, (cross_b, cross_f), lambda side, i: 2 * i + side, v, done + [v_done])
    got = gated_rms(k, q, o_banks, o_steps, k.gla_norm[:, :], gate, g_done, y)
    return out_projection(k, q, "od_out", mixed + mix_transposes(k, q, y, 4, [got]))


def pool_hgrn_mixer(k, q, layer):
    A = k.arena
    A.restart()
    y = k.acc
    gate, v = A.take(NB, 512), A.take(NB, 512)
    qT, kT, la = A.take(HEADS, T), A.take(HEADS, T), A.take(HEADS, T)
    diag, cross = A.take(2, 4, P), A.take(2, 2, P)
    work = [A.take(HEADS, T) for _ in range(4)]
    f = work[0]
    u = work[2].rearrange("p a b -> p (a b)").rearrange("p (a b) -> p a b", a=NB)
    for c in range(2):
        bank, step = project(k, q, ("in2", c), [("tok", 0, 256, 0)])
        u_done = evacuate(k, q, bank, step, u[:, :, 256 * c:256 * c + 256], bank.tile[:, :].rearrange("p (a b) -> p a b", a=NB))
    for c in range(2):
        bank, step = project(k, q, ("in2", 2 + c), FEAT2)
        q_done = evacuate(k, q, bank, step, qT[:, 2 * c:2 * c + 2, :], bank.tile[:, :].rearrange("p (a b) -> p a b", a=2), scale=HD ** -0.5)
    for c in range(2):
        bank, step = project(k, q, ("in2", 4 + c), FEAT2)
        f_done = evacuate(k, q, bank, step, f[:, 2 * c:2 * c + 2, :], bank.tile[:, :].rearrange("p (a b) -> p a b", a=2))
    for c in range(2):
        v_done = token_major(k, q, ("in2", 6 + c), v[:, :, 256 * c:256 * c + 256])
    for c in range(2):
        g_done = token_major(k, q, ("in2", 8 + c), gate[:, :, 256 * c:256 * c + 256], func=ACT.Silu)
    ln = log_sigmoid(k, q, f, la, [f_done])
    a = q.dve.do(lambda e: e.tensor_scalar(kT, f, -1.0, 0.0, ALU.mult, ALU.min), after=[ln])
    a = q.dve.do(lambda e: e.tensor_tensor(kT, kT, la, ALU.subtract))
    kk = q.act.do(lambda e: e.activation(kT, kT, ACT.Exp), after=[a])
    la_done = q.dve.do(lambda e: e.scalar_tensor_tensor(out=la, in0=f, scalar=0.0, in1=la, op0=ALU.min, op1=ALU.subtract))
    if layer == 1:
        lbp, lbd = k.lb_param, k.lb_work
        q.dve.do(lambda e: e.tensor_tensor(lbd[:, 0, :], lbp[:, 1, :], lbp[:, 0, :], ALU.subtract), after=[k.params])
        d = log_sigmoid(k, q, lbd[:, 0, :], lbd[:, 1, :], [])
        q.dve.do(lambda e: e.scalar_tensor_tensor(out=lbd[:, 2, :], in0=lbd[:, 0, :], scalar=0.0, in1=lbd[:, 1, :], op0=ALU.min, op1=ALU.subtract), after=[d])
        q.dve.do(lambda e: e.tensor_scalar(lbd[:, 3, :], lbd[:, 0, :], -1.0, 0.0, ALU.mult, ALU.min))
        d = q.dve.do(lambda e: e.tensor_tensor(lbd[:, 3, :], lbd[:, 3, :], lbd[:, 1, :], ALU.subtract))
        one = q.act.do(lambda e: e.activation(lbd[:, 0, :], lbd[:, 3, :], ACT.Exp), after=[d])
        q.dve.do(lambda e: e.tensor_tensor(kT, kT, bcast(lbd[:, 0, :], T), ALU.mult), after=[one, kk])
        q.dve.do(lambda e: e.tensor_tensor(la, la, bcast(lbd[:, 3, :], T), ALU.add))
        q.dve.do(lambda e: e.tensor_tensor(f, la, bcast(lbd[:, 2, :], T), ALU.subtract))
        d = log_sigmoid(k, q, f, work[1], [])
        q.dve.do(lambda e: e.tensor_tensor(la, la, bcast(lbd[:, 2, :], T), ALU.max))
        la_done = q.dve.do(lambda e: e.tensor_tensor(la, la, work[1], ALU.add), after=[d])
    clear = q.dve.do(lambda e: e.memset(diag.rearrange("p a b c -> p (a b c)"), 0.0))
    rows_of = lambda side, i: (slice(0, P), 2 * side + i)
    pooled = work[3]
    mixed = []
    for half in range(2):
        bank = k.banks.take()
        groups = [(bank.tile[:, i * T:(i + 1) * T],
                   [(u[:, sb, (2 * half + i) * P:(2 * half + i + 1) * P], k.pool_mat[:, sb, 2 * half + i, :]) for sb in range(NB)]) for i in range(2)]
        step = product(q, bank, groups, after=[u_done, k.pool_here])
        p_done = evacuate(k, q, bank, step, pooled[:, 2 * half:2 * half + 2, :], bank.tile[:, :].rearrange("p (a b) -> p a b", a=2))
        bank = k.banks.take()
        groups = [(bank.tile[:, i * T:(i + 1) * T], [(k.pool_w[:, layer, 2 * half + i, :], pooled[:, 2 * half + i, :])]) for i in range(2)]
        step = product(q, bank, groups, after=[p_done, k.params])
        for i in range(2):
            g = 2 * half + i
            got = q.act.do(lambda e, g=g, i=i, bank=bank: e.activation(k.mixT[:, g, :], bank.tile[:, i * T:(i + 1) * T], ACT.Copy,
                                                                       scale=k.pool_scale[:, layer, g:g + 1]), after=[step])
        bank.free = [got]
        mixed.append(got)
    q.dve.wait(mixed[-1])
    done = decayed_scores(k, q, la, qT, kT, rows_of, diag, cross, [q_done, kk, la_done], True, [clear], work)
    o_banks, o_steps = decayed_values(k, q, diag, (None, cross), lambda side, i: 2 * side + i, v, done + [v_done])
    got = gated_rms(k, q, o_banks, o_steps, k.hgrn_g[:, layer, :], gate, g_done, y)
    return out_projection(k, q, "out2", mixed + mix_transposes(k, q, y, 4, [got]))


def ffn(k, q):
    A = k.arena
    A.restart()
    hidden = A.take(FT, T)
    silu = [A.take(T), A.take(T)]
    out_banks, work_banks = k.all_banks[0:4], Banks(k.all_banks[4:8])
    for b in range(4):
        out_banks[b].taken = list(out_banks[b].free)
    chunk, down = {}, {}
    h_done = [None] * FT
    silu_free = [[], []]
    for f in range(FT + FFN_LAG):
        if f < FT:
            if f % 2 == 0:
                chunk = {name: k.ring.next((name, f // 2)) for name in ("gate", "up")}
            cols = slice((f % 2) * P, (f % 2) * P + P)
            bank = work_banks.take()
            groups = [(bank.tile[:, i * T:(i + 1) * T], [(chunk[name][1][:, kk, cols], k.xT[:, kk, :]) for kk in range(KT)])
                      for i, name in enumerate(("gate", "up"))]
            step = product(q, bank, groups, after=[chunk["gate"][2], chunk["up"][2]] + k.xT_ready)
            if f % 2 == 1:
                for name in ("gate", "up"):
                    k.ring.release(chunk[name][0], step)
            s = silu[f % 2]
            a = q.act.do(lambda e, s=s, bank=bank: e.activation(s, bank.tile[:, 0:T], ACT.Silu), after=[step] + silu_free[f % 2], chain=False)
            h_done[f] = q.dve.do(lambda e, f=f, s=s, bank=bank: e.tensor_tensor(hidden[:, f, :], s, bank.tile[:, T:2 * T], ALU.mult), after=[a], chain=False)
            silu_free[f % 2] = [h_done[f]]
            bank.free = [h_done[f]]
        if f >= FFN_LAG:
            g = f - FFN_LAG
            if g % 2 == 0:
                down = k.ring.next(("down", g // 2))

            def emit(e, g=g, w=down[1]):
                for tb in range(NB):
                    for n in range(2):
                        ins = e.matmul(out_banks[2 * tb + n].tile[:, :], hidden[:, g, tb * P:(tb + 1) * P], w[:, g % 2, BANK * n:BANK * n + BANK],
                                       start=g == 0, stop=g == FT - 1)
                return ins

            after = [down[2], h_done[g]] + ([s for b in out_banks for s in b.free] if g == 0 else [])
            step = q.pe.do(emit, after=after, chain=False)
            if g % 2 == 1:
                k.ring.release(down[0], step)
    done = [[], []]
    for tb in range(NB):
        for n in range(2):
            bank = out_banks[2 * tb + n]
            cols = slice(BANK * n, BANK * n + BANK)
            a = q.act.do(lambda e, tb=tb, cols=cols, bank=bank: e.activation(k.acc[:, tb, cols], bank.tile[:, :], ACT.Copy, scale=0.5),
                         after=[step], chain=False)
            bank.free = [a]
            done[tb].append(q.dve.do(lambda e, tb=tb, cols=cols: e.scalar_tensor_tensor(
                out=k.acc[:, tb, cols], in0=k.x_tok[:, tb, cols], scalar=ALPHA, in1=k.acc[:, tb, cols], op0=ALU.mult, op1=ALU.add),
                after=[a] + k.x_ready, chain=False))
    return done


def route(k, q, layer):
    R = k.route
    bank = k.banks.take()
    lg = bank.tile[:, 0:NB * N_GROUPS].rearrange("p (a b) -> p a b", a=NB)
    le = bank.tile[:, 64:64 + NB * N_EXPERTS].rearrange("p (a b) -> p a b", a=NB)
    groups = []
    for tb in range(NB):
        for out, w in ((lg, k.w_grp[layer]), (le, k.w_exp[layer])):
            groups.append((out[:, tb, :], [(k.xT[:, i, tb * P:(tb + 1) * P], w[:, i, :]) for i in range(KT)]))
    step = product(q, bank, groups, after=k.xT_ready + [k.params])
    do = q.dve.do
    tt, ts, red = (lambda *a: lambda e: e.tensor_tensor(*a)), (lambda *a: lambda e: e.tensor_scalar(*a)), (lambda *a: lambda e: e.tensor_reduce(*a))
    do(tt(R.gl, lg, mid_bcast(k.b_grp[:, layer, :], NB), ALU.add), after=[step])
    bank.free = [do(tt(R.el, le, mid_bcast(k.b_exp[:, layer, :], NB), ALU.add))]

    def first_of(values, best, onehot, order, n):
        do(red(best, values, AXX, ALU.max))
        do(tt(onehot, values, bcast(best, n), ALU.is_equal))
        do(tt(onehot, onehot, mid_bcast(order, NB), ALU.mult))
        do(red(R.top, onehot, AXX, ALU.max))
        return do(tt(onehot, onehot, bcast(R.top, n), ALU.is_equal))

    first_of(R.gl, R.gmax, R.goh, k.tab("desc_grp"), N_GROUPS)
    d = do(tt(R.gl, R.gl, bcast(R.gmax, N_GROUPS), ALU.subtract))
    ex = q.act.do(lambda e: e.activation(R.gl, R.gl, ACT.Exp), after=[d])
    do(ts(R.goh, R.goh, 1.0, BIG, ALU.subtract, ALU.mult))
    el8 = R.el.rearrange("p a (g e) -> p (a g) e", e=PER_GROUP)
    do(tt(el8, el8, bcast(R.goh.rearrange("p a g -> p (a g)"), PER_GROUP), ALU.add))
    first_of(R.el, R.m1, R.oh1, k.tab("desc_exp"), N_EXPERTS)
    do(lambda e: e.scalar_tensor_tensor(out=R.el, in0=R.oh1, scalar=-BIG, in1=R.el, op0=ALU.mult, op1=ALU.add))
    first_of(R.el, R.m2, R.oh2, k.tab("desc_exp"), N_EXPERTS)
    d = do(tt(R.m2, R.m2, R.m1, ALU.subtract))
    ex2 = q.act.do(lambda e: e.activation(R.m2, R.m2, ACT.Exp), after=[d])
    chosen = do(tt(R.hot, R.oh1, R.oh2, ALU.add))
    bank = k.banks.take()
    view = bank.tile[:, 0:3 * N_EXPERTS].rearrange("p (a b) -> p a b", a=3)
    earlier, ones = k.tab("earlier"), k.tab("ones")
    step = product(q, bank, [(view[:, 0, :], [(earlier, R.hot[:, 0, :])]),
                             (view[:, 1, :], [(earlier, R.hot[:, 1, :]), (ones, R.hot[:, 0, :])]),
                             (view[:, 2, :], [(ones, R.hot[:, 0, :]), (ones, R.hot[:, 1, :])])], after=[chosen])
    do(red(R.top[:, 0:1], view[:, 2, :], AXX, ALU.max), after=[step])
    most = do(lambda e: e.tensor_copy(k.most[0:1, 0:1], R.top[0:1, 0:1]))
    do(lambda e: e.scalar_tensor_tensor(out=k.rank, in0=view[:, 0:2, :], scalar=1.0, in1=R.hot, op0=ALU.add, op1=ALU.mult))
    bank.free = [do(ts(k.rank, k.rank, -1.0, None, ALU.add))]
    do(red(R.gmax, R.gl, AXX, ALU.add), after=[ex])
    do(ts(R.m1, R.m2, 1.0, None, ALU.add), after=[ex2])
    do(tt(R.gmax, R.gmax, R.m1, ALU.mult))
    do(lambda e: e.reciprocal(R.m1, R.gmax))
    do(tt(R.m2, R.m2, R.m1, ALU.mult))
    do(tt(R.oh1, R.oh1, bcast(R.m1, N_EXPERTS), ALU.mult))
    do(tt(R.oh2, R.oh2, bcast(R.m2, N_EXPERTS), ALU.mult))
    routed = do(tt(k.gate_w, R.oh1, R.oh2, ALU.add))
    return routed, most


def expert_buffers(k):
    A = k.arena
    A.restart()
    b = Tiles()
    b.sel = [A.take(NB, P) for _ in range(2)]
    b.sel_w = [A.take(NB, P) for _ in range(2)]
    b.sel_wT = [A.take(T) for _ in range(3)]
    b.xg = [A.take(KT, P) for _ in range(2)]
    b.silu, b.h, b.hT = A.take(BANK), A.take(BANK), A.take(FT_E, P)
    b.y = [A.take(D) for _ in range(2)]
    b.spill = [k.mixT[:, :, :].rearrange("p k t -> p (k t)"), k.pool_or_distance[:, :]]
    return b


def experts(k, q, buf, ring, ready):
    n_pairs = N_EXPERTS // PAIR
    gate_bank, up_bank, y_banks = k.all_banks[0], k.all_banks[1], k.all_banks[2:4]
    work = Banks(k.all_banks[4:8])
    none = []
    sel_step, sel_w_step, xg_step, wT_step, y_step, comb = {}, {}, {}, {}, {}, {}
    gate_step, h_step = {}, {}

    def select(g):
        i = g % 2
        e0 = slice(PAIR * g, PAIR * g + PAIR)
        after = [xg_step[g - 2][1]] if g >= 2 else list(ready)
        for tb in range(NB):
            out = buf.sel[i][:, tb, :].rearrange("p (a b) -> p a b", a=PAIR)
            q.dve.do(lambda e, out=out, tb=tb: e.tensor_tensor(out, mid_bcast(k.tab("slot_no"), PAIR), bcast(k.rank[:, tb, e0], CAP), ALU.is_equal),
                     after=after, chain=False)
        sel_step[g] = Step(q.dve.sem, q.dve.count)
        for tb in range(NB):
            out = buf.sel_w[i][:, tb, :].rearrange("p (a b) -> p a b", a=PAIR)
            src = buf.sel[i][:, tb, :].rearrange("p (a b) -> p a b", a=PAIR)
            sel_w_step[g] = q.dve.do(lambda e, out=out, src=src, tb=tb: e.tensor_tensor(out, src, bcast(k.gate_w[:, tb, e0], CAP), ALU.mult),
                                     after=[wT_step[g - 2][0]] if g >= 2 else [])

    def gather(g):
        i = g % 2
        got = []
        for half in range(2):
            bank = work.take()
            view = bank.tile[:, :].rearrange("p (a b) -> p a b", a=4)
            groups = [(view[:, kk, :], [(k.x_tok[:, tb, (4 * half + kk)::KT], buf.sel[i][:, tb, :]) for tb in range(NB)]) for kk in range(4)]
            step = product(q, bank, groups, after=[sel_step[g]] + k.x_ready)
            if g >= 2:
                (q.act if half == 0 else q.dve).wait(gate_step[g - 2])
            got.append(evacuate(k, q, bank, step, buf.xg[i][:, 4 * half:4 * half + 4, :], view, engine="act" if half == 0 else "dve"))
        xg_step[g] = (got, step)
        bank = work.take()
        step = transposes(q, bank, k.ident, [(bank.tile[:, tb * P:(tb + 1) * P], buf.sel_w[i][:, tb, :]) for tb in range(NB)], after=[sel_w_step[g]])
        if g >= 3:
            q.act.wait(comb[g - 3])
        wT_step[g] = (step, evacuate(k, q, bank, step, buf.sel_wT[g % 3], bank.tile[:, 0:T]))

    def paired(bank_of, name, g, halves, per, lhs, n_cols, after):
        for half in range(halves):
            chunks = [ring.next((name, g, half, j)) for j in range(PAIR)]

            def emit(e, half=half, chunks=chunks):
                for kk in range(per):
                    for n in range(n_cols):
                        for j in range(PAIR):
                            r = slice(CAP * j, CAP * j + CAP)
                            ins = e.matmul(bank_of[n].tile[r, :], lhs[:, half * per + kk, r], chunks[j][1][:, kk, BANK * n:BANK * n + BANK],
                                           start=half == 0 and kk == 0, stop=half == halves - 1 and kk == per - 1)
                return ins

            free = [s for b in bank_of for s in b.free] if half == 0 else []
            step = q.pe.do(emit, after=[c[2] for c in chunks] + free + after, chain=False)
            for c in chunks:
                ring.release(c[0], step)
        return step

    def combine(g):
        i = g % 2
        for tb in range(NB):
            for n in range(2):
                bank = work.take()
                cols = slice(BANK * n, BANK * n + BANK)
                step = product(q, bank, [(bank.tile[:, :], [(buf.sel_wT[g % 3][:, tb * P:(tb + 1) * P], buf.y[i][:, cols])])],
                               after=[wT_step[g][1]] + y_step[g])
                got = q.dve.do(lambda e, tb=tb, cols=cols, bank=bank: e.tensor_tensor(k.acc[:, tb, cols], k.acc[:, tb, cols], bank.tile[:, :], ALU.add),
                               after=[step], chain=True)
                bank.free = [got]
        comb[g] = step
        return got

    select(0)
    gather(0)
    for g in range(n_pairs):
        i = g % 2
        gate_s = paired([gate_bank], "gate", g, 2, KT // 2, buf.xg[i], 1, xg_step[g][0])
        up_s = paired([up_bank], "up", g, 2, KT // 2, buf.xg[i], 1, [])
        gate_step[g] = up_s
        if g + 1 < n_pairs:
            select(g + 1)
        a = q.act.do(lambda e: e.activation(buf.silu, gate_bank.tile[:, :], ACT.Silu), after=[gate_s] + ([h_step[g - 1]] if g else none), chain=False)
        gate_bank.free = [a]
        if g:
            q.dve.wait(comb_hT)
        h_step[g] = q.dve.do(lambda e: e.tensor_tensor(buf.h, buf.silu, up_bank.tile[:, :], ALU.mult), after=[a, up_s], chain=False)
        up_bank.free = [h_step[g]]
        if g + 1 < n_pairs:
            gather(g + 1)
        bank = work.take()
        view = bank.tile[:, :].rearrange("p (a b) -> p a b", a=FT_E)
        step = transposes(q, bank, k.ident, [(view[:, f, :], buf.h[:, f::FT_E]) for f in range(FT_E)], after=[h_step[g]])
        comb_hT = step
        if g:
            q.act.wait(down_step)
        hT = evacuate(k, q, bank, step, buf.hT, view)
        if g:
            combine(g - 1)
        down_step = paired(y_banks, "down", g, 2, FT_E // 2, buf.hT, 2, [hT])
        y_step[g] = []
        for n in range(2):
            eng = q.act if n == 0 else q.dve
            if g >= 2:
                eng.wait(comb[g - 2])
            y_step[g].append(evacuate(k, q, y_banks[n], down_step, buf.y[i][:, BANK * n:BANK * n + BANK], engine="act" if n == 0 else "dve"))
    return combine(n_pairs - 1)


def moe(k, q, layer, nc, new_sem, A):
    routed, most = route(k, q, layer)
    for tb in range(NB):
        base = q.dve.do(lambda e, tb=tb: e.tensor_scalar(k.acc[:, tb, :], k.x_tok[:, tb, :], ALPHA, None, ALU.mult), after=k.x_ready)
    buf = expert_buffers(k)
    last = experts(k, q, buf, k.ring, [routed, base])
    q.play(nc, [k.ring])
    most_value = nc.values_load(k.most[0:1, 0:1], min_val=0, max_val=T)
    with nc.If(most_value > CAP):
        with nc.Fori(1, (most_value + (CAP - 1)) // CAP):
            over = Engines(new_sem, f"over{layer}")
            ring_sems = [over.sem("slot0"), over.sem("slot1")]
            ring = Ring([t for t in buf.spill], ring_sems, moe_plan(A, layer), over.sp)
            saved = [list(b.free) for b in k.all_banks]
            ready, k.x_ready = k.x_ready, []
            for b in k.all_banks:
                b.free = []
            down = over.dve.do(lambda e: e.tensor_scalar(k.rank, k.rank, -float(CAP), None, ALU.add))
            experts(k, over, buf, ring, [down])
            over.play(nc, [ring])
            nums = sorted(s.num for s in over.sems)
            nc.all_engine_barrier(sems_to_clear=range(nums[0], nums[-1] + 1))
            for b, free in zip(k.all_banks, saved):
                b.free = free
            k.x_ready = ready
    return [[last], [last]]


def build(nc, A, out, taps=None):
    table, cols = constant_tables()
    with ExitStack() as ctx:
        ctx.enter_context(nc.allow_non_contiguous_dma("small parameters"))

        def sb(name, shape, dt=F32):
            return ctx.enter_context(nc.sbuf_tensor(name, shape, dt))

        def new_sem(name):
            return ctx.enter_context(nc.semaphore(name))

        k = Tiles()
        tables = sb("tables", [P, table.shape[1]])
        k.tab = lambda name: tables[:, cols[name][0]:cols[name][0] + cols[name][1]]
        k.ident = k.tab("ident")
        k.neg_half = k.tab("neg_half")
        k.masks = sb("level_masks", [P, 2 * len(LEVELS) + 1, P], U8)
        k.x_tok, k.acc = sb("x_tok", [P, NB, D]), sb("acc", [P, NB, D])
        k.xT, k.mixT = sb("xT", [P, KT, T]), sb("mixT", [P, KT, T])
        k.norm_gb = [sb(f"norm_gb{i}", [P, 2, D]) for i in range(2)]
        k.bn, k.mv = sb("bn", [P, NB, 12]), sb("mv", [P, NB, 2])
        k.ve, k.rstd = sb("ve", [P, NB]), sb("rstd", [P, NB])
        k.hbn, k.hmv, k.hrs = sb("head_bn", [P, 8, 6]), sb("head_mv", [P, 8, 2]), sb("head_rs", [P, 16])
        k.tags = sb("softmax_stats", [P, 2, 8])
        k.rot_tmp = sb("rot_tmp", [P, 2 * T])
        k.junk = k.rot_tmp[:, 0:T]
        k.refs = sb("level_refs", [P, 4, HEADS, 4])
        k.rank, k.gate_w = (sb(name, [P, NB, N_EXPERTS])[:, :, :] for name in ("rank", "gate_w"))
        k.most = sb("most", [1, 1], I32)
        R = k.route = Tiles()
        R.gl, R.goh = (sb(name, [P, NB, N_GROUPS])[:, :, :] for name in ("group_logits", "group_hot"))
        R.el, R.oh1, R.oh2, R.hot = (sb(name, [P, NB, N_EXPERTS])[:, :, :] for name in ("expert_logits", "first_hot", "second_hot", "chosen_hot"))
        R.gmax, R.m1, R.m2, R.top = (sb(name, [P, NB])[:, :] for name in ("group_max", "first_max", "second_max", "place"))
        k.ret_decay, k.neg_rate = sb("ret_decay", [P, 2 * HEADS]), sb("neg_rate", [P, 2 * HEADS])
        k.lqk, k.lam = sb("lqk", [P, 4, DIFF_D]), sb("lam", [P, 4])
        k.subln, k.gla_norm, k.hgrn_g = sb("subln", [P, HD]), sb("gla_norm", [P, HD]), sb("hgrn_g", [P, DEPTH, HD])
        k.q_norm, k.kv_norm = sb("q_norm", [P, 2]), sb("kv_norm", [P, 1])
        k.w_uq, k.w_ukv = sb("w_uq", [P, 2, HEADS * MLA_QD]), sb("w_ukv", [P, HEADS * 192])
        k.gla_w2, k.gla_b = sb("gla_w2", [GATE_RANK, 2, 256]), sb("gla_b", [P, 2, 2])
        k.pool_w, k.pool_scale = sb("pool_w", [P, DEPTH, 4, P]), sb("pool_scale", [P, DEPTH, 4])
        k.lb_param, k.lb_work = sb("lb_param", [P, DEPTH, 4]), sb("lb_work", [P, 4, 4])
        k.w_grp = [sb(f"w_grp{i}", [P, KT, N_GROUPS]) for i in range(DEPTH)]
        k.w_exp = [sb(f"w_exp{i}", [P, KT, N_EXPERTS]) for i in range(DEPTH)]
        k.b_grp, k.b_exp = sb("b_grp", [P, DEPTH, N_GROUPS]), sb("b_exp", [P, DEPTH, N_EXPERTS])
        slots = [sb(f"ring{i}", [P, SLOT]) for i in range(RING)]
        k.pool_or_distance = sb("wide_tables", [P, NB * 4 * T])
        k.distance = k.pool_or_distance[:, 0:2 * NB * T].rearrange("p (w s t) -> p w s t", w=2, s=NB)
        k.pool_mat = k.pool_or_distance[:, :].rearrange("p (s g t) -> p s g t", s=NB, g=4)
        words = (nc.sbuf_bytes_remaining // 4 // 64) * 64 - 64
        k.arena = Arena(sb("arena", [P, words]), words)
        k.all_banks = [Bank(ctx.enter_context(nc.psum_tensor(f"bank{i}", [P, BANK], F32))) for i in range(8)]
        k.banks, k.banks_b = Banks(k.all_banks[0:4]), Banks(k.all_banks[4:8])

        q = Engines(new_sem, "main")
        k.ring = Ring(slots, [new_sem(f"slot{i}_loaded") for i in range(RING)], weight_plan(A), q.sp)
        x_sem, tab_sem, par_sem, wide_sem, out_sem = (new_sem(n) for n in ("x_loaded", "tables_loaded", "params_loaded", "wide_loaded", "out_stored"))
        k.norm_sem = [new_sem("norm_a_loaded"), new_sem("norm_b_loaded")]
        k.norm_free, k.norm_no = [[], []], 0
        k.norm_rows = []
        for layer in range(DEPTH):
            k.norm_rows += [(A["ln1_g"][layer], A["ln1_b"][layer]), (A["ln2_g"][layer], A["ln2_b"][layer])]
        for layer in range(DEPTH):
            k.norm_rows += [(A["ln_g_2"][layer, i], A["ln_b_2"][layer, i]) for i in range(3)]
        k.x_free, k.xT_free = [], []

        x_here = q.act.dma(k.x_tok[:, :, :], A["x"][0].rearrange("(b p) d -> p b d", p=P), x_sem, 16)
        q.act.dma(tables[:, :], A["tables"], tab_sem, 16)
        n_masks = 2 * len(LEVELS) + 1
        wide_masks = k.acc[:, :, :].rearrange("p b d -> p (b d)")[:, 0:n_masks * P].rearrange("p (a b) -> p a b", a=n_masks)
        tab_here = q.act.dma(wide_masks, A["masks"], tab_sem, 32)
        k.distance_here = q.act.dma(k.pool_or_distance[:, 0:2 * NB * T], A["distance"], wide_sem, 16)
        small = [
            (k.ret_decay[:, 0:HEADS], A["ev_ret_decay_f"][0].partition_broadcast(P)),
            (k.ret_decay[:, HEADS:2 * HEADS], A["ev_ret_decay_b"][0].partition_broadcast(P)),
            (k.subln[:, :], A["ev_subln"][0].partition_broadcast(P)),
            (k.gla_norm[:, :], A["od_gla_norm"][0].partition_broadcast(P)),
            (k.q_norm[:, :], A["od_q_norm"][0].rearrange("(j p) -> p j", p=P)),
            (k.kv_norm[:, :], A["od_kv_norm"].rearrange("a p -> p a")),
            (k.w_uq[:, :, :], A["od_w_uq"][0].rearrange("(j p) n -> p j n", p=P)),
            (k.w_ukv[:, :], A["od_w_ukv"][0]),
            (k.gla_w2[:, 0, :], A["od_gla_w2_f"][0]),
            (k.gla_w2[:, 1, :], A["od_gla_w2_b"][0]),
            (k.gla_b[:, 0, :], A["od_gla_b_f"][0].rearrange("(j p) -> p j", p=P)),
            (k.gla_b[:, 1, :], A["od_gla_b_b"][0].rearrange("(j p) -> p j", p=P)),
        ]
        for i, name in enumerate(("ev_lq1", "ev_lk1", "ev_lq2", "ev_lk2")):
            small.append((k.lqk[:, i, :], A[name][0].partition_broadcast(P)))
        for i in range(DEPTH):
            small += [
                (k.hgrn_g[:, i, :], A["hgrn_norm_g_2"][i].partition_broadcast(P)),
                (k.pool_w[:, i, :, :], A["pool_w_2"][i].rearrange("g c d -> c g d")),
                (k.pool_scale[:, i, :], A["pool_scale_2"][i].rearrange("(g p) -> p g", p=P)),
                (k.lb_param[:, i, :], A["lb_param_2"][i].rearrange("(g p) -> p g", p=P)),
                (k.w_grp[i][:, :, :], rows(A["moe_w_grp"][i])),
                (k.w_exp[i][:, :, :], rows(A["moe_w_exp"][i])),
                (k.b_grp[:, i, :], A["moe_b_grp"][i].partition_broadcast(P)),
                (k.b_exp[:, i, :], A["moe_b_exp"][i].partition_broadcast(P)),
            ]
        for dst, src in small:
            q.act.dma(dst, src, par_sem, 16 * len(small))
        k.params = Step(par_sem, 16 * len(small))
        load_norm(k, q, 0)
        load_norm(k, q, 1)

        for queue in (q.pe, q.dve, q.act, q.pool):
            queue.wait(tab_here)
        q.dve.do(lambda e: e.tensor_copy(k.masks[:, :, :], wide_masks))
        k.x_ready = [x_here, x_here]
        to_feature_major(k, q, k.x_ready)

        def tap(name):
            if taps is not None and name in taps:
                s = q.act.dma(taps[name].rearrange("(b p) d -> p b d", p=P), k.x_tok[:, :, :], out_sem, 16 * (tap.n + 1), after=k.x_ready)
                tap.n += 1
                q.act.wait(s)
        tap.n = 0

        layer_norm(k, q, retention_diff_mixer(k, q))
        tap("ln0")
        layer_norm(k, q, moe(k, q, 0, nc, new_sem, A))
        tap("ln1")
        layer_norm(k, q, mla_gla_mixer(k, q))
        tap("ln2")
        layer_norm(k, q, moe(k, q, 1, nc, new_sem, A))
        tap("ln3")
        k.pool_here = q.act.dma(k.pool_or_distance[:, :], A["pool_mat"], wide_sem, 32, after=[Step(q.dve.sem, q.dve.count)])
        for layer in range(DEPTH):
            layer_norm(k, q, ffn(k, q))
            tap(f"ln{4 + 3 * layer}")
            layer_norm(k, q, pool_hgrn_mixer(k, q, layer))
            tap(f"ln{5 + 3 * layer}")
            layer_norm(k, q, ffn(k, q))
            tap(f"ln{6 + 3 * layer}")
        stored = q.act.dma(out.rearrange("a (b p) d -> p (a b) d", p=P), k.x_tok[:, :, :], out_sem, 16 * (tap.n + 1), after=k.x_ready)
        q.act.wait(stored)
        q.play(nc, [k.ring])
        assert k.ring.asked == k.ring.loaded == len(k.ring.plan)


_INS = ['x', 'ev_w_in', 'ev_ret_decay_f', 'ev_ret_decay_b', 'ev_lq1', 'ev_lk1', 'ev_lq2', 'ev_lk2', 'ev_subln', 'ev_w_out',
        'od_w_in', 'od_q_norm', 'od_w_uq', 'od_kv_norm', 'od_w_ukv', 'od_gla_w2_f', 'od_gla_b_f', 'od_gla_w2_b', 'od_gla_b_b',
        'od_gla_norm', 'od_w_out', 'ln1_g', 'ln1_b', 'ln2_g', 'ln2_b', 'moe_w_grp', 'moe_b_grp', 'moe_w_exp', 'moe_b_exp',
        'moe_w_gate', 'moe_w_up', 'moe_w_down', 'w_in_2', 'pool_w_2', 'pool_scale_2', 'lb_param_2', 'hgrn_norm_g_2', 'w_out_2',
        'ffn1_gate_2', 'ffn1_up_2', 'ffn1_down_2', 'ffn2_gate_2', 'ffn2_up_2', 'ffn2_down_2', 'ln_g_2', 'ln_b_2']


def kernel(**inputs):
    import concourse.bacc as bacc
    from concourse.bass_utils import run_bass_kernel_spmd

    arrays = {name: np.ascontiguousarray(inputs[name]) for name in _INS}
    arrays["tables"] = constant_tables()[0]
    arrays["masks"] = level_masks()
    arrays["distance"] = distance_tables().reshape(P, -1)
    arrays["pool_mat"] = pool_tables().reshape(P, -1)
    nc = bacc.Bacc("TRN2", target_bir_lowering=False, num_devices=1)
    feed, A = {}, {}
    for name, a in arrays.items():
        feed[f"in_{name}"] = a
        A[name] = nc.dram_tensor(f"in_{name}", a.shape, mybir.dt.from_np(a.dtype), kind="ExternalInput").ap()
    out = nc.dram_tensor("out_0", (1, T, D), F32, kind="ExternalOutput").ap()
    build(nc, A, out)
    r = run_bass_kernel_spmd(nc, [feed], core_ids=[0])
    return r.results[0]["out_0"]
```

```python
from contextlib import ExitStack

import concourse.bass as bass
import numpy as np
from concourse import mybir

F32 = mybir.dt.float32
F32R = mybir.dt.float32r
I32 = mybir.dt.int32
U8 = mybir.dt.uint8
ALU = mybir.AluOpType
ACT = mybir.ActivationFunctionType
AXX = mybir.AxisListType.X

P = 128
T = 256
NB = T // P
D = 1024
KT = D // P
BANK = 512
HEADS = 4
HD = 128
DIFF_D = 64
MLA_NOPE, MLA_ROPE, MLA_QR, MLA_KVR = 64, 32, 256, 128
MLA_QD = MLA_NOPE + MLA_ROPE
GATE_RANK = 16
GLA_TAU = 16.0
CHUNK = 64
N_GROUPS, PER_GROUP, N_EXPERTS = 4, 8, 32
D_EXPERT = 512
FT_E = D_EXPERT // P
D_FF = 2816
FT = D_FF // P
DEPTH = 2
ALPHA = (2.0 * DEPTH) ** 0.25
LN_EPS = 1e-5
RMS_EPS = 1e-6
LAM_INIT = 0.2
SLOT = 2048
RING = 7
PARTS = 4
PART = 1024
HIDDEN = 6
CAP = 64
PAIR = 2
BIG = 1e30
WINDOWS = (2, 4, 8, 16)


def rotary_tables(rows, half, theta, width):
    pos = np.arange(T, dtype=np.float32)
    inv = np.power(np.float32(theta), -np.arange(0, 2 * half, 2, dtype=np.float32) / np.float32(2 * half)).astype(np.float32)
    ang = (pos[:, None] * inv[None, :]).astype(np.float32)
    cos = np.ones((rows, T), np.float32)
    sin = np.zeros((rows, T), np.float32)
    swap = np.zeros((rows, rows), np.float32)
    for r in range(rows):
        i = r % width
        if i < 2 * half:
            cos[r] = np.cos(ang[:, i % half])
            sin[r] = np.sin(ang[:, i % half]) * (-1.0 if i < half else 1.0)
            swap[r + half if i < half else r - half, r] = 1.0
    return cos, sin, swap


def constant_tables():
    parts = {}
    parts["ident"] = np.eye(P, dtype=np.float32)
    parts["ones"] = np.ones((P, P), np.float32)
    parts["earlier"] = np.triu(np.ones((P, P), np.float32), 1)
    parts["slot_no"] = np.tile(np.arange(CAP, dtype=np.float32), (P, 1))
    parts["desc_grp"] = np.tile(np.arange(N_GROUPS, 0, -1, dtype=np.float32), (P, 1))
    parts["desc_exp"] = np.tile(np.arange(N_EXPERTS, 0, -1, dtype=np.float32), (P, 1))
    parts["neg_half"] = np.full((P, 16), -0.5, np.float32)
    for name, half, theta, width in (("ret", 64, 10000.0, 128), ("dif", 8, 500000.0, 64)):
        c, s, w = rotary_tables(P, half, theta, width)
        parts[name + "_cos"], parts[name + "_sin"], parts[name + "_swap"] = c, s, w
    c, s, w = rotary_tables(MLA_ROPE, MLA_ROPE // 2, 500000.0, MLA_ROPE)
    at = slice(MLA_NOPE, MLA_QD)
    for key, v in (("mla_cos", c), ("mla_sin", s), ("mla_swap", w)):
        full = np.zeros((P, v.shape[1]), np.float32)
        full[at] = v
        parts[key] = full
    scan = np.ones((P, 2 * T), np.float32)
    scan[:, ::CHUNK] = 0.0
    parts["scan"] = scan
    cols, at = {}, 0
    for key, v in parts.items():
        cols[key] = (at, v.shape[1])
        at += v.shape[1]
    return np.concatenate(list(parts.values()), axis=1), cols


def distance_tables():
    s = np.arange(P)[:, None, None] + P * np.arange(NB)[None, :, None]
    t = np.arange(T)[None, None, :]
    return np.stack([np.maximum(t - s, 0), np.maximum(s - t, 0)], axis=1).astype(np.float32)


def pool_tables():
    out = np.zeros((T, len(WINDOWS), T), np.float32)
    for g, w in enumerate(WINDOWS):
        for t in range(T):
            n = min(t + 1, w)
            out[t - n + 1:t + 1, g, t] = np.float32(1.0) / np.float32(n)
            out[t, g, t] -= 1.0
    return np.ascontiguousarray(out.reshape(NB, P, len(WINDOWS), T).transpose(1, 0, 2, 3))


LEVELS = tuple(range(7, 0, -1))


def level_masks():
    s, t = np.arange(P)[:, None], np.arange(P)[None, :]
    out = []
    for flip in (False, True):
        a, b = (t, s) if flip else (s, t)
        for m in LEVELS:
            n = 1 << m
            out.append((a // n == b // n) & (a % n < n // 2) & (b % n >= n // 2))
    out.append(s == t)
    return np.stack(out, axis=1).astype(np.float32)


class Step:

    def __init__(self, sem, count):
        self.sem, self.count = sem, count


class Queue:

    def __init__(self, sem):
        self.sem, self.count, self.met, self.items = sem, 0, {}, []

    def wait(self, step):
        if self.met.get(id(step.sem), 0) < step.count:
            self.met[id(step.sem)] = step.count
            self.items.append(("wait", step.sem, step.count))

    def do(self, emit, after=(), chain=True):
        for step in after:
            self.wait(step)
        if chain and self.count:
            self.wait(Step(self.sem, self.count))
        self.count += 1
        self.items.append(("run", emit, self.sem, 1))
        return Step(self.sem, self.count)

    def dma(self, out, in_, sem, count, after=()):
        for step in after:
            self.wait(step)
        self.items.append(("run", lambda e: e.dma_start(out, in_), sem, 16))
        return Step(sem, count)

    def play(self, engine):
        for kind, what, *rest in self.items:
            if kind == "wait":
                engine.wait_ge(what, rest[0])
            else:
                what(engine).then_inc(rest[0], rest[1])
        self.items = []


class Tiles:
    pass


class Bank:

    def __init__(self, tile):
        self.tile, self.free = tile, []


class Banks:

    def __init__(self, banks):
        self.banks, self.n = banks, 0

    def take(self):
        self.n += 1
        return self.banks[(self.n - 1) % len(self.banks)]


class Ring:

    def __init__(self, slots, sems, plan, queue):
        self.slots, self.sems, self.plan, self.queue = slots, sems, plan, queue
        self.asked, self.loaded, self.released = 0, 0, [None] * len(plan)

    def next(self, key):
        n = self.asked
        self.asked += 1
        assert self.plan[n][0] == key, (self.plan[n][0], key)
        src = self.plan[n][1]
        a, b = src.shape[1:]
        k = n % len(self.slots)
        view = self.slots[k][:, 0:a * b].rearrange("p (a b) -> p a b", a=a)
        return n, view, Step(self.sems[k], 16 * (n // len(self.slots) + 1))

    def release(self, n, step):
        self.released[n] = step

    def load(self):
        k = len(self.slots)
        while self.loaded < len(self.plan):
            n = self.loaded
            if n >= k and self.released[n - k] is None:
                break
            src = self.plan[n][1]
            a, b = src.shape[1:]
            dst = self.slots[n % k][:, 0:a * b].rearrange("p (a b) -> p a b", a=a)
            self.queue.dma(dst, src, self.sems[n % k], 16 * (n // k + 1), after=[self.released[n - k]] if n >= k else [])
            self.loaded += 1


class Engines:

    def __init__(self, new_sem, name):
        self.sems = []

        def sem(what):
            self.sems.append(new_sem(f"{name}_{what}"))
            return self.sems[-1]

        self.sem = sem
        self.pe, self.act, self.dve, self.pool, self.sp = (Queue(sem(w)) for w in ("pe_done", "act_done", "dve_done", "pool_done", "sp_done"))

    def play(self, nc, rings):
        for ring in rings:
            ring.load()
        with nc.Block(no_gpsimd_drain=True) as block:
            block.sync(self.sp.play)
            block.tensor(self.pe.play)
            block.scalar(self.act.play)
            block.vector(self.dve.play)
            block.gpsimd(self.pool.play)


class Arena:

    def __init__(self, tile, words):
        self.tile, self.words, self.at = tile, words, 0

    def restart(self):
        self.at = 0

    def take(self, *shape):
        n = int(np.prod(shape))
        assert self.at + n <= self.words, (self.at, n, self.words)
        v = self.tile[:, self.at:self.at + n]
        self.at += n
        if len(shape) == 2:
            v = v.rearrange("p (a b) -> p a b", a=shape[0])
        elif len(shape) == 3:
            v = v.rearrange("p (a b c) -> p a b c", a=shape[0], b=shape[1])
        return v


def interleave(*streams):
    streams = list(streams)
    while streams:
        for s in list(streams):
            try:
                next(s)
            except StopIteration:
                streams.remove(s)


def product(q, bank, groups, after=()):

    def emit(e):
        for out, parts in groups:
            for i, (lhs, rhs) in enumerate(parts):
                ins = e.matmul(out, lhs, rhs, start=i == 0, stop=i == len(parts) - 1)
        return ins

    return q.pe.do(emit, after=list(bank.free) + list(after), chain=False)


def transposes(q, bank, ident, pairs, after=()):
    def emit(e):
        for out, in_ in pairs:
            ins = e.transpose(out, in_, ident)
        return ins

    return q.pe.do(emit, after=list(bank.free) + list(after), chain=False)


def bcast(ap, n):
    return ap.unsqueeze(ap.ndim).to_broadcast(list(ap.shape) + [n])


def mid_bcast(ap, n):
    return ap.unsqueeze(1).to_broadcast([ap.shape[0], n] + list(ap.shape[1:]))


def rows(w, k=KT):
    return w.rearrange("(p k) n -> p k n", k=k)


def tiled_rows(w):
    return w.rearrange("(k p) n -> p k n", p=P)


def moe_plan(A, layer):
    out = []
    for g in range(N_EXPERTS // PAIR):
        for name, per in (("gate", KT // 2), ("up", KT // 2), ("down", FT_E // 2)):
            w = A["moe_w_" + name]
            for half in range(2):
                for j in range(PAIR):
                    k = KT if name != "down" else FT_E
                    src = rows(w[layer, PAIR * g + j], k)[:, half * per:(half + 1) * per, :]
                    out.append(((name, g, half, j), src))
    return out


def weight_plan(A):
    plan = [(("ev_in", c), rows(A["ev_w_in"][0])[:, :, 256 * c:256 * c + 256]) for c in (8, 9, 10, 11, 12, 13, 0, 1, 2, 3, 4, 5, 6, 7)]
    plan += [(("ev_out", c), tiled_rows(A["ev_w_out"][0])[:, :, 256 * c:256 * c + 256]) for c in range(4)]
    plan += moe_plan(A, 0)
    for c, (a, b) in enumerate(OD_COLUMNS):
        plan.append((("od_in", c), rows(A["od_w_in"][0])[:, :, a:b]))
    plan += [(("od_out", c), tiled_rows(A["od_w_out"][0])[:, :, 256 * c:256 * c + 256]) for c in range(4)]
    plan += moe_plan(A, 1)
    for layer in range(DEPTH):
        plan += ffn_plan(A, layer, 1)
        plan += [(("in2", c), rows(A["w_in_2"][layer])[:, :, 256 * c:256 * c + 256]) for c in (4, 5, 0, 1, 2, 3, 6, 7, 8, 9)]
        plan += [(("out2", c), tiled_rows(A["w_out_2"][layer])[:, :, 256 * c:256 * c + 256]) for c in range(4)]
        plan += ffn_plan(A, layer, 2)
    return plan


def ffn_plan(A, layer, which):
    out = []
    lag = FFN_LAG // 2
    for c in range(FT // 2 + lag):
        if c < FT // 2:
            for name in ("gate", "up"):
                src = rows(A[f"ffn{which}_{name}_2"][layer])[:, :, 256 * c:256 * c + 256]
                out.append(((name, c), src))
        if c >= lag:
            d = c - lag
            out.append((("down", d), tiled_rows(A[f"ffn{which}_down_2"][layer])[:, 2 * d:2 * d + 2, :]))
    return out


FFN_LAG = 2
OD_COLUMNS = ((0, 256), (256, 416), (1952, 1984), (416, 672), (672, 928), (928, 1184), (1184, 1440), (1440, 1696), (1696, 1952))


def to_feature_major(k, q, after_block):
    done = []
    for tb in range(NB):
        for half in range(2):
            bank = k.banks_b.take()
            view = bank.tile[:, :].rearrange("p (k t) -> p k t", k=4)
            pairs = [(view[:, i, :], k.x_tok[:, tb, (4 * half + i)::KT]) for i in range(4)]
            step = transposes(q, bank, k.ident, pairs, after=[after_block[tb]])
            at = (slice(0, P), slice(4 * half, 4 * half + 4), slice(tb * P, (tb + 1) * P))
            high = q.act.do(lambda e, view=view, at=at: e.activation(k.xh[at], view, ACT.Copy), after=[step], chain=False)
            low = q.dve.do(lambda e, view=view, at=at: e.tensor_tensor(k.xl[at], view, k.xh[at].bitcast(F32), ALU.subtract), after=[high], chain=False)
            bank.free = [low]
            done.append(low)
    k.xT_ready = done


def load_norm(k, q, n):
    sem, free = k.norm_sem, k.norm_free
    for i, row in enumerate(k.norm_rows[n]):
        q.pool.dma(k.norm_gb[:, i, :], row.partition_broadcast(P), sem, 32 * (n + 1), after=free)


def layer_norm(k, q, after_block):
    n = k.norm_no
    k.norm_no += 1
    k.split.prefetch(k, q)
    gb = k.norm_gb
    gb_here = Step(k.norm_sem, 32 * (n + 1))
    for tb in range(NB):
        for h in range(2):
            q.dve.do(lambda e, tb=tb, h=h: e.bn_stats(k.bn[:, tb, 6 * h:6 * h + 6], k.acc[:, tb, 512 * h:512 * h + 512]),
                     after=after_block[tb], chain=h == 0)
        q.dve.do(lambda e, tb=tb: e.bn_aggr(k.mv[:, tb, :], k.bn[:, tb, :]))
    var = q.dve.do(lambda e: e.tensor_scalar(k.ve[:, :], k.mv[:, :, 1], LN_EPS, None, ALU.add))
    rstd = q.pool.do(lambda e: e.tensor_tensor(k.rstd[:, :], k.ve[:, :], k.neg_half[:, 0:NB], ALU.pow), after=[var])
    shift = q.dve.do(lambda e: e.scalar_tensor_tensor(out=k.shift[:, :], in0=k.mv[:, :, 0], scalar=-1.0, in1=k.rstd[:, :],
                                                      op0=ALU.mult, op1=ALU.mult), after=[rstd])
    scaled = [q.act.do(lambda e, tb=tb: e.activation(k.x_tok[:, tb, :], k.acc[:, tb, :], ACT.Identity, bias=k.shift[:, tb:tb + 1],
                                                     scale=k.rstd[:, tb:tb + 1]), after=[shift]) for tb in range(NB)]
    block_done = []
    for tb in range(NB):
        q.dve.do(lambda e, tb=tb: e.tensor_tensor(k.x_tok[:, tb, :], k.x_tok[:, tb, :], gb[:, 0, :], ALU.mult), after=[scaled[tb], gb_here])
        block_done.append(q.dve.do(lambda e, tb=tb: e.tensor_tensor(k.x_tok[:, tb, :], k.x_tok[:, tb, :], gb[:, 1, :], ALU.add)))
    k.norm_free = [block_done[-1]]
    if n + 1 < len(k.norm_rows):
        load_norm(k, q, n + 1)
    k.x_ready = block_done
    to_feature_major(k, q, block_done)


class Splitter:

    def __init__(self, high, low):
        self.high, self.low, self.n, self.free, self.pending = high, low, 0, [[] for _ in high], {}

    def split(self, q, src, here):
        i = self.n % len(self.high)
        self.n += 1
        a, b = src.shape[1:]
        hi, lo = (t[i][:, 0:a * b].rearrange("p (a b) -> p a b", a=a) for t in (self.high, self.low))
        high = q.act.do(lambda e: e.activation(hi, src, ACT.Copy), after=[here] + self.free[i], chain=False)
        low = q.dve.do(lambda e: e.tensor_tensor(lo, src, hi.bitcast(F32), ALU.subtract), after=[high], chain=False)
        return i, hi, lo, low

    def chunk(self, k, q, key):
        if key not in self.pending:
            self.prefetch(k, q)
        parts = self.pending.pop(key)
        self.prefetch(k, q)
        return parts

    def prefetch(self, k, q):
        if k.ring.asked == len(k.ring.plan) or k.ring.plan[k.ring.asked][0][0] not in SPLIT_CHUNKS or len(self.pending) > 0:
            return
        key = k.ring.plan[k.ring.asked][0]
        n, w, here = k.ring.next(key)
        cols = w.shape[2]
        parts = [(c, self.split(q, w[:, :, c:min(c + P, cols)], here)) for c in range(0, cols, P)]
        k.ring.release(n, parts[-1][1][3])
        self.pending[key] = parts


SPLIT_CHUNKS = ("ev_in", "od_in", "in2")


def three_passes(out, products):
    parts = []
    for (lh, ll), (rh, rl) in products:
        parts += [(lh, rh), (lh, rl), (ll, rh)]
    return out, parts


def project(k, q, key, kind):
    bank = k.banks.take()
    parts = k.split.chunk(k, q, key)
    cols = parts[-1][0] + parts[-1][1][1].shape[2]
    for c, (i, hi, lo, here) in parts:
        n = hi.shape[2]
        if kind == "feat":
            groups = [three_passes(bank.tile[:, c // P * T:(c // P + 1) * T],
                                   [((hi[:, j, :], lo[:, j, :]), (k.xh[:, j, :], k.xl[:, j, :])) for j in range(KT)])]
        else:
            groups = []
            for tb in range(NB):
                ts = slice(tb * P, (tb + 1) * P)
                groups.append(three_passes(bank.tile[:, tb * cols + c:tb * cols + c + n],
                                           [((k.xh[:, j, ts], k.xl[:, j, ts]), (hi[:, j, :], lo[:, j, :])) for j in range(KT)]))
        step = product(q, bank, groups, after=[here] + k.xT_ready)
        k.split.free[i] = [step]
    return bank, step


def evacuate(k, q, bank, step, dst, src=None, scale=None, func=None, engine="act"):
    src = bank.tile[:, :] if src is None else src
    if func is None:
        func = ACT.Copy
    if engine == "act":
        got = q.act.do(lambda e, src=src, func=func: e.activation(dst, src, func, scale=1.0 if scale is None else scale), after=[step], chain=False)
    elif scale is None:
        got = q.dve.do(lambda e, src=src: e.tensor_copy(dst, src), after=[step], chain=False)
    else:
        got = q.dve.do(lambda e, src=src: e.tensor_scalar(dst, src, scale, None, ALU.mult), after=[step], chain=False)
    bank.free = [got]
    return got


def token_major(k, q, key, dst, func=None):
    bank, step = project(k, q, key, "tok")
    return evacuate(k, q, bank, step, dst, bank.tile[:, :].rearrange("p (a b) -> p a b", a=NB), func=func)


def rotate(k, q, raw, out, cos, sin, swap, after, at=slice(0, P)):
    bank = k.banks.take()
    view = bank.tile[at, :].rearrange("p (a b) -> p a b", a=2)
    swapped = product(q, bank, [(view[:, i, :], [(swap, raw[:, i, :])]) for i in range(2)], after=after)
    q.dve.do(lambda e: e.tensor_tensor(out, raw, mid_bcast(cos, 2), ALU.mult), after=after)
    tmp = k.rot_tmp[at, :].rearrange("p (a b) -> p a b", a=2)
    got = q.dve.do(lambda e: e.tensor_tensor(tmp, view, mid_bcast(sin, 2), ALU.mult), after=[swapped])
    bank.free = [got]
    return q.dve.do(lambda e: e.tensor_tensor(out, out, tmp, ALU.add))


def out_projection(k, q, name, mix_ready):
    done = []
    for c in range(4):
        n, w, here = k.ring.next((name, c))
        bank = k.banks.take()
        view = bank.tile[:, :].rearrange("p (a b) -> p a b", a=NB)
        groups = [(view[:, tb, :], [(k.mixT[:, i, tb * P:(tb + 1) * P], w[:, i, :]) for i in range(KT)]) for tb in range(NB)]
        step = product(q, bank, groups, after=[here] + mix_ready)
        k.ring.release(n, step)
        cols = slice(256 * c, 256 * c + 256)
        got = q.dve.do(lambda e, cols=cols, view=view: e.scalar_tensor_tensor(
            out=k.acc[:, :, cols], in0=k.x_tok[:, :, cols], scalar=ALPHA, in1=view, op0=ALU.mult, op1=ALU.add),
            after=[step] + k.x_ready, chain=False)
        bank.free = [got]
        done.append(got)
    return [done, done]


def mix_transposes(k, q, src, base, after):
    done = []
    for half in range(2):
        bank = k.banks.take()
        view = bank.tile[:, :].rearrange("p (i t) -> p i t", i=2)
        pairs = [(view[:, i, tb * P:(tb + 1) * P], src[:, tb, (2 * half + i) * P:(2 * half + i + 1) * P])
                 for i in range(2) for tb in range(NB)]
        step = transposes(q, bank, k.ident, pairs, after=after)
        dst = k.mixT[:, base + 2 * half:base + 2 * half + 2, :]
        done.append(evacuate(k, q, bank, step, dst, view, engine="act" if half else "dve"))
    return done


def sums_of_squares(k, q, banks, steps, groups, width, out):
    for b, (bank, step) in enumerate(zip(banks, steps)):
        for g in range(groups):
            got = q.act.do(lambda e, bank=bank, b=b, g=g: e.activation(
                k.junk[:, 0:width], bank[:, g * width:(g + 1) * width], ACT.Square,
                accum_out=out[:, b * groups + g:b * groups + g + 1]), after=[step])
    return got


def rms_scale(k, q, sums, n, width, eps, after):
    a = q.dve.do(lambda e: e.tensor_scalar(sums[:, 0:n], sums[:, 0:n], 1.0 / width, eps, ALU.mult, ALU.add), after=[after])
    return q.pool.do(lambda e: e.tensor_tensor(sums[:, 0:n], sums[:, 0:n], k.neg_half[:, 0:n], ALU.pow), after=[a])


def softmax_rows(k, q, bank, step, e_out, scale, tag, free):
    view = bank.tile[:, :].rearrange("p (a b) -> p a b", a=NB)
    q.dve.do(lambda e: e.tensor_reduce(tag[:, 0:2], view, AXX, ALU.max), after=[step])
    neg = q.dve.do(lambda e: e.tensor_scalar(tag[:, 2:4], tag[:, 0:2], -scale, None, ALU.mult))
    for b in range(NB):
        got = q.act.do(lambda e, b=b: e.activation(e_out[:, b, :], view[:, b, :], ACT.Exp, bias=tag[:, 2 + b:3 + b], scale=scale,
                                                   accum_out=tag[:, 4 + b:5 + b]), after=[neg] + free)
    bank.free = [got]
    return got


def rotated(k, q, c0, dst, which, raw, got):
    for pair in range(2):
        bank, step = project(k, q, ("ev_in", c0 + pair), "feat")
        for s in got.raw_free:
            q.act.wait(s)
        here = evacuate(k, q, bank, step, raw, bank.tile[:, :].rearrange("p (a b) -> p a b", a=2))
        yield
        done = rotate(k, q, raw, dst[:, 2 * pair:2 * pair + 2, :], k.tab(which + "_cos"), k.tab(which + "_sin"),
                      k.tab(which + "_swap"), [here])
        got.raw_free = [done]
        got.last = done
        yield


def diff_heads(k, q, heads, b, dq, dk, dv, ready, lam_ready, o_banks, o_steps):
    scale = DIFF_D ** -0.5
    for h in heads:
        ex = []
        for m, e_out in enumerate((b.e1, b.e2)):
            r = slice(m * DIFF_D, (m + 1) * DIFF_D)
            bank = k.banks_b.take()
            view = bank.tile[:, :].rearrange("p (a b) -> p a b", a=NB)
            step = product(q, bank, [(view[:, i, :], [(dq[r, h, i * P:(i + 1) * P], dk[r, h, :])]) for i in range(NB)], after=ready)
            ex.append(softmax_rows(k, q, bank, step, e_out, scale, b.tags[:, m, :], b.free))
        yield
        tags = b.tags
        q.dve.do(lambda e, tags=tags: e.reciprocal(tags[:, :, 6:8], tags[:, :, 4:6]), after=ex)
        q.dve.do(lambda e, tags=tags: e.tensor_scalar(tags[:, 1, 6:8], tags[:, 1, 6:8], k.lam[:, 2:3], None, ALU.mult), after=[lam_ready])
        for i in range(NB):
            q.dve.do(lambda e, i=i, tags=tags: e.tensor_scalar(b.e2[:, i, :], b.e2[:, i, :], tags[:, 1, 6 + i:7 + i], None, ALU.mult))
            p = q.dve.do(lambda e, i=i, tags=tags: e.scalar_tensor_tensor(out=b.e1[:, i, :], in0=b.e1[:, i, :], scalar=tags[:, 0, 6 + i:7 + i],
                                                               in1=b.e2[:, i, :], op0=ALU.mult, op1=ALU.add))
        yield
        turned, o_steps[h] = probabilities_times_v(k, q, b.e1, b.pt, p, b.pt_free, dv, h, ready[-1], o_banks)
        b.pt_free = [o_steps[h][1]]
        b.free = [turned, p]
        yield


def retention_heads(k, q, heads, b, rq, rk, rv, ready, rates, o_banks, o_steps):
    for h in heads:
        decay, scores = b.e2, b.e1
        q.dve.do(lambda e, h=h, decay=decay: e.tensor_scalar(decay, k.distance[:, 0, :, :], k.neg_rate[:, h:h + 1], None, ALU.mult),
                 after=[rates, k.distance_here] + b.free)
        arg = q.dve.do(lambda e, h=h, decay=decay: e.scalar_tensor_tensor(out=decay, in0=k.distance[:, 1, :, :], scalar=k.neg_rate[:, HEADS + h:HEADS + h + 1],
                                                             in1=decay, op0=ALU.mult, op1=ALU.add))
        dec = q.act.do(lambda e, decay=decay: e.activation(decay, decay, ACT.Exp), after=[arg])
        yield
        bank = k.banks_b.take()
        view = bank.tile[:, :].rearrange("p (a b) -> p a b", a=NB)
        step = product(q, bank, [(view[:, sb, :], [(rk[:, h, sb * P:(sb + 1) * P], rq[:, h, :])]) for sb in range(NB)], after=ready)
        got = q.dve.do(lambda e, scores=scores, view=view, decay=decay: e.scalar_tensor_tensor(out=scores, in0=view, scalar=HD ** -0.5, in1=decay, op0=ALU.mult, op1=ALU.mult),
                       after=[step, dec])
        bank.free = [got]
        yield
        o_steps[h] = [product(q, o_banks[tb], [(o_banks[tb].tile[:, h * HD:(h + 1) * HD],
                                                [(scores[:, sb, tb * P:(tb + 1) * P], rv[:, sb, h * HD:(h + 1) * HD]) for sb in range(NB)])],
                              after=[got]) for tb in range(NB)]
        b.free = [o_steps[h][1]]
        yield


def retention_diff_mixer(k, q):
    A = k.arena
    A.restart()
    y = k.acc
    raw = A.take(2, T)
    dq, dk, rq, rk = (A.take(HEADS, T) for _ in range(4))
    dv, rv, gate = (A.take(NB, 512) for _ in range(3))
    bufs = []
    for i in range(2):
        b = Tiles()
        b.e1, b.e2, b.pt = A.take(NB, T), A.take(NB, T), k.mixT[:, 4 + 2 * i:6 + 2 * i, :]
        b.tags, b.free, b.pt_free = k.tags[:, 2 * i:2 * i + 2, :], [], []
        bufs.append(b)
    a = q.act.do(lambda e: e.activation(k.neg_rate[:, :], k.ret_decay[:, :], ACT.Exp), after=[k.params])
    rates = q.dve.do(lambda e: e.tensor_scalar(k.neg_rate[:, :], k.neg_rate[:, :], -1.0, None, ALU.mult), after=[a])
    lam = k.lam
    for i in range(2):
        q.dve.do(lambda e, i=i: e.tensor_tensor(k.lqk[:, 2 * i, :], k.lqk[:, 2 * i, :], k.lqk[:, 2 * i + 1, :], ALU.mult), after=[k.params])
        s = q.dve.do(lambda e, i=i: e.tensor_reduce(lam[:, i:i + 1], k.lqk[:, 2 * i, :], AXX, ALU.add))
    s = q.act.do(lambda e: e.activation(lam[:, 0:2], lam[:, 0:2], ACT.Exp), after=[s])
    q.dve.do(lambda e: e.tensor_tensor(lam[:, 2:3], lam[:, 1:2], lam[:, 0:1], ALU.subtract), after=[s])
    neg_lam = q.dve.do(lambda e: e.tensor_scalar(lam[:, 2:3], lam[:, 2:3], -LAM_INIT, None, ALU.add))
    q.dve.do(lambda e: e.tensor_scalar(k.subln[:, :], k.subln[:, :], 1.0 - LAM_INIT, None, ALU.mult), after=[k.params])
    for i in range(DEPTH):
        for raw_w, (hi, lo) in zip(k.router_raw[i], (k.w_grp[i], k.w_exp[i])):
            q.dve.do(lambda e, raw_w=raw_w, hi=hi: e.tensor_copy(hi[:, :, :], raw_w))
            q.dve.do(lambda e, raw_w=raw_w, hi=hi, lo=lo: e.tensor_tensor(lo[:, :, :], raw_w, hi[:, :, :].bitcast(F32), ALU.subtract))
    router_done = Step(q.dve.sem, q.dve.count)

    q.act.wait(router_done)
    got = Tiles()
    got.raw_free = []
    interleave(rotated(k, q, 8, dq, "dif", raw, got))
    dq_done = got.last
    interleave(rotated(k, q, 10, dk, "dif", raw, got))
    dk_done = got.last
    for c in range(2):
        dv_done = token_major(k, q, ("ev_in", 12 + c), dv[:, :, 256 * c:256 * c + 256])

    def retention_projections():
        yield from rotated(k, q, 0, rq, "ret", raw, got)
        got.rq = got.last
        yield from rotated(k, q, 2, rk, "ret", raw, got)
        got.rk = got.last
        for c in range(2):
            got.rv = token_major(k, q, ("ev_in", 4 + c), rv[:, :, 256 * c:256 * c + 256])
            yield
        for c in range(2):
            got.gate = token_major(k, q, ("ev_in", 6 + c), gate[:, :, 256 * c:256 * c + 256])
            yield

    o_banks, o_steps = [k.banks_o.take() for _ in range(NB)], [None] * HEADS
    ready = [dq_done, dk_done, dv_done]
    interleave(*[diff_heads(k, q, (2 * i, 2 * i + 1), bufs[i], dq, dk, dv, ready, neg_lam, o_banks, o_steps) for i in range(2)],
               retention_projections())
    got.gate = silu_in_place(k, q, gate, got.gate)
    last = [o_steps[3][tb] for tb in range(NB)]
    ss = sums_of_squares(k, q, [b.tile for b in o_banks], last, HEADS, HD, k.hrs)
    rs = rms_scale(k, q, k.hrs, 8, HD, RMS_EPS, ss)
    for tb in range(NB):
        for h in range(HEADS):
            i = tb * HEADS + h
            done = q.dve.do(lambda e, tb=tb, h=h, i=i, o_banks=o_banks: e.scalar_tensor_tensor(
                out=y[:, tb, 512 + h * HD:512 + (h + 1) * HD], in0=o_banks[tb].tile[:, h * HD:(h + 1) * HD], scalar=k.hrs[:, i:i + 1],
                in1=k.subln[:, :], op0=ALU.mult, op1=ALU.mult), after=[rs], chain=h == 0)
        o_banks[tb].free = [done]

    o_banks, o_steps = [k.banks_o.take() for _ in range(NB)], [None] * HEADS
    mixed = []

    def diff_out():
        yield
        yield
        mixed.extend(mix_transposes(k, q, y[:, :, 512:1024], 4, [done]))

    ready = [got.rq, got.rk, got.rv]
    interleave(*[retention_heads(k, q, (2 * i, 2 * i + 1), bufs[i], rq, rk, rv, ready, rates, o_banks, o_steps) for i in range(2)], diff_out())
    for tb in range(NB):
        for h in range(HEADS):
            i = tb * HEADS + h
            q.dve.do(lambda e, tb=tb, h=h, i=i, o_banks=o_banks: e.bn_stats(k.hbn[:, i, :], o_banks[tb].tile[:, h * HD:(h + 1) * HD]), after=[o_steps[3][tb]],
                     chain=False)
        for h in range(HEADS):
            i = tb * HEADS + h
            q.dve.do(lambda e, i=i: e.bn_aggr(k.hmv[:, i, :], k.hbn[:, i, :]), chain=h == 0)
    var = q.dve.do(lambda e: e.tensor_scalar(k.hrs[:, 0:8], k.hmv[:, :, 1], LN_EPS, None, ALU.add))
    rs = q.pool.do(lambda e: e.tensor_tensor(k.hrs[:, 0:8], k.hrs[:, 0:8], k.neg_half[:, 0:8], ALU.pow), after=[var])
    for tb in range(NB):
        for h in range(HEADS):
            i = tb * HEADS + h
            done = q.dve.do(lambda e, tb=tb, h=h, i=i, o_banks=o_banks: e.tensor_scalar(
                y[:, tb, h * HD:(h + 1) * HD], o_banks[tb].tile[:, h * HD:(h + 1) * HD], k.hmv[:, i, 0:1], k.hrs[:, i:i + 1],
                ALU.subtract, ALU.mult), after=[rs], chain=h == 0)
        o_banks[tb].free = [done]
    done = q.dve.do(lambda e: e.tensor_tensor(y[:, :, 0:512], y[:, :, 0:512], gate, ALU.mult), after=[got.gate])
    return out_projection(k, q, "ev_out", mixed + mix_transposes(k, q, y, 0, [done]))


def probabilities_times_v(k, q, p, pt, p_ready, pt_free, v, h, v_ready, o_banks):
    bank = k.banks_b.take()
    view = bank.tile[:, :].rearrange("p (a b) -> p a b", a=NB)
    step = transposes(q, bank, k.ident, [(view[:, kb, b * P:(b + 1) * P], p[:, b, kb * P:(kb + 1) * P])
                                         for kb in range(NB) for b in range(NB)], after=[p_ready])
    for s in pt_free:
        q.act.wait(s)
    got = evacuate(k, q, bank, step, pt, view)
    out = []
    for tb in range(NB):
        out.append(product(q, o_banks[tb], [(o_banks[tb].tile[:, h * HD:(h + 1) * HD],
                                             [(pt[:, kb, tb * P:(tb + 1) * P], v[:, kb, h * HD:(h + 1) * HD]) for kb in range(NB)])],
                           after=[got, v_ready]))
    return step, out


def decayed_scores(k, q, la, qT, kT, heads_on, sides, diag, cross, ready, forward, first, work, refs, got):
    n = la.shape[1]
    b, f, qf, kf = work
    flat = lambda a: a.rearrange("p a b -> p (a b)")
    if forward:
        q.dve.do(lambda e: e.tensor_tensor_scan(flat(b), k.tab("scan")[:, 0:n * T], flat(la), 0.0, ALU.mult, ALU.add), after=ready)
        tot = b[:, :, CHUNK - 1::CHUNK]
    else:
        q.dve.do(lambda e: e.tensor_tensor(flat(f)[:, 1:n * T], flat(la)[:, 0:n * T - 1], k.tab("scan")[:, 1:n * T], ALU.mult), after=ready)
        q.dve.do(lambda e: e.memset(flat(f)[:, 0:1], 0.0))
        q.dve.do(lambda e: e.tensor_tensor_scan(flat(b), k.tab("scan")[:, 0:n * T], flat(f), 0.0, ALU.mult, ALU.add))
        q.dve.do(lambda e: e.tensor_tensor(refs[:, 2, 0:n, :], b[:, :, CHUNK - 1::CHUNK], la[:, :, CHUNK - 1::CHUNK], ALU.add))
        tot = refs[:, 2, 0:n, :]
    yield
    q.dve.do(lambda e: e.memset(refs[:, 0:2, :, :], 0.0))
    q.dve.do(lambda e, tot=tot: e.tensor_copy(refs[:, 0, 0:n, 0::2], tot[:, :, 0::2]))
    q.dve.do(lambda e, tot=tot: e.tensor_copy(refs[:, 1, 0:n, 1:2], tot[:, :, 1:2]), chain=False)
    q.dve.do(lambda e, tot=tot: e.tensor_tensor(refs[:, 1, 0:n, 0:1], tot[:, :, 0:1], tot[:, :, 1:2], ALU.add), chain=False)
    q.dve.do(lambda e, tot=tot: e.tensor_scalar(refs[:, 1, 0:n, 3:4], tot[:, :, 2:3], -1.0, None, ALU.mult), chain=False)
    mask_base = 0 if forward else len(LEVELS)

    def blockwise(lhs, rhs, mask, after):
        steps, copies = [], []
        for side in sides:
            bank = k.banks_b.take()
            view = bank.tile[:, :].rearrange("p (a b) -> p a b", a=4)
            groups = []
            for i in range(2):
                r, j = heads_on(side, i)
                for blk in range(NB):
                    ts = slice(blk * P, (blk + 1) * P)
                    groups.append((view[:, 2 * i + blk, :], [(lhs[r, j, ts], rhs[r, j, ts])]))
            step = product(q, bank, groups, after=after)
            steps.append(step)

            def copy(side=side, bank=bank, view=view, step=step):
                done = q.dve.do(lambda e: e.copy_predicated(diag[:, side, :, :], mid_bcast(mask, 4), view), after=[step] + first)
                bank.free = [done]

            copies.append(copy)
        return steps, copies

    def factor(m, free):
        size = 1 << m
        if m >= 7:
            mid, width = refs[:, m - 7, 0:n, :].rearrange("p a b -> p (a b)"), CHUNK
        else:
            mid, width = flat(b)[:, size // 2 - (1 if forward else 0)::size], size
        bv, fv = (flat(a).rearrange("p (a b) -> p a b", b=width) for a in (b, f))
        d = q.dve.do(lambda e, mid=mid, width=width: e.tensor_tensor(fv, bv, bcast(mid, width), ALU.subtract), after=free)
        if len(sides) == 2:
            d = q.dve.do(lambda e: e.scalar_tensor_tensor(out=flat(f), in0=flat(f), scalar=-1.0, in1=flat(f), op0=ALU.mult, op1=ALU.min))
            return q.act.do(lambda e: e.activation(flat(f), flat(f), ACT.Exp), after=[d])
        q.act.do(lambda e: e.activation(flat(f), flat(f), ACT.Abs), after=[d])
        return q.act.do(lambda e: e.activation(flat(f), flat(f), ACT.Exp, scale=-1.0))

    copies = blockwise(kT, qT, k.masks[:, 2 * len(LEVELS), :], ready)[1] if forward else []
    levels = (8,) + LEVELS
    ex = factor(levels[0], [])
    factors_free = []
    for m in levels:
        yield
        qd = q.dve.do(lambda e: e.tensor_tensor(flat(qf), flat(f), flat(qT), ALU.mult), after=[ex] + factors_free)
        kd = q.pool.do(lambda e: e.tensor_tensor(flat(kf), flat(f), flat(kT), ALU.mult), after=[ex] + factors_free + ready)
        for copy in copies:
            copy()
        if m == 8:
            sb, tb = (0, 1) if forward else (1, 0)
            factors_free, copies = [], []
            for side in sides:
                bank = k.banks_b.take()
                view = bank.tile[:, 0:2 * P].rearrange("p (a b) -> p a b", a=2)
                groups = []
                for i in range(2):
                    r, j = heads_on(side, i)
                    groups.append((view[:, i, :], [(kf[r, j, sb * P:(sb + 1) * P], qf[r, j, tb * P:(tb + 1) * P])]))
                step = product(q, bank, groups, after=[qd, kd])
                factors_free.append(step)
                copies.append(lambda side=side, bank=bank, view=view, step=step: got.append(evacuate(k, q, bank, step, cross[:, side, :, :], view)))
        else:
            factors_free, copies = blockwise(kf, qf, k.masks[:, mask_base + LEVELS.index(m), :], [qd, kd])
        if m > 1:
            ex = factor(m - 1, [kd])
    yield
    for copy in copies:
        copy()
    got.append(Step(q.dve.sem, q.dve.count))


def decayed_values(k, q, diag, crosses, head_of, v, ready):
    o_banks = [k.banks_o.take() for _ in range(NB)]
    steps = []
    for tb in range(NB):
        groups = []
        for side in range(2):
            for i in range(2):
                h = head_of(side, i)
                vs = slice(h * HD, (h + 1) * HD)
                parts = [(diag[:, side, 2 * i + tb, :], v[:, tb, vs])]
                if crosses[tb] is not None:
                    parts.append((crosses[tb][:, side, i, :], v[:, 1 - tb, vs]))
                groups.append((o_banks[tb].tile[:, vs], parts))
        steps.append(product(q, o_banks[tb], groups, after=ready))
    return o_banks, steps


def silu_in_place(k, q, gate, ready):
    return q.act.do(lambda e: e.activation(gate, gate, ACT.Silu), after=[ready])


def gated_rms(k, q, o_banks, steps, gain, gate, gate_ready, y):
    ss = sums_of_squares(k, q, [b.tile for b in o_banks], steps, HEADS, HD, k.hrs)
    rs = rms_scale(k, q, k.hrs, 8, HD, RMS_EPS, ss)
    for tb in range(NB):
        for h in range(HEADS):
            i = tb * HEADS + h
            got = q.dve.do(lambda e, tb=tb, h=h, i=i: e.scalar_tensor_tensor(
                out=y[:, tb, h * HD:(h + 1) * HD], in0=o_banks[tb].tile[:, h * HD:(h + 1) * HD], scalar=k.hrs[:, i:i + 1],
                in1=gain, op0=ALU.mult, op1=ALU.mult), after=[rs, k.params], chain=h == 0)
        o_banks[tb].free = [got]
    return q.dve.do(lambda e: e.tensor_tensor(y[:, :, 0:512], y[:, :, 0:512], gate, ALU.mult), after=[gate_ready])


def log_sigmoid(k, q, z, tmp, ready):
    a = q.dve.do(lambda e: e.scalar_tensor_tensor(out=tmp, in0=z, scalar=-1.0, in1=z, op0=ALU.mult, op1=ALU.min), after=ready)
    q.act.do(lambda e: e.activation(tmp, tmp, ACT.Exp), after=[a])
    return q.act.do(lambda e: e.activation(tmp, tmp, ACT.Ln, bias=1.0))


def mla_gla_mixer(k, q):
    A = k.arena
    A.restart()
    y = k.acc
    gla_v, gate = A.take(NB, 512), A.take(NB, 512)
    gq, gk = A.take(2, T), A.take(2, T)
    gla_end = A.at
    cq, ckv = A.take(NB, MLA_QR), A.take(NB, MLA_KVR)
    cqT, ckvT = A.take(2, T), A.take(1, T)
    A.at = gla_end
    bufs = [Tiles(), Tiles()]
    bufs[1].e1, bufs[1].pt = A.take(NB, T), A.take(NB, T)
    A.at = gla_end + 3 * NB * T
    qh, kh = A.take(HEADS, T), A.take(HEADS, T)
    v = A.take(NB, 512)
    bufs[0].e1, bufs[0].pt = A.take(NB, T), A.take(NB, T)
    narrow = k.rot_tmp[:, 0:NB * P].rearrange("p (a b) -> p a b", a=NB)
    mla_end = A.at
    lr_at = A.words - T
    assert mla_end <= lr_at
    A.at = lr_at
    narrow_T = A.take(1, T)
    bank, step = project(k, q, ("od_in", 0), "tok")
    sq = sums_of_squares(k, q, [bank.tile[:, b * 256:(b + 1) * 256] for b in range(NB)], [step, step], 1, MLA_QR, k.hrs)
    kv_cols = MLA_KVR + MLA_ROPE
    bank2, step2 = project(k, q, ("od_in", 1), "tok")
    sk = sums_of_squares(k, q, [bank2.tile[:, b * kv_cols:b * kv_cols + MLA_KVR] for b in range(NB)], [step2, step2], 1, MLA_KVR, k.hrs[:, 8:10])
    rs = rms_scale(k, q, k.hrs, 2, MLA_QR, RMS_EPS, sq)
    rk = rms_scale(k, q, k.hrs[:, 8:10], 2, MLA_KVR, RMS_EPS, sk)
    for b in range(NB):
        a = q.dve.do(lambda e, b=b, bank=bank: e.tensor_scalar(cq[:, b, :], bank.tile[:, b * 256:(b + 1) * 256], k.hrs[:, b:b + 1], None, ALU.mult), after=[rs])
    bank.free = [a]
    for b in range(NB):
        c = q.dve.do(lambda e, b=b: e.tensor_scalar(ckv[:, b, :], bank2.tile[:, b * kv_cols:b * kv_cols + MLA_KVR], k.hrs[:, 8 + b:9 + b], None, ALU.mult), after=[rk])
    ropes = slice(MLA_NOPE, MLA_QD)
    kr_raw = narrow_T[ropes, 0:1, :]
    q.dve.do(lambda e: e.memset(narrow, 0.0))
    kr = q.dve.do(lambda e: e.tensor_copy(narrow[:, :, ropes], bank2.tile[:, 0:NB * kv_cols].rearrange("p (a b) -> p a b", a=NB)[:, :, MLA_KVR:kv_cols]))
    bank2.free = [kr]
    lr_bank, step = project(k, q, ("od_in", 2), "tok")
    lr_view = lr_bank.tile[:, 0:NB * 2 * GATE_RANK].rearrange("p (a b) -> p a b", a=NB)
    for way in range(2):
        got = q.dve.do(lambda e, way=way: e.tensor_copy(narrow[:, :, 32 * way:32 * way + GATE_RANK], lr_view[:, :, GATE_RANK * way:GATE_RANK * (way + 1)]),
                       after=[step])
    lr_bank.free = [got]
    bank_n = k.banks.take()
    step = transposes(q, bank_n, k.ident, [(bank_n.tile[:, b * P:(b + 1) * P], narrow[:, b, :]) for b in range(NB)], after=[got])
    kr = lr_done = evacuate(k, q, bank_n, step, narrow_T[:, 0, :], bank_n.tile[:, 0:T], engine="dve")
    tb_bank = k.banks.take()
    view = tb_bank.tile[:, :].rearrange("p (a b) -> p a b", a=2)
    step = transposes(q, tb_bank, k.ident, [(view[:, j, b * P:(b + 1) * P], cq[:, b, j * P:(j + 1) * P]) for j in range(2) for b in range(NB)], after=[a])
    for j in range(2):
        cq_done = q.dve.do(lambda e, j=j, view=view: e.tensor_scalar(cqT[:, j, :], view[:, j, :], k.q_norm[:, j:j + 1], None, ALU.mult), after=[step, k.params])
    tb_bank.free = [cq_done]
    tb2 = k.banks.take()
    step = transposes(q, tb2, k.ident, [(tb2.tile[:, b * P:(b + 1) * P], ckv[:, b, :]) for b in range(NB)], after=[c])
    ckv_done = q.dve.do(lambda e: e.tensor_scalar(ckvT[:, 0, :], tb2.tile[:, 0:T], k.kv_norm[:, 0:1], None, ALU.mult), after=[step])
    tb2.free = [ckv_done]
    for pair in range(2):
        bank = k.banks.take()
        groups = [(bank.tile[0:MLA_QD, i * T:(i + 1) * T],
                   [(k.w_uq[:, j, (2 * pair + i) * MLA_QD:(2 * pair + i + 1) * MLA_QD], cqT[:, j, :]) for j in range(2)]) for i in range(2)]
        step = product(q, bank, groups, after=[cq_done, k.params])
        src = bank.tile[0:MLA_QD, :].rearrange("p (a b) -> p a b", a=2)
        q_raw = evacuate(k, q, bank, step, qh[0:MLA_QD, 2 * pair:2 * pair + 2, :], src)
        bank = k.banks.take()
        groups = [(bank.tile[0:MLA_NOPE, i * T:(i + 1) * T], [(k.w_ukv[:, (2 * pair + i) * 192:(2 * pair + i) * 192 + MLA_NOPE], ckvT[:, 0, :])])
                  for i in range(2)]
        step = product(q, bank, groups, after=[ckv_done])
        src = bank.tile[0:MLA_NOPE, :].rearrange("p (a b) -> p a b", a=2)
        k_raw = evacuate(k, q, bank, step, kh[0:MLA_NOPE, 2 * pair:2 * pair + 2, :], src)
        bank = k.banks.take()
        groups = [(bank.tile[:, (b * 2 + i) * HD:(b * 2 + i + 1) * HD],
                   [(ckvT[:, 0, b * P:(b + 1) * P], k.w_ukv[:, (2 * pair + i) * 192 + MLA_NOPE:(2 * pair + i + 1) * 192])])
                  for b in range(NB) for i in range(2)]
        step = product(q, bank, groups, after=[ckv_done])
        v_done = evacuate(k, q, bank, step, v[:, :, 256 * pair:256 * pair + 256], bank.tile[:, :].rearrange("p (a b) -> p a b", a=2), engine="dve")
    cos, sin, swap = (k.tab(n)[ropes, :] for n in ("mla_cos", "mla_sin", "mla_swap"))
    for pair in range(2):
        part = qh[ropes, 2 * pair:2 * pair + 2, :]
        bank = k.banks.take()
        view = bank.tile[ropes, :].rearrange("p (a b) -> p a b", a=2)
        step = product(q, bank, [(view[:, i, :], [(swap, part[:, i, :])]) for i in range(2)], after=[q_raw])
        t2 = k.rot_tmp[ropes, :].rearrange("p (a b) -> p a b", a=2)
        g = q.dve.do(lambda e, view=view, t2=t2: e.tensor_tensor(t2, view, mid_bcast(sin, 2), ALU.mult), after=[step])
        bank.free = [g]
        q.dve.do(lambda e, part=part: e.tensor_tensor(part, part, mid_bcast(cos, 2), ALU.mult))
        q_done = q.dve.do(lambda e, part=part, t2=t2: e.tensor_tensor(part, part, t2, ALU.add))
    bank = k.banks.take()
    step = product(q, bank, [(bank.tile[ropes, 0:T], [(swap, kr_raw[:, 0, :])])], after=[kr])
    g = q.dve.do(lambda e, bank=bank: e.tensor_tensor(k.rot_tmp[ropes, 0:T], bank.tile[ropes, 0:T], sin, ALU.mult), after=[step])
    bank.free = [g]
    q.dve.do(lambda e: e.tensor_tensor(kr_raw[:, 0, :], kr_raw[:, 0, :], cos, ALU.mult))
    k_done = q.dve.do(lambda e: e.tensor_tensor(kh[ropes, :, :], mid_bcast(kr_raw[:, 0, :], HEADS), mid_bcast(k.rot_tmp[ropes, 0:T], HEADS), ALU.add))
    mixed = []

    def attention(pair):
        b, tags, free, pt_free = bufs[pair], k.tags[:, pair, :], [], []
        out_bank = k.banks_o.take()
        for i in range(2):
            h = 2 * pair + i
            bank = k.banks_b.take()
            view = bank.tile[:, :].rearrange("p (a b) -> p a b", a=NB)
            step = product(q, bank, [(view[:, c, :], [(qh[0:MLA_QD, h, c * P:(c + 1) * P], kh[0:MLA_QD, h, :])]) for c in range(NB)],
                           after=[q_done, k_done, k_raw, v_done])
            ex = softmax_rows(k, q, bank, step, b.e1, MLA_QD ** -0.5, tags, free)
            yield
            q.dve.do(lambda e: e.reciprocal(tags[:, 6:8], tags[:, 4:6]), after=[ex])
            for c in range(NB):
                p = q.dve.do(lambda e, c=c: e.tensor_scalar(b.e1[:, c, :], b.e1[:, c, :], tags[:, 6 + c:7 + c], None, ALU.mult), chain=c == 0)
            yield
            bank = k.banks_b.take()
            view = bank.tile[:, :].rearrange("p (a b) -> p a b", a=NB)
            step = transposes(q, bank, k.ident, [(view[:, kb, c * P:(c + 1) * P], b.e1[:, c, kb * P:(kb + 1) * P])
                                                 for kb in range(NB) for c in range(NB)], after=[p])
            free = [step, p]
            for x in pt_free:
                q.act.wait(x)
            turned = evacuate(k, q, bank, step, b.pt, view)
            yield
            step = product(q, out_bank, [(out_bank.tile[:, i * T:(i + 1) * T],
                                          [(v[:, kb, h * HD:(h + 1) * HD], b.pt[:, kb, :]) for kb in range(NB)])], after=[turned])
            pt_free = [step]
            yield
        mixed.append(evacuate(k, q, out_bank, step, k.mixT[:, 2 * pair:2 * pair + 2, :], out_bank.tile[:, :].rearrange("p (a b) -> p a b", a=2)))

    G = Tiles()

    def gla_projections():
        for c, dst, scale in ((3, gq, 64 ** -0.5), (4, gk, None)):
            bank, step = project(k, q, ("od_in", c), "feat")
            done = evacuate(k, q, bank, step, dst, bank.tile[:, :].rearrange("p (a b) -> p a b", a=2), scale=scale)
            if c == 3:
                G.q_done = done
            yield
        G.k_done = done
        for c in range(2):
            G.v_done = token_major(k, q, ("od_in", 5 + c), gla_v[:, :, 256 * c:256 * c + 256])
            yield
        for c in range(2):
            G.gate = token_major(k, q, ("od_in", 7 + c), gate[:, :, 256 * c:256 * c + 256])
            yield

    interleave(attention(0), attention(1), gla_projections())

    A.at = gla_end
    diag = A.take(2, 4, P)
    crosses = [k.mixT[:, 4 + 2 * i:6 + 2 * i, :].rearrange("p a (b c) -> p a b c", b=2) for i in range(2)]
    la = [A.take(2, T), A.take(2, T)]
    work = [[A.take(2, T) for _ in range(4)] for _ in range(2)]
    assert A.at <= lr_at
    for x in mixed + [Step(q.pe.sem, q.pe.count)]:
        for queue in (q.act, q.dve, q.pool):
            queue.wait(x)
    q.act.wait(Step(q.dve.sem, q.dve.count))
    q.dve.wait(Step(q.act.sem, q.act.count))
    clear = q.dve.do(lambda e: e.memset(diag.rearrange("p a b c -> p (a b c)"), 0.0))
    rows_of = lambda side, i: (slice(64 * side, 64 * side + 64), i)
    steps = []
    for way in range(2):
        zt = work[way][0]
        bank = k.banks.take()
        view = bank.tile[:, :].rearrange("p (a b) -> p a b", a=2)
        step = product(q, bank, [(view[:, j, :], [(k.gla_w2[32 * way:32 * way + GATE_RANK, j * P:(j + 1) * P], narrow_T[32 * way:32 * way + GATE_RANK, 0, :])]) for j in range(2)],
                       after=[lr_done, k.params])
        for j in range(2):
            z = q.dve.do(lambda e, way=way, j=j, zt=zt, view=view: e.tensor_scalar(zt[:, j, :], view[:, j, :], k.gla_b[:, way, j:j + 1], None, ALU.add), after=[step])
        bank.free = [z]
        steps.append(q.dve.do(lambda e, way=way, zt=zt: e.scalar_tensor_tensor(out=la[way], in0=zt, scalar=-1.0, in1=zt, op0=ALU.mult, op1=ALU.min)))
    for func, bias in ((ACT.Exp, 0.0), (ACT.Ln, 1.0)):
        for way in range(2):
            steps[way] = q.act.do(lambda e, way=way, func=func, bias=bias: e.activation(la[way], la[way], func, bias=bias), after=[steps[way]])
    for way in range(2):
        zt = work[way][0]
        q.dve.do(lambda e, way=way, zt=zt: e.scalar_tensor_tensor(out=la[way], in0=zt, scalar=0.0, in1=la[way], op0=ALU.min, op1=ALU.subtract),
                 after=[steps[way]])
        steps[way] = q.dve.do(lambda e, way=way: e.tensor_scalar(la[way], la[way], 1.0 / GLA_TAU, None, ALU.mult))
    done = []
    interleave(*[decayed_scores(k, q, la[way], gq, gk, rows_of, (0, 1), diag, crosses[way], [G.q_done, G.k_done, steps[way]], way == 0,
                                [clear], work[way], k.refs[way], done) for way in range(2)])
    gate_done = silu_in_place(k, q, gate, G.gate)
    o_banks, o_steps = decayed_values(k, q, diag, (crosses[1], crosses[0]), lambda side, i: 2 * i + side, gla_v, done + [G.v_done])
    got = gated_rms(k, q, o_banks, o_steps, k.gla_norm[:, :], gate, gate_done, y)
    return out_projection(k, q, "od_out", mixed + mix_transposes(k, q, y, 4, [got]))


def pool_hgrn_mixer(k, q, layer):
    A = k.arena
    A.restart()
    y = k.acc
    gate, v = A.take(NB, 512), A.take(NB, 512)
    qT, kT, la = A.take(HEADS, T), A.take(HEADS, T), A.take(HEADS, T)
    diag, cross = A.take(2, 4, P), A.take(2, 2, P)
    work = [A.take(HEADS, T) for _ in range(3)] + [k.mixT[:, 4:8, :]]
    f = work[0]
    u = work[2].rearrange("p a b -> p (a b)").rearrange("p (a b) -> p a b", a=NB)
    for c in range(2):
        bank, step = project(k, q, ("in2", 4 + c), "feat")
        f_done = evacuate(k, q, bank, step, f[:, 2 * c:2 * c + 2, :], bank.tile[:, :].rearrange("p (a b) -> p a b", a=2))
    for c in range(2):
        bank, step = project(k, q, ("in2", c), "tok")
        u_done = evacuate(k, q, bank, step, u[:, :, 256 * c:256 * c + 256], bank.tile[:, :].rearrange("p (a b) -> p a b", a=NB))
    for c in range(2):
        bank, step = project(k, q, ("in2", 2 + c), "feat")
        q_done = evacuate(k, q, bank, step, qT[:, 2 * c:2 * c + 2, :], bank.tile[:, :].rearrange("p (a b) -> p a b", a=2), scale=HD ** -0.5)
    pooled = work[3]
    mixed = []
    for half in range(2):
        bank = k.banks.take()
        groups = [(bank.tile[:, i * T:(i + 1) * T],
                   [(u[:, sb, (2 * half + i) * P:(2 * half + i + 1) * P], k.pool_mat[:, sb, 2 * half + i, :]) for sb in range(NB)]) for i in range(2)]
        step = product(q, bank, groups, after=[u_done, k.pool_here])
        p_done = evacuate(k, q, bank, step, pooled[:, 2 * half:2 * half + 2, :], bank.tile[:, :].rearrange("p (a b) -> p a b", a=2))
        bank = k.banks.take()
        groups = [(bank.tile[:, i * T:(i + 1) * T], [(k.pool_w[:, layer, 2 * half + i, :], pooled[:, 2 * half + i, :])]) for i in range(2)]
        step = product(q, bank, groups, after=[p_done])
        for i in range(2):
            g = 2 * half + i
            got = q.act.do(lambda e, g=g, i=i, bank=bank: e.activation(k.mixT[:, g, :], bank.tile[:, i * T:(i + 1) * T], ACT.Copy,
                                                            scale=k.pool_scale[:, layer, g:g + 1]), after=[step])
        bank.free = [got]
        mixed.append(got)
    ln = log_sigmoid(k, q, f, la, [f_done])
    a = q.dve.do(lambda e: e.tensor_scalar(kT, f, -1.0, 0.0, ALU.mult, ALU.min), after=[ln])
    a = q.dve.do(lambda e: e.tensor_tensor(kT, kT, la, ALU.subtract))
    kk = q.act.do(lambda e: e.activation(kT, kT, ACT.Exp), after=[a])
    la_done = q.dve.do(lambda e: e.scalar_tensor_tensor(out=la, in0=f, scalar=0.0, in1=la, op0=ALU.min, op1=ALU.subtract))
    if layer == 1:
        lbp, lbd = k.lb_param, k.lb_work
        q.dve.do(lambda e: e.tensor_tensor(lbd[:, 0, :], lbp[:, 1, :], lbp[:, 0, :], ALU.subtract), after=[k.params])
        d = log_sigmoid(k, q, lbd[:, 0, :], lbd[:, 1, :], [])
        q.dve.do(lambda e: e.scalar_tensor_tensor(out=lbd[:, 2, :], in0=lbd[:, 0, :], scalar=0.0, in1=lbd[:, 1, :], op0=ALU.min, op1=ALU.subtract), after=[d])
        q.dve.do(lambda e: e.tensor_scalar(lbd[:, 3, :], lbd[:, 0, :], -1.0, 0.0, ALU.mult, ALU.min))
        d = q.dve.do(lambda e: e.tensor_tensor(lbd[:, 3, :], lbd[:, 3, :], lbd[:, 1, :], ALU.subtract))
        one = q.act.do(lambda e: e.activation(lbd[:, 0, :], lbd[:, 3, :], ACT.Exp), after=[d])
        kk = q.dve.do(lambda e: e.tensor_tensor(kT, kT, bcast(lbd[:, 0, :], T), ALU.mult), after=[one, kk])
        q.dve.do(lambda e: e.tensor_tensor(la, la, bcast(lbd[:, 3, :], T), ALU.add))
        q.dve.do(lambda e: e.tensor_tensor(f, la, bcast(lbd[:, 2, :], T), ALU.subtract))
        d = log_sigmoid(k, q, f, work[1], [])
        q.dve.do(lambda e: e.tensor_tensor(la, la, bcast(lbd[:, 2, :], T), ALU.max))
        la_done = q.dve.do(lambda e: e.tensor_tensor(la, la, work[1], ALU.add), after=[d])
    clear = q.dve.do(lambda e: e.memset(diag.rearrange("p a b c -> p (a b c)"), 0.0))
    for queue in (q.dve, q.pool, q.act):
        queue.wait(mixed[-1])

    G = Tiles()

    def value_projections():
        for c in range(2):
            G.v_done = token_major(k, q, ("in2", 6 + c), v[:, :, 256 * c:256 * c + 256])
            for _ in range(2):
                yield
        for c in range(2):
            G.gate = token_major(k, q, ("in2", 8 + c), gate[:, :, 256 * c:256 * c + 256])
            for _ in range(2):
                yield

    done = []
    heads = [slice(2 * s, 2 * s + 2) for s in range(2)]
    interleave(*[decayed_scores(k, q, la[:, hs, :], qT[:, hs, :], kT[:, hs, :], lambda side, i: (slice(0, P), i), (s,), diag, cross,
                                [q_done, kk, la_done], True, [clear], [w[:, hs, :] for w in work], k.refs[s], done)
                 for s, hs in enumerate(heads)], value_projections())
    gate_done = silu_in_place(k, q, gate, G.gate)
    o_banks, o_steps = decayed_values(k, q, diag, (None, cross), lambda side, i: 2 * side + i, v, done + [G.v_done])
    got = gated_rms(k, q, o_banks, o_steps, k.hgrn_g[:, layer, :], gate, gate_done, y)
    return out_projection(k, q, "out2", mixed + mix_transposes(k, q, y, 4, [got]))


class FfnWeights:

    def __init__(self, k, q):
        self.k, self.q, self.chunk, self.ready = k, q, {}, []
        self.order = [part for f in range(FT + FFN_LAG)
                      for part in [("gate", f), ("up", f)] * (f < FT) + [("down", f - FFN_LAG)] * (f >= FFN_LAG)]
        self.fill()

    def fill(self):
        k, q = self.k, self.q
        while self.order and len(self.ready) < PARTS:
            name, tile = self.order.pop(0)
            if tile % 2 == 0 and name != "up":
                for part in ("gate", "up") if name == "gate" else ("down",):
                    self.chunk[part] = k.ring.next((part, tile // 2))
            n, w, here = self.chunk[name]
            src = w[:, :, (tile % 2) * P:(tile % 2 + 1) * P] if name != "down" else w[:, tile % 2:tile % 2 + 1, :]
            parts = k.split.split(q, src, here)
            self.ready.append(((name, tile), parts))
            if tile % 2 == 1:
                k.ring.release(n, parts[3])

    def take(self, name, tile):
        assert self.ready[0][0] == (name, tile)
        return self.ready[0][1]

    def used(self, buffer, step):
        self.k.split.free[buffer] = [step]
        self.ready.pop(0)
        self.fill()


def ffn(k, q, weights):
    A = k.arena
    silu, hidden = k.ffn_tmp[0], k.ffn_tmp[1]
    out_banks, work_banks = k.all_banks[0:4], Banks(k.all_banks[4:8])
    for x in after_everything(q):
        q.act.wait(x)
        q.dve.wait(x)
    for tb in range(NB):
        scaled = q.dve.do(lambda e, tb=tb: e.tensor_scalar(k.acc[:, tb, :], k.x_tok[:, tb, :], ALPHA, None, ALU.mult), after=k.x_ready)
    h_done = [None] * FT
    silu_free, slot_free = [[], []], [[] for _ in range(HIDDEN)]
    for f in range(FT + FFN_LAG):
        if f < FT:
            bank = work_banks.take()
            for i, name in enumerate(("gate", "up")):
                b, hi, lo, here = weights.take(name, f)
                step = product(q, bank, [three_passes(bank.tile[:, i * T:(i + 1) * T],
                                                      [((hi[:, j, :], lo[:, j, :]), (k.xh[:, j, :], k.xl[:, j, :])) for j in range(KT)])],
                               after=[here] + k.xT_ready)
                weights.used(b, step)
                if i == 0:
                    gate_step = step
            s, h, u = silu[:, f % 2, :], hidden[:, f % 2, :], bank.tile[:, T:2 * T]
            hh, hl = k.hid_high[:, f % HIDDEN, :], k.hid_low[:, f % HIDDEN, :]
            a = q.act.do(lambda e, s=s, bank=bank: e.activation(s, bank.tile[:, 0:T], ACT.Silu), after=[gate_step, step] + silu_free[f % 2], chain=False)
            h0 = q.dve.do(lambda e, h=h, s=s, u=u: e.tensor_tensor(h, s, u, ALU.mult), after=[a], chain=True)
            bank.free = [h0]
            h1 = q.act.do(lambda e, hh=hh, h=h: e.activation(hh, h, ACT.Copy), after=[h0] + slot_free[f % HIDDEN], chain=False)
            h_done[f] = q.dve.do(lambda e, hl=hl, h=h, hh=hh: e.tensor_tensor(hl, h, hh.bitcast(F32), ALU.subtract), after=[h1], chain=False)
            silu_free[f % 2] = [h_done[f]]
        if f >= FFN_LAG:
            g = f - FFN_LAG
            b, hi, lo, here = weights.take("down", g)

            def emit(e, g=g, hi=hi, lo=lo):
                for tb in range(NB):
                    ts = slice(tb * P, (tb + 1) * P)
                    hh, hl = k.hid_high[:, g % HIDDEN, ts], k.hid_low[:, g % HIDDEN, ts]
                    for n in range(2):
                        cols = slice(BANK * n, BANK * n + BANK)
                        for i, (lhs, rhs) in enumerate(((hh, hi), (hh, lo), (hl, hi))):
                            ins = e.matmul(out_banks[2 * tb + n].tile[:, :], lhs, rhs[:, 0, cols], start=g == 0 and i == 0, stop=g == FT - 1 and i == 2)
                return ins

            step = q.pe.do(emit, after=[here, h_done[g]] + ([s for b in out_banks for s in b.free] if g == 0 else []), chain=False)
            weights.used(b, step)
            slot_free[g % HIDDEN] = [step]
    done = [[], []]
    for tb in range(NB):
        for n in range(2):
            bank = out_banks[2 * tb + n]
            cols = slice(BANK * n, BANK * n + BANK)
            got = q.dve.do(lambda e, tb=tb, cols=cols, bank=bank: e.scalar_tensor_tensor(
                out=k.acc[:, tb, cols], in0=bank.tile[:, :], scalar=0.5, in1=k.acc[:, tb, cols], op0=ALU.mult, op1=ALU.add),
                after=[step, scaled], chain=False)
            bank.free = [got]
            done[tb].append(got)
    return done


def after_everything(q):
    return [Step(e.sem, e.count) for e in (q.pe, q.act, q.dve)]


def route(k, q, layer):
    R = k.route
    bank = k.banks.take()
    lg = bank.tile[:, 0:NB * N_GROUPS].rearrange("p (a b) -> p a b", a=NB)
    le = bank.tile[:, 64:64 + NB * N_EXPERTS].rearrange("p (a b) -> p a b", a=NB)
    groups = []
    for tb in range(NB):
        ts = slice(tb * P, (tb + 1) * P)
        for out, (wh, wl) in ((lg, k.w_grp[layer]), (le, k.w_exp[layer])):
            groups.append(three_passes(out[:, tb, :], [((k.xh[:, i, ts], k.xl[:, i, ts]), (wh[:, i, :], wl[:, i, :])) for i in range(KT)]))
    step = product(q, bank, groups, after=k.xT_ready + [k.params])
    do = q.dve.do
    tt, ts, red = (lambda *a: lambda e: e.tensor_tensor(*a)), (lambda *a: lambda e: e.tensor_scalar(*a)), (lambda *a: lambda e: e.tensor_reduce(*a))
    do(tt(R.gl, lg, mid_bcast(k.b_grp[:, layer, :], NB), ALU.add), after=[step])
    bank.free = [do(tt(R.el, le, mid_bcast(k.b_exp[:, layer, :], NB), ALU.add))]

    def first_of(values, best, onehot, order, n):
        do(red(best, values, AXX, ALU.max))
        do(tt(onehot, values, bcast(best, n), ALU.is_equal))
        do(tt(onehot, onehot, mid_bcast(order, NB), ALU.mult))
        do(red(R.top, onehot, AXX, ALU.max))
        return do(tt(onehot, onehot, bcast(R.top, n), ALU.is_equal))

    first_of(R.gl, R.gmax, R.goh, k.tab("desc_grp"), N_GROUPS)
    d = do(tt(R.gl, R.gl, bcast(R.gmax, N_GROUPS), ALU.subtract))
    ex = q.act.do(lambda e: e.activation(R.gl, R.gl, ACT.Exp), after=[d])
    do(ts(R.goh, R.goh, 1.0, BIG, ALU.subtract, ALU.mult))
    el8 = R.el.rearrange("p a (g e) -> p (a g) e", e=PER_GROUP)
    do(tt(el8, el8, bcast(R.goh.rearrange("p a g -> p (a g)"), PER_GROUP), ALU.add))
    first_of(R.el, R.m1, R.oh1, k.tab("desc_exp"), N_EXPERTS)
    do(lambda e: e.scalar_tensor_tensor(out=R.el, in0=R.oh1, scalar=-BIG, in1=R.el, op0=ALU.mult, op1=ALU.add))
    first_of(R.el, R.m2, R.oh2, k.tab("desc_exp"), N_EXPERTS)
    d = do(tt(R.m2, R.m2, R.m1, ALU.subtract))
    ex2 = q.act.do(lambda e: e.activation(R.m2, R.m2, ACT.Exp), after=[d])
    chosen = do(tt(R.hot, R.oh1, R.oh2, ALU.add))
    bank = k.banks.take()
    view = bank.tile[:, 0:3 * N_EXPERTS].rearrange("p (a b) -> p a b", a=3)
    earlier, ones = k.tab("earlier"), k.tab("ones")
    step = product(q, bank, [(view[:, 0, :], [(earlier, R.hot[:, 0, :])]),
                             (view[:, 1, :], [(earlier, R.hot[:, 1, :]), (ones, R.hot[:, 0, :])]),
                             (view[:, 2, :], [(ones, R.hot[:, 0, :]), (ones, R.hot[:, 1, :])])], after=[chosen])
    do(red(R.top[:, 0:1], view[:, 2, :], AXX, ALU.max), after=[step])
    most = do(lambda e: e.tensor_copy(k.most[0:1, 0:1], R.top[0:1, 0:1]))
    do(lambda e: e.scalar_tensor_tensor(out=k.rank, in0=view[:, 0:2, :], scalar=1.0, in1=R.hot, op0=ALU.add, op1=ALU.mult))
    bank.free = [do(ts(k.rank, k.rank, -1.0, None, ALU.add))]
    do(red(R.gmax, R.gl, AXX, ALU.add), after=[ex])
    do(ts(R.m1, R.m2, 1.0, None, ALU.add), after=[ex2])
    do(tt(R.gmax, R.gmax, R.m1, ALU.mult))
    do(lambda e: e.reciprocal(R.m1, R.gmax))
    do(tt(R.m2, R.m2, R.m1, ALU.mult))
    do(tt(R.oh1, R.oh1, bcast(R.m1, N_EXPERTS), ALU.mult))
    do(tt(R.oh2, R.oh2, bcast(R.m2, N_EXPERTS), ALU.mult))
    routed = do(tt(k.gate_w, R.oh1, R.oh2, ALU.add))
    return routed, most


def expert_buffers(k):
    A = k.arena
    A.restart()
    b = Tiles()
    b.sel = [A.take(NB, P) for _ in range(2)]
    b.sel_w = [A.take(NB, P) for _ in range(2)]
    b.sel_wT = [A.take(T) for _ in range(3)]
    b.xg = [A.take(KT, P) for _ in range(2)]
    b.silu, b.h, b.hT = A.take(BANK), A.take(BANK), A.take(FT_E, P)
    b.y = [A.take(D) for _ in range(2)]
    b.spill = [k.mixT[:, :, :].rearrange("p k t -> p (k t)"), k.pool_or_distance[:, :]]
    return b


def experts(k, q, buf, ring, ready):
    n_pairs = N_EXPERTS // PAIR
    gate_bank, up_bank, y_banks = k.all_banks[0], k.all_banks[1], k.all_banks[2:4]
    work = Banks(k.all_banks[4:8])
    none = []
    sel_step, sel_w_step, xg_step, wT_step, y_step, comb = {}, {}, {}, {}, {}, {}
    gate_step, h_step = {}, {}

    def select(g):
        i = g % 2
        e0 = slice(PAIR * g, PAIR * g + PAIR)
        after = [xg_step[g - 2][1]] if g >= 2 else list(ready)
        for tb in range(NB):
            out = buf.sel[i][:, tb, :].rearrange("p (a b) -> p a b", a=PAIR)
            q.dve.do(lambda e, out=out, tb=tb: e.tensor_tensor(out, mid_bcast(k.tab("slot_no"), PAIR), bcast(k.rank[:, tb, e0], CAP), ALU.is_equal),
                     after=after, chain=False)
        sel_step[g] = Step(q.dve.sem, q.dve.count)
        for tb in range(NB):
            out = buf.sel_w[i][:, tb, :].rearrange("p (a b) -> p a b", a=PAIR)
            src = buf.sel[i][:, tb, :].rearrange("p (a b) -> p a b", a=PAIR)
            sel_w_step[g] = q.dve.do(lambda e, out=out, src=src, tb=tb: e.tensor_tensor(out, src, bcast(k.gate_w[:, tb, e0], CAP), ALU.mult),
                                     after=[wT_step[g - 2][0]] if g >= 2 else [])

    def gather(g):
        i = g % 2
        got = []
        for half in range(2):
            bank = work.take()
            view = bank.tile[:, :].rearrange("p (a b) -> p a b", a=4)
            groups = [(view[:, kk, :], [(k.x_tok[:, tb, (4 * half + kk)::KT], buf.sel[i][:, tb, :]) for tb in range(NB)]) for kk in range(4)]
            step = product(q, bank, groups, after=[sel_step[g]] + k.x_ready)
            if g >= 2:
                (q.act if half == 0 else q.dve).wait(gate_step[g - 2])
            got.append(evacuate(k, q, bank, step, buf.xg[i][:, 4 * half:4 * half + 4, :], view, engine="act" if half == 0 else "dve"))
        xg_step[g] = (got, step)
        bank = work.take()
        step = transposes(q, bank, k.ident, [(bank.tile[:, tb * P:(tb + 1) * P], buf.sel_w[i][:, tb, :]) for tb in range(NB)], after=[sel_w_step[g]])
        if g >= 3:
            q.act.wait(comb[g - 3])
        wT_step[g] = (step, evacuate(k, q, bank, step, buf.sel_wT[g % 3], bank.tile[:, 0:T]))

    def paired(bank_of, name, g, halves, per, lhs, n_cols, after):
        for half in range(halves):
            chunks = [ring.next((name, g, half, j)) for j in range(PAIR)]

            def emit(e, half=half, chunks=chunks):
                for kk in range(per):
                    for n in range(n_cols):
                        for j in range(PAIR):
                            r = slice(CAP * j, CAP * j + CAP)
                            ins = e.matmul(bank_of[n].tile[r, :], lhs[:, half * per + kk, r], chunks[j][1][:, kk, BANK * n:BANK * n + BANK],
                                           start=half == 0 and kk == 0, stop=half == halves - 1 and kk == per - 1)
                return ins

            free = [s for b in bank_of for s in b.free] if half == 0 else []
            step = q.pe.do(emit, after=[c[2] for c in chunks] + free + after, chain=False)
            for c in chunks:
                ring.release(c[0], step)
        return step

    def combine(g):
        i = g % 2
        for tb in range(NB):
            for n in range(2):
                bank = work.take()
                cols = slice(BANK * n, BANK * n + BANK)
                step = product(q, bank, [(bank.tile[:, :], [(buf.sel_wT[g % 3][:, tb * P:(tb + 1) * P], buf.y[i][:, cols])])],
                               after=[wT_step[g][1]] + y_step[g])
                got = q.dve.do(lambda e, tb=tb, cols=cols, bank=bank: e.tensor_tensor(k.acc[:, tb, cols], k.acc[:, tb, cols], bank.tile[:, :], ALU.add),
                               after=[step], chain=True)
                bank.free = [got]
        comb[g] = step
        return got

    select(0)
    gather(0)
    for g in range(n_pairs):
        i = g % 2
        gate_s = paired([gate_bank], "gate", g, 2, KT // 2, buf.xg[i], 1, xg_step[g][0])
        up_s = paired([up_bank], "up", g, 2, KT // 2, buf.xg[i], 1, [])
        gate_step[g] = up_s
        if g + 1 < n_pairs:
            select(g + 1)
        a = q.act.do(lambda e: e.activation(buf.silu, gate_bank.tile[:, :], ACT.Silu), after=[gate_s] + ([h_step[g - 1]] if g else none), chain=False)
        gate_bank.free = [a]
        if g:
            q.dve.wait(comb_hT)
        h_step[g] = q.dve.do(lambda e: e.tensor_tensor(buf.h, buf.silu, up_bank.tile[:, :], ALU.mult), after=[a, up_s], chain=False)
        up_bank.free = [h_step[g]]
        if g + 1 < n_pairs:
            gather(g + 1)
        bank = work.take()
        view = bank.tile[:, :].rearrange("p (a b) -> p a b", a=FT_E)
        step = transposes(q, bank, k.ident, [(view[:, f, :], buf.h[:, f::FT_E]) for f in range(FT_E)], after=[h_step[g]])
        comb_hT = step
        if g:
            q.act.wait(down_step)
        hT = evacuate(k, q, bank, step, buf.hT, view)
        if g:
            combine(g - 1)
        down_step = paired(y_banks, "down", g, 2, FT_E // 2, buf.hT, 2, [hT])
        y_step[g] = []
        for n in range(2):
            eng = q.act if n == 0 else q.dve
            if g >= 2:
                eng.wait(comb[g - 2])
            y_step[g].append(evacuate(k, q, y_banks[n], down_step, buf.y[i][:, BANK * n:BANK * n + BANK], engine="act" if n == 0 else "dve"))
    return combine(n_pairs - 1)


def moe(k, q, layer, nc, new_sem, A):
    routed, most = route(k, q, layer)
    for tb in range(NB):
        base = q.dve.do(lambda e, tb=tb: e.tensor_scalar(k.acc[:, tb, :], k.x_tok[:, tb, :], ALPHA, None, ALU.mult), after=k.x_ready)
    buf = expert_buffers(k)
    last = experts(k, q, buf, k.ring, [routed, base])
    q.play(nc, [k.ring])
    most_value = nc.values_load(k.most[0:1, 0:1], min_val=0, max_val=T)
    with nc.If(most_value > CAP):
        with nc.Fori(1, (most_value + (CAP - 1)) // CAP):
            over = Engines(new_sem, f"over{layer}")
            ring_sems = [over.sem("slot0"), over.sem("slot1")]
            ring = Ring([t for t in buf.spill], ring_sems, moe_plan(A, layer), over.sp)
            saved = [list(b.free) for b in k.all_banks]
            ready, k.x_ready = k.x_ready, []
            for b in k.all_banks:
                b.free = []
            down = over.dve.do(lambda e: e.tensor_scalar(k.rank, k.rank, -float(CAP), None, ALU.add))
            experts(k, over, buf, ring, [down])
            over.play(nc, [ring])
            nums = sorted(s.num for s in over.sems)
            nc.all_engine_barrier(sems_to_clear=range(nums[0], nums[-1] + 1))
            for b, free in zip(k.all_banks, saved):
                b.free = free
            k.x_ready = ready
    return [[last], [last]]


def build(nc, A, out, taps=None):
    table, cols = constant_tables()
    with ExitStack() as ctx:
        ctx.enter_context(nc.allow_non_contiguous_dma("small parameters"))

        def sb(name, shape, dt=F32):
            return ctx.enter_context(nc.sbuf_tensor(name, shape, dt))

        def new_sem(name):
            return ctx.enter_context(nc.semaphore(name))

        k = Tiles()
        tables = sb("tables", [P, table.shape[1]])
        k.tab = lambda name: tables[:, cols[name][0]:cols[name][0] + cols[name][1]]
        k.ident = k.tab("ident")
        k.neg_half = k.tab("neg_half")
        k.masks = sb("level_masks", [P, 2 * len(LEVELS) + 1, P], U8)
        k.x_tok, k.acc = sb("x_tok", [P, NB, D]), sb("acc", [P, NB, D])
        k.mixT = sb("mixT", [P, KT, T])
        k.xh, k.xl = (sb(name, [P, KT, T], F32R) for name in ("xT_high", "xT_low"))
        k.split = Splitter(*[[sb(f"w_{x}{i}", [P, PART], F32R) for i in range(PARTS)] for x in ("high", "low")])
        k.norm_gb = sb("norm_gb", [P, 2, D])
        k.bn, k.mv = sb("bn", [P, NB, 12]), sb("mv", [P, NB, 2])
        k.ve, k.rstd, k.shift = (sb(name, [P, NB]) for name in ("var_eps", "rstd", "shift"))
        k.hbn, k.hmv, k.hrs = sb("head_bn", [P, 8, 6]), sb("head_mv", [P, 8, 2]), sb("head_rs", [P, 16])
        k.tags = sb("softmax_stats", [P, 4, 8])
        k.rot_tmp = sb("rot_tmp", [P, 2 * T])
        k.junk = k.acc[:, 0, 512:512 + T]
        k.refs = [sb(f"level_refs{i}", [P, 3, 2, 4])[:, :, :, :] for i in range(2)]
        k.rank, k.gate_w = (sb(name, [P, NB, N_EXPERTS])[:, :, :] for name in ("rank", "gate_w"))
        k.most = sb("most", [1, 1], I32)
        R = k.route = Tiles()
        R.gl, R.goh = (sb(name, [P, NB, N_GROUPS])[:, :, :] for name in ("group_logits", "group_hot"))
        R.el, R.oh1, R.oh2, R.hot = (sb(name, [P, NB, N_EXPERTS])[:, :, :] for name in ("expert_logits", "first_hot", "second_hot", "chosen_hot"))
        R.gmax, R.m1, R.m2, R.top = (sb(name, [P, NB])[:, :] for name in ("group_max", "first_max", "second_max", "place"))
        k.ret_decay, k.neg_rate = sb("ret_decay", [P, 2 * HEADS]), sb("neg_rate", [P, 2 * HEADS])
        k.lqk, k.lam = sb("lqk", [P, 4, DIFF_D]), sb("lam", [P, 4])
        k.subln, k.gla_norm, k.hgrn_g = sb("subln", [P, HD]), sb("gla_norm", [P, HD]), sb("hgrn_g", [P, DEPTH, HD])
        k.q_norm, k.kv_norm = sb("q_norm", [P, 2]), sb("kv_norm", [P, 1])
        k.gla_b = sb("gla_b", [P, 2, 2])
        k.pool_scale = sb("pool_scale", [P, DEPTH, 4])
        at = cols["ret_cos"][0]
        k.pool_w = tables[:, at:at + DEPTH * 4 * P].rearrange("p (l g n) -> p l g n", l=DEPTH, g=4)
        k.lb_param, k.lb_work = sb("lb_param", [P, DEPTH, 4]), sb("lb_work", [P, 4, 4])
        k.w_grp = [[sb(f"w_grp{i}_{x}", [P, KT, N_GROUPS], F32R) for x in ("high", "low")] for i in range(DEPTH)]
        k.w_exp = [[sb(f"w_exp{i}_{x}", [P, KT, N_EXPERTS], F32R) for x in ("high", "low")] for i in range(DEPTH)]
        k.b_grp, k.b_exp = sb("b_grp", [P, DEPTH, N_GROUPS]), sb("b_exp", [P, DEPTH, N_EXPERTS])
        slots = [sb(f"ring{i}", [P, SLOT]) for i in range(RING)]
        k.pool_or_distance = sb("wide_tables", [P, NB * 4 * T])
        k.distance = k.pool_or_distance[:, 0:2 * NB * T].rearrange("p (w s t) -> p w s t", w=2, s=NB)
        k.pool_mat = k.pool_or_distance[:, :].rearrange("p (s g t) -> p s g t", s=NB, g=4)
        k.w_uq = k.pool_or_distance[:, 0:768].rearrange("p (j n) -> p j n", j=2)
        k.w_ukv = k.pool_or_distance[:, 768:1536]
        k.gla_w2 = k.pool_or_distance[:, 1536:1792]
        words = nc.sbuf_bytes_remaining // 4 // 8 * 8 - 8
        arena = sb("arena", [P, words])
        arena_at = nc.sbuf_base - 4 * words
        k.arena = Arena(arena, words)
        k.ffn_tmp = [arena[:, 2 * T * i:2 * T * (i + 1)].rearrange("p (a b) -> p a b", a=2) for i in range(2)]
        k.hid_high, k.hid_low = (nc.alloc_sbuf_tensor_at(f"hidden_{x}", [P, HIDDEN, T], F32R, offset=arena_at + 4 * T * (4 + HIDDEN * i))
                                 for i, x in enumerate(("high", "low")))
        k.all_banks = [Bank(ctx.enter_context(nc.psum_tensor(f"bank{i}", [P, BANK], F32))) for i in range(8)]
        k.banks, k.banks_o, k.banks_b = Banks(k.all_banks[0:2]), Banks(k.all_banks[2:4]), Banks(k.all_banks[4:8])

        q = Engines(new_sem, "main")
        k.ring = Ring(slots, [new_sem(f"slot{i}_loaded") for i in range(RING)], weight_plan(A), q.sp)
        x_sem, tab_sem, par_sem, wide_sem, out_sem = (new_sem(n) for n in ("x_loaded", "tables_loaded", "params_loaded", "wide_loaded", "out_stored"))
        k.norm_sem = new_sem("norm_loaded")
        k.norm_free, k.norm_no = [], 0
        k.norm_rows = []
        for layer in range(DEPTH):
            k.norm_rows += [(A["ln1_g"][layer], A["ln1_b"][layer]), (A["ln2_g"][layer], A["ln2_b"][layer])]
        for layer in range(DEPTH):
            k.norm_rows += [(A["ln_g_2"][layer, i], A["ln_b_2"][layer, i]) for i in range(3)]

        x_here = q.act.dma(k.x_tok[:, :, :], A["x"][0].rearrange("(b p) d -> p b d", p=P), x_sem, 16)
        q.act.dma(tables[:, :], A["tables"], tab_sem, 16)
        n_masks = 2 * len(LEVELS) + 1
        wide_masks = k.acc[:, :, :].rearrange("p b d -> p (b d)")[:, 0:n_masks * P].rearrange("p (a b) -> p a b", a=n_masks)
        tab_here = q.act.dma(wide_masks, A["masks"], tab_sem, 32)
        k.distance_here = q.act.dma(k.pool_or_distance[:, 0:2 * NB * T], A["distance"], wide_sem, 16)
        raw_at = k.mixT[:, :, :].rearrange("p k t -> p (k t)")
        router_raw = []
        for i in range(DEPTH):
            at = 288 * i
            router_raw.append((raw_at[:, at:at + 32].rearrange("p (k n) -> p k n", k=KT), raw_at[:, at + 32:at + 288].rearrange("p (k n) -> p k n", k=KT)))
        k.router_raw = router_raw
        small = [
            (k.ret_decay[:, 0:HEADS], A["ev_ret_decay_f"][0].partition_broadcast(P)),
            (k.ret_decay[:, HEADS:2 * HEADS], A["ev_ret_decay_b"][0].partition_broadcast(P)),
            (k.subln[:, :], A["ev_subln"][0].partition_broadcast(P)),
            (k.gla_norm[:, :], A["od_gla_norm"][0].partition_broadcast(P)),
            (k.q_norm[:, :], A["od_q_norm"][0].rearrange("(j p) -> p j", p=P)),
            (k.kv_norm[:, :], A["od_kv_norm"].rearrange("a p -> p a")),
            (k.gla_b[:, 0, :], A["od_gla_b_f"][0].rearrange("(j p) -> p j", p=P)),
            (k.gla_b[:, 1, :], A["od_gla_b_b"][0].rearrange("(j p) -> p j", p=P)),
        ]
        for i, name in enumerate(("ev_lq1", "ev_lk1", "ev_lq2", "ev_lk2")):
            small.append((k.lqk[:, i, :], A[name][0].partition_broadcast(P)))
        for i in range(DEPTH):
            small += [
                (k.hgrn_g[:, i, :], A["hgrn_norm_g_2"][i].partition_broadcast(P)),
                (k.pool_scale[:, i, :], A["pool_scale_2"][i].rearrange("(g p) -> p g", p=P)),
                (k.lb_param[:, i, :], A["lb_param_2"][i].rearrange("(g p) -> p g", p=P)),
                (router_raw[i][0], rows(A["moe_w_grp"][i])),
                (router_raw[i][1], rows(A["moe_w_exp"][i])),
                (k.b_grp[:, i, :], A["moe_b_grp"][i].partition_broadcast(P)),
                (k.b_exp[:, i, :], A["moe_b_exp"][i].partition_broadcast(P)),
            ]
        for dst, src in small:
            q.act.dma(dst, src, par_sem, 16 * len(small))
        params = k.params = Step(par_sem, 16 * len(small))
        load_norm(k, q, 0)

        for queue in (q.pe, q.dve, q.act, q.pool):
            queue.wait(tab_here)
        q.dve.do(lambda e: e.tensor_copy(k.masks[:, :, :], wide_masks))
        k.x_ready = [x_here, x_here]
        to_feature_major(k, q, k.x_ready)

        def tap(name):
            if taps is not None and name in taps:
                s = q.act.dma(taps[name].rearrange("(b p) d -> p b d", p=P), k.x_tok[:, :, :], out_sem, 16 * (tap.n + 1), after=k.x_ready)
                tap.n += 1
                q.act.wait(s)
        tap.n = 0

        k.split.prefetch(k, q)
        layer_norm(k, q, retention_diff_mixer(k, q))
        tap("ln0")
        layer_norm(k, q, moe(k, q, 0, nc, new_sem, A))
        tap("ln1")
        for dst, src in ((k.w_uq, A["od_w_uq"][0].rearrange("(j p) n -> p j n", p=P)), (k.w_ukv, A["od_w_ukv"][0]),
                         (k.gla_w2[0:GATE_RANK, :], A["od_gla_w2_f"][0]), (k.gla_w2[32:32 + GATE_RANK, :], A["od_gla_w2_b"][0])):
            q.act.dma(dst, src, wide_sem, 16 * 5)
        k.params = Step(wide_sem, 16 * 5)
        layer_norm(k, q, mla_gla_mixer(k, q))
        k.params = params
        tap("ln2")
        mixed = moe(k, q, 1, nc, new_sem, A)
        weights = FfnWeights(k, q)
        layer_norm(k, q, mixed)
        tap("ln3")
        k.pool_here = q.act.dma(k.pool_or_distance[:, :], A["pool_mat"], wide_sem, 16 * 8, after=[Step(q.dve.sem, q.dve.count)])
        for i in range(DEPTH):
            q.act.dma(k.pool_w[:, i, :, :], A["pool_w_2"][i].rearrange("g c d -> c g d"), wide_sem, 16 * 8)
        for layer in range(DEPTH):
            layer_norm(k, q, ffn(k, q, weights))
            tap(f"ln{4 + 3 * layer}")
            mixed = pool_hgrn_mixer(k, q, layer)
            weights = FfnWeights(k, q)
            layer_norm(k, q, mixed)
            tap(f"ln{5 + 3 * layer}")
            mixed = ffn(k, q, weights)
            if layer + 1 < DEPTH:
                weights = FfnWeights(k, q)
            layer_norm(k, q, mixed)
            tap(f"ln{6 + 3 * layer}")
        stored = q.act.dma(out.rearrange("a (b p) d -> p (a b) d", p=P), k.x_tok[:, :, :], out_sem, 16 * (tap.n + 1), after=k.x_ready)
        q.act.wait(stored)
        q.play(nc, [k.ring])
        assert k.ring.asked == k.ring.loaded == len(k.ring.plan)


_INS = ['x', 'ev_w_in', 'ev_ret_decay_f', 'ev_ret_decay_b', 'ev_lq1', 'ev_lk1', 'ev_lq2', 'ev_lk2', 'ev_subln', 'ev_w_out',
        'od_w_in', 'od_q_norm', 'od_w_uq', 'od_kv_norm', 'od_w_ukv', 'od_gla_w2_f', 'od_gla_b_f', 'od_gla_w2_b', 'od_gla_b_b',
        'od_gla_norm', 'od_w_out', 'ln1_g', 'ln1_b', 'ln2_g', 'ln2_b', 'moe_w_grp', 'moe_b_grp', 'moe_w_exp', 'moe_b_exp',
        'moe_w_gate', 'moe_w_up', 'moe_w_down', 'w_in_2', 'pool_w_2', 'pool_scale_2', 'lb_param_2', 'hgrn_norm_g_2', 'w_out_2',
        'ffn1_gate_2', 'ffn1_up_2', 'ffn1_down_2', 'ffn2_gate_2', 'ffn2_up_2', 'ffn2_down_2', 'ln_g_2', 'ln_b_2']


def kernel(**inputs):
    import concourse.bacc as bacc
    from concourse.bass_utils import run_bass_kernel_spmd

    arrays = {name: np.ascontiguousarray(inputs[name]) for name in _INS}
    arrays["tables"] = constant_tables()[0]
    arrays["masks"] = level_masks()
    arrays["distance"] = distance_tables().reshape(P, -1)
    arrays["pool_mat"] = pool_tables().reshape(P, -1)
    nc = bacc.Bacc("TRN2", target_bir_lowering=False, num_devices=1)
    feed, A = {}, {}
    for name, a in arrays.items():
        feed[f"in_{name}"] = a
        A[name] = nc.dram_tensor(f"in_{name}", a.shape, mybir.dt.from_np(a.dtype), kind="ExternalInput").ap()
    out = nc.dram_tensor("out_0", (1, T, D), F32, kind="ExternalOutput").ap()
    build(nc, A, out)
    r = run_bass_kernel_spmd(nc, [feed], core_ids=[0])
    return r.results[0]["out_0"]
```

```python
from contextlib import ExitStack

import concourse.bass as bass
import numpy as np
from concourse import mybir

F32 = mybir.dt.float32
F32R = mybir.dt.float32r
I32 = mybir.dt.int32
U8 = mybir.dt.uint8
ALU = mybir.AluOpType
ACT = mybir.ActivationFunctionType
AXX = mybir.AxisListType.X

P = 128
T = 256
NB = T // P
D = 1024
KT = D // P
BANK = 512
HEADS = 4
HD = 128
DIFF_D = 64
MLA_NOPE, MLA_ROPE, MLA_QR, MLA_KVR = 64, 32, 256, 128
MLA_QD = MLA_NOPE + MLA_ROPE
GATE_RANK = 16
GLA_TAU = 16.0
CHUNK = 64
N_GROUPS, PER_GROUP, N_EXPERTS = 4, 8, 32
D_EXPERT = 512
FT_E = D_EXPERT // P
D_FF = 2816
FT = D_FF // P
DEPTH = 2
ALPHA = (2.0 * DEPTH) ** 0.25
LN_EPS = 1e-5
RMS_EPS = 1e-6
LAM_INIT = 0.2
SLOT = 2048
RING = 7
PARTS = 4
PART = 1024
EXTRA_ORDER = (1, 2, 3, 0)
HIDDEN = 6
CAP = 64
PAIR = 2
BIG = 1e30
WINDOWS = (2, 4, 8, 16)


def rotary_tables(rows, half, theta, width):
    pos = np.arange(T, dtype=np.float32)
    inv = np.power(np.float32(theta), -np.arange(0, 2 * half, 2, dtype=np.float32) / np.float32(2 * half)).astype(np.float32)
    ang = (pos[:, None] * inv[None, :]).astype(np.float32)
    cos = np.ones((rows, T), np.float32)
    sin = np.zeros((rows, T), np.float32)
    swap = np.zeros((rows, rows), np.float32)
    for r in range(rows):
        i = r % width
        if i < 2 * half:
            cos[r] = np.cos(ang[:, i % half])
            sin[r] = np.sin(ang[:, i % half]) * (-1.0 if i < half else 1.0)
            swap[r + half if i < half else r - half, r] = 1.0
    return cos, sin, swap


def constant_tables():
    parts = {}
    parts["ident"] = np.eye(P, dtype=np.float32)
    parts["neg_half"] = np.full((P, 16), -0.5, np.float32)
    for name, half, theta, width in (("dif", 8, 500000.0, 64), ("ret", 64, 10000.0, 128)):
        c, s, w = rotary_tables(P, half, theta, width)
        parts[name + "_cos"], parts[name + "_sin"], parts[name + "_swap"] = c, s, w
    parts["ones"] = np.ones((P, P), np.float32)
    parts["earlier"] = np.triu(np.ones((P, P), np.float32), 1)
    parts["slot_no"] = np.tile(np.arange(CAP, dtype=np.float32), (P, 1))
    parts["desc_grp"] = np.tile(np.arange(N_GROUPS, 0, -1, dtype=np.float32), (P, 1))
    parts["desc_exp"] = np.tile(np.arange(N_EXPERTS, 0, -1, dtype=np.float32), (P, 1))
    c, s, w = rotary_tables(MLA_ROPE, MLA_ROPE // 2, 500000.0, MLA_ROPE)
    at = slice(MLA_NOPE, MLA_QD)
    for key, v in (("mla_cos", c), ("mla_sin", s), ("mla_swap", w)):
        full = np.zeros((P, v.shape[1]), np.float32)
        full[at] = v
        parts[key] = full
    scan = np.ones((P, 2 * T), np.float32)
    scan[:, ::CHUNK] = 0.0
    parts["scan"] = scan
    cols, at = {}, 0
    for key, v in parts.items():
        cols[key] = (at, v.shape[1])
        at += v.shape[1]
    return np.concatenate(list(parts.values()), axis=1), cols


def distance_tables():
    s = np.arange(P)[:, None, None] + P * np.arange(NB)[None, :, None]
    t = np.arange(T)[None, None, :]
    return np.stack([np.maximum(t - s, 0), np.maximum(s - t, 0)], axis=1).astype(np.float32)


def pool_tables():
    out = np.zeros((T, len(WINDOWS), T), np.float32)
    for g, w in enumerate(WINDOWS):
        for t in range(T):
            n = min(t + 1, w)
            out[t - n + 1:t + 1, g, t] = np.float32(1.0) / np.float32(n)
            out[t, g, t] -= 1.0
    return np.ascontiguousarray(out.reshape(NB, P, len(WINDOWS), T).transpose(1, 0, 2, 3))


LEVELS = tuple(range(7, 0, -1))


def level_masks():
    s, t = np.arange(P)[:, None], np.arange(P)[None, :]
    out = []
    for flip in (False, True):
        a, b = (t, s) if flip else (s, t)
        for m in LEVELS:
            n = 1 << m
            out.append((a // n == b // n) & (a % n < n // 2) & (b % n >= n // 2))
    out.append(s == t)
    return np.stack(out, axis=1).astype(np.float32)


class Step:

    def __init__(self, sem, count):
        self.sem, self.count = sem, count


class Queue:

    def __init__(self, sem):
        self.sem, self.count, self.met, self.items = sem, 0, {}, []

    def wait(self, step):
        if self.met.get(id(step.sem), 0) < step.count:
            self.met[id(step.sem)] = step.count
            self.items.append(("wait", step.sem, step.count))

    def do(self, emit, after=(), chain=True):
        for step in after:
            self.wait(step)
        if chain and self.count:
            self.wait(Step(self.sem, self.count))
        self.count += 1
        self.items.append(("run", emit, self.sem, 1))
        return Step(self.sem, self.count)

    def dma(self, out, in_, sem, count, after=()):
        for step in after:
            self.wait(step)
        self.items.append(("run", lambda e: e.dma_start(out, in_), sem, 16))
        return Step(sem, count)

    def play(self, engine):
        for kind, what, *rest in self.items:
            if kind == "wait":
                engine.wait_ge(what, rest[0])
            else:
                what(engine).then_inc(rest[0], rest[1])
        self.items = []


class Tiles:
    pass


class Bank:

    def __init__(self, tile):
        self.tile, self.free = tile, []


class Banks:

    def __init__(self, banks):
        self.banks, self.n = banks, 0

    def take(self):
        self.n += 1
        return self.banks[(self.n - 1) % len(self.banks)]


class Ring:

    def __init__(self, slots, sems, plan, queue, extra=0):
        self.slots, self.sems, self.plan, self.queue = slots, sems, plan, queue
        self.asked, self.loaded, self.released = 0, 0, [None] * len(plan)
        self.lent, self.first_extra = [], len(slots) - extra
        self.slot, self.before, self.run, self.count = [], [], [], []
        last = [(-1, k) for k in range(len(slots))]
        loads, run = [0] * len(slots), -1
        for n, (key, sources, expert) in enumerate(plan):
            if expert and (n == 0 or not plan[n - 1][2]):
                run += 1
                for k in range(self.first_extra, len(slots)):
                    last[k] = (n - 1, k)
            k = min(range(len(slots) if expert else self.first_extra), key=lambda k: last[k])
            replaced = last[k][0] if k < self.first_extra or (last[k][0] >= 0 and self.slot[last[k][0]] == k) else -1
            loads[k] += len(sources)
            self.slot.append(k)
            self.before.append(replaced)
            self.run.append(run)
            self.count.append(16 * loads[k])
            last[k] = (n, k)

    def view(self, n):
        a, b = self.plan[n][1][0].shape[1], sum(src.shape[2] for src in self.plan[n][1])
        return self.slots[self.slot[n]][:, 0:a * b].rearrange("p (a b) -> p a b", a=a)

    def next(self, key):
        n = self.asked
        self.asked += 1
        assert self.plan[n][0] == key, (self.plan[n][0], key)
        return n, self.view(n), Step(self.sems[self.slot[n]], self.count[n])

    def release(self, n, step):
        self.released[n] = step

    def lend(self, steps):
        self.lent.append(steps)

    def last_reads(self):
        return [next(self.released[n] for n in range(self.asked - 1, -1, -1) if self.slot[n] == k)
                for k in range(self.first_extra, len(self.slots))]

    def load(self):
        while self.loaded < len(self.plan):
            n = self.loaded
            k, before = self.slot[n], self.before[n]
            if before >= 0:
                if self.released[before] is None:
                    break
                after = [self.released[before]]
            elif k >= self.first_extra:
                if len(self.lent) <= self.run[n]:
                    break
                after = self.lent[self.run[n]][k - self.first_extra]
            else:
                after = []
            at, view = 0, self.view(n)
            for src in self.plan[n][1]:
                self.queue.dma(view[:, :, at:at + src.shape[2]], src, self.sems[k], self.count[n], after=after)
                at += src.shape[2]
            self.loaded += 1


class Engines:

    def __init__(self, new_sem, name):
        self.sems = []

        def sem(what):
            self.sems.append(new_sem(f"{name}_{what}"))
            return self.sems[-1]

        self.sem = sem
        self.pe, self.act, self.dve, self.pool, self.sp = (Queue(sem(w)) for w in ("pe_done", "act_done", "dve_done", "pool_done", "sp_done"))

    def play(self, nc, rings):
        for ring in rings:
            ring.load()
        with nc.Block(no_gpsimd_drain=True) as block:
            block.sync(self.sp.play)
            block.tensor(self.pe.play)
            block.scalar(self.act.play)
            block.vector(self.dve.play)
            block.gpsimd(self.pool.play)


class Arena:

    def __init__(self, tile, words):
        self.tile, self.words, self.at = tile, words, 0

    def restart(self):
        self.at = 0

    def take(self, *shape):
        n = int(np.prod(shape))
        assert self.at + n <= self.words, (self.at, n, self.words)
        v = self.tile[:, self.at:self.at + n]
        self.at += n
        if len(shape) == 2:
            v = v.rearrange("p (a b) -> p a b", a=shape[0])
        elif len(shape) == 3:
            v = v.rearrange("p (a b c) -> p a b c", a=shape[0], b=shape[1])
        return v


def interleave(*streams):
    streams = list(streams)
    while streams:
        for s in list(streams):
            try:
                next(s)
            except StopIteration:
                streams.remove(s)


def product(q, bank, groups, after=(), first=True, last=True):

    def emit(e):
        for out, parts in groups:
            for i, (lhs, rhs) in enumerate(parts):
                ins = e.matmul(out, lhs, rhs, start=first and i == 0, stop=last and i == len(parts) - 1)
        return ins

    return q.pe.do(emit, after=list(bank.free) + list(after), chain=False)


def transposes(q, bank, ident, pairs, after=()):
    def emit(e):
        for out, in_ in pairs:
            ins = e.transpose(out, in_, ident)
        return ins

    return q.pe.do(emit, after=list(bank.free) + list(after), chain=False)


def bcast(ap, n):
    return ap.unsqueeze(ap.ndim).to_broadcast(list(ap.shape) + [n])


def mid_bcast(ap, n):
    return ap.unsqueeze(1).to_broadcast([ap.shape[0], n] + list(ap.shape[1:]))


def rows(w, k=KT):
    return w.rearrange("(p k) n -> p k n", k=k)


def tiled_rows(w):
    return w.rearrange("(k p) n -> p k n", p=P)


def moe_plan(A, layer):
    out = []
    for g in range(N_EXPERTS // PAIR):
        for name, per in (("gate", KT // 2), ("up", KT // 2), ("down", FT_E // 2)):
            w = A["moe_w_" + name]
            for half in range(2):
                for j in range(PAIR):
                    k = KT if name != "down" else FT_E
                    src = rows(w[layer, PAIR * g + j], k)[:, half * per:(half + 1) * per, :]
                    out.append(((name, g, half, j), [src], True))
    return out


def weight_plan(A):
    plan = [(("ev_in", c), rows(A["ev_w_in"][0])[:, :, 256 * c:256 * c + 256]) for c in (8, 9, 10, 11, 12, 13, 0, 1, 2, 3, 4, 5, 6, 7)]
    plan += [(("ev_out", c), tiled_rows(A["ev_w_out"][0])[:, :, 256 * c:256 * c + 256]) for c in range(4)]
    plan += moe_plan(A, 0)
    for c, parts in enumerate(OD_COLUMNS):
        plan.append((("od_in", c), [rows(A["od_w_in"][0])[:, :, a:b] for a, b in parts]))
    plan += [(("od_out", c), tiled_rows(A["od_w_out"][0])[:, :, 256 * c:256 * c + 256]) for c in range(4)]
    plan += moe_plan(A, 1)
    for layer in range(DEPTH):
        plan += ffn_plan(A, layer, 1)
        plan += [(("in2", c), rows(A["w_in_2"][layer])[:, :, 256 * c:256 * c + 256]) for c in (4, 5, 0, 1, 2, 3, 6, 7, 8, 9)]
        plan += [(("out2", c), tiled_rows(A["w_out_2"][layer])[:, :, 256 * c:256 * c + 256]) for c in range(4)]
        plan += ffn_plan(A, layer, 2)
    return [entry if len(entry) == 3 else (entry[0], entry[1] if isinstance(entry[1], list) else [entry[1]], False) for entry in plan]


def ffn_plan(A, layer, which):
    out = []
    lag = FFN_LAG // 2
    for c in range(FT // 2 + lag):
        if c < FT // 2:
            for name in ("gate", "up"):
                src = rows(A[f"ffn{which}_{name}_2"][layer])[:, :, 256 * c:256 * c + 256]
                out.append(((name, c), src))
        if c >= lag:
            d = c - lag
            out.append((("down", d), tiled_rows(A[f"ffn{which}_down_2"][layer])[:, 2 * d:2 * d + 2, :]))
    return out


FFN_LAG = 2
OD_COLUMNS = (((0, 256),), ((256, 416), (1888, 1984))) + tuple(((a, a + 256),) for a in range(416, 1952, 256))


def to_feature_major(k, q, after_block):
    done = [[] for _ in range(NB)]
    for tb in range(NB):
        for half in range(2):
            bank = k.banks_b.take()
            view = bank.tile[:, :].rearrange("p (k t) -> p k t", k=4)
            pairs = [(view[:, i, :], k.x_tok[:, tb, (4 * half + i)::KT]) for i in range(4)]
            step = transposes(q, bank, k.ident, pairs, after=[after_block[tb]])
            at = (slice(0, P), slice(4 * half, 4 * half + 4), slice(tb * P, (tb + 1) * P))
            high = q.act.do(lambda e, view=view, at=at: e.activation(k.xh[at], view, ACT.Copy), after=[step], chain=False)
            low = q.dve.do(lambda e, view=view, at=at: e.tensor_tensor(k.xl[at], view, k.xh[at].bitcast(F32), ALU.subtract), after=[high], chain=False)
            bank.free = [low]
            done[tb].append(low)
    k.xT_blocks, k.xT_ready = done, done[0] + done[1]


def load_norm(k, q, n):
    sem, free = k.norm_sem, k.norm_free
    for i, row in enumerate(k.norm_rows[n]):
        q.pool.dma(k.norm_gb[:, i, :], row.partition_broadcast(P), sem, 32 * (n + 1), after=free)


def half_stats(k, q, tb, h, after):
    q.dve.do(lambda e: e.bn_stats(k.bn[:, tb, 6 * h:6 * h + 6], k.acc[:, tb, BANK * h:BANK * h + BANK]), after=after, chain=False)


def layer_norm(k, q, finish, halves=(0, 1), before=None, between=None, after=None):
    n = k.norm_no
    k.norm_no += 1
    gb = k.norm_gb
    gb_here = Step(k.norm_sem, 32 * (n + 1))
    if before:
        before()
    block_done = []
    for tb in range(NB):
        whole = finish[tb]()
        for h in halves:
            half_stats(k, q, tb, h, whole[h] if len(halves) == 2 else whole)
        q.dve.do(lambda e, tb=tb: e.bn_aggr(k.mv[:, tb, :], k.bn[:, tb, :]))
        var = q.dve.do(lambda e, tb=tb: e.tensor_scalar(k.ve[:, tb:tb + 1], k.mv[:, tb, 1:2], LN_EPS, None, ALU.add))
        rstd = q.pool.do(lambda e, tb=tb: e.tensor_tensor(k.rstd[:, tb:tb + 1], k.ve[:, tb:tb + 1], k.neg_half[:, 0:1], ALU.pow), after=[var])
        q.dve.do(lambda e, tb=tb: e.scalar_tensor_tensor(out=k.x_tok[:, tb, :], in0=k.acc[:, tb, :], scalar=k.mv[:, tb, 0:1], in1=gb[:, 0, :],
                                                  op0=ALU.subtract, op1=ALU.mult), after=[gb_here])
        block_done.append(q.dve.do(lambda e, tb=tb: e.scalar_tensor_tensor(out=k.x_tok[:, tb, :], in0=k.x_tok[:, tb, :], scalar=k.rstd[:, tb:tb + 1],
                                                                    in1=gb[:, 1, :], op0=ALU.mult, op1=ALU.add), after=[rstd]))
    k.norm_free = [block_done[-1]]
    if n + 1 < len(k.norm_rows):
        load_norm(k, q, n + 1)
    k.x_ready = block_done
    if n + 1 == len(k.norm_rows):
        return
    if between:
        between()
    to_feature_major(k, q, block_done)
    if after:
        after()


class Splitter:

    def __init__(self, high, low):
        self.high, self.low, self.n, self.free, self.pending = high, low, 0, [[] for _ in high], {}

    def split(self, q, src, here, i=None):
        if i is None:
            i = self.n % len(self.high)
            self.n += 1
        a, b = src.shape[1:]
        hi, lo = (t[i][:, 0:a * b].rearrange("p (a b) -> p a b", a=a) for t in (self.high, self.low))
        high = q.act.do(lambda e: e.activation(hi, src, ACT.Copy), after=[here] + self.free[i], chain=False)
        low = q.dve.do(lambda e: e.tensor_tensor(lo, src, hi.bitcast(F32), ALU.subtract), after=[high], chain=False)
        return i, hi, lo, low

    def chunk(self, k, q, key):
        if key not in self.pending:
            self.prefetch(k, q)
        parts = self.pending.pop(key)
        self.prefetch(k, q)
        return parts

    def prefetch(self, k, q):
        if k.ring.asked == len(k.ring.plan) or k.ring.plan[k.ring.asked][0][0] not in SPLIT_CHUNKS or len(self.pending) > 0:
            return
        key = k.ring.plan[k.ring.asked][0]
        n, w, here = k.ring.next(key)
        if moving(key):
            parts = [(r, self.split(q, w[:, r:r + KT // 2, :], here)) for r in (0, KT // 2)]
        else:
            parts = [(c, self.split(q, w[:, :, c:c + P], here)) for c in range(0, w.shape[2], P)]
        k.ring.release(n, parts[-1][1][3])
        self.pending[key] = parts


STATIONARY_CHUNKS = {"ev_in": (8, 9, 10, 11, 0, 1, 2, 3), "od_in": (2, 3), "in2": (4, 5, 2, 3)}


def moving(key):
    return key[1] not in STATIONARY_CHUNKS.get(key[0], ())


SPLIT_CHUNKS = ("ev_in", "ev_out", "od_in", "od_out", "in2", "out2")


def three_passes(out, products):
    parts = []
    for (lh, ll), (rh, rl) in products:
        parts += [(lh, rh), (lh, rl), (ll, rh)]
    return out, parts


def block_times_rows(k, out, tb, parts):
    ts = slice(tb * P, (tb + 1) * P)
    return three_passes(out, [((k.xh[:, r + j, ts], k.xl[:, r + j, ts]), (hi[:, j, :], lo[:, j, :]))
                              for r, (i, hi, lo, here) in parts for j in range(KT // 2)])


def tokens_times_chunk(k, q, key, bank, after):
    return blocks_times_parts(k, q, k.split.chunk(k, q, key), [bank] * NB, after)


def blocks_times_parts(k, q, parts, banks, after, first=True):
    cols = parts[0][1][1].shape[2]
    steps = []
    for tb in range(NB):
        at = tb * cols if banks[0] is banks[1] else 0
        steps.append(product(q, banks[tb], [block_times_rows(k, banks[tb].tile[:, at:at + cols], tb, parts)],
                             after=[part[3] for _, part in parts] + after[tb], first=first))
    for _, part in parts:
        k.split.free[part[0]] = [steps[-1]]
    return steps


def project(k, q, key, kind, banks=None):
    bank = (banks or k.banks).take()
    assert moving(key) == (kind == "tok")
    if kind == "tok":
        return bank, tokens_times_chunk(k, q, key, bank, k.xT_blocks)[-1]
    for c, (i, hi, lo, here) in k.split.chunk(k, q, key):
        step = product(q, bank, [three_passes(bank.tile[:, c // P * T:(c // P + 1) * T],
                                              [((hi[:, j, :], lo[:, j, :]), (k.xh[:, j, :], k.xl[:, j, :])) for j in range(KT)])],
                       after=[here] + k.xT_ready)
        k.split.free[i] = [step]
    return bank, step


def evacuate(k, q, bank, step, dst, src=None, scale=None, func=None, engine="act"):
    src = bank.tile[:, :] if src is None else src
    if func is None:
        func = ACT.Copy
    if engine == "act":
        got = q.act.do(lambda e, src=src, func=func: e.activation(dst, src, func, scale=1.0 if scale is None else scale), after=[step], chain=False)
    elif scale is None:
        got = q.dve.do(lambda e, src=src: e.tensor_copy(dst, src), after=[step], chain=False)
    else:
        got = q.dve.do(lambda e, src=src: e.tensor_scalar(dst, src, scale, None, ALU.mult), after=[step], chain=False)
    bank.free = [got]
    return got


def token_major(k, q, key, dst, func=None):
    bank, step = project(k, q, key, "tok")
    return evacuate(k, q, bank, step, dst, bank.tile[:, :].rearrange("p (a b) -> p a b", a=NB), func=func)


def rotate(k, q, raw, out, cos, sin, swap, after, at=slice(0, P)):
    bank = k.banks.take()
    view = bank.tile[at, :].rearrange("p (a b) -> p a b", a=2)
    swapped = product(q, bank, [(view[:, i, :], [(swap, raw[:, i, :])]) for i in range(2)], after=after)
    q.dve.do(lambda e: e.tensor_tensor(out, raw, mid_bcast(cos, 2), ALU.mult), after=after)
    tmp = k.rot_tmp[at, :].rearrange("p (a b) -> p a b", a=2)
    got = q.dve.do(lambda e: e.tensor_tensor(tmp, view, mid_bcast(sin, 2), ALU.mult), after=[swapped])
    bank.free = [got]
    return q.dve.do(lambda e: e.tensor_tensor(out, out, tmp, ALU.add))


def load_router(k, q, layer, after):
    wide = k.mixT[:, 0:KT // 2, :].rearrange("p k t -> p (k t)").rearrange("p (k n) -> p k n", k=KT)
    for step in after:
        q.pool.wait(step)
    clear = q.pool.do(lambda e: e.memset(wide[:, :, N_GROUPS + N_EXPERTS:], 0.0))
    for dst, src in ((wide[:, :, 0:N_GROUPS], k.router[layer][0]), (wide[:, :, N_GROUPS:N_GROUPS + N_EXPERTS], k.router[layer][1])):
        here = q.pool.dma(dst, rows(src), k.router_sem, 32 * (layer + 1))

    def split():
        q.act.wait(clear)
        q.dve.wait(clear)
        assert k.split.n % PARTS == 0
        k.router_parts = k.split.split(q, wide, here, i=0)

    return split


def begin_out_projection(k, q, name, r, ready):
    if (name, 0) not in k.split.pending:
        k.split.prefetch(k, q)
    parts = [part for part in k.split.pending[name, 0] if part[0] == r]
    banks = [k.banks_b.take() for _ in range(NB)]
    for tb in range(NB):
        product(q, banks[tb], [block_times_rows(k, banks[tb].tile[:, 0:256], tb, parts)], after=[parts[0][1][3]] + ready, last=False)
    return banks


def out_projection(k, q, name, begun, mix_ready, meanwhile=None):

    def evacuated(src, blocks, cols, after):
        return q.dve.do(lambda e: e.scalar_tensor_tensor(out=k.acc[:, blocks, cols], in0=k.x_tok[:, blocks, cols], scalar=ALPHA,
                                                         in1=src, op0=ALU.mult, op1=ALU.add),
                        after=after + k.x_ready, chain=False)

    done = []
    for c in range(4):
        cols = slice(256 * c, 256 * c + 256)
        parts = k.split.chunk(k, q, (name, c))
        if c == 0:
            r, banks = begun
            steps = blocks_times_parts(k, q, [part for part in parts if part[0] == r], banks, mix_ready, first=False)
            for part in parts:
                k.split.free[part[1][0]] = [steps[-1]]
            for tb in range(NB):
                got = evacuated(banks[tb].tile[:, 0:256].unsqueeze(1), slice(tb, tb + 1), cols, [steps[tb]])
                banks[tb].free = [got]
            done.append(got)
        elif c < 3:
            bank = k.banks.take()
            steps = blocks_times_parts(k, q, parts, [bank] * NB, mix_ready)
            done.append(evacuated(bank.tile[:, :].rearrange("p (a b) -> p a b", a=NB), slice(0, NB), cols, steps))
            bank.free = [done[-1]]
        else:
            last_banks = [k.banks_b.take() for _ in range(NB)]
            steps = blocks_times_parts(k, q, parts, last_banks, mix_ready)
        if c == 1:
            for tb in range(NB):
                half_stats(k, q, tb, 0, done)
        if c == 2 and meanwhile:
            meanwhile()

    def finish(tb):
        got = evacuated(last_banks[tb].tile[:, 0:256].unsqueeze(1), slice(tb, tb + 1), cols, [steps[tb]])
        last_banks[tb].free = [got]
        return [got, done[2]]

    return [lambda: finish(0), lambda: finish(1)]


def mix_transposes(k, q, src, tb, base, after, banks):
    bank = banks.take()
    view = bank.tile[:, :].rearrange("p (i t) -> p i t", i=4)
    step = transposes(q, bank, k.ident, [(view[:, i, :], src[:, tb, i * P:(i + 1) * P]) for i in range(4)], after=after)

    def write():
        got = mix_parts(k, q, view, (slice(0, P), slice(base, base + 4), slice(tb * P, (tb + 1) * P)), step)
        bank.free = [got]
        return got

    return write


def mix_parts(k, q, src, at, ready):
    high = q.act.do(lambda e: e.activation(k.xh[at], src, ACT.Copy), after=[ready], chain=False)
    return q.dve.do(lambda e: e.tensor_tensor(k.xl[at], src, k.xh[at].bitcast(F32), ALU.subtract), after=[high], chain=False)


def normed_heads(k, q, name, stats, scale, base, rest):
    banks = begin_out_projection(k, q, name, KT // 2 - base, rest)
    stats(0)
    y, ready = scale(0)
    write = mix_transposes(k, q, y, 0, base, [ready], k.banks_b)
    stats(1)
    first = write()
    y, ready = scale(1)
    second = mix_transposes(k, q, y, 1, base, [ready], k.banks_b)()
    return (base, banks), [rest + [first], rest + [second]]


def sums_of_squares(k, q, bank, step, groups, width, out):
    for g in range(groups):
        got = q.act.do(lambda e, g=g: e.activation(k.junk[:, 0:width], bank[:, g * width:(g + 1) * width], ACT.Square, accum_out=out[:, g:g + 1]),
                       after=[step])
    return got


def rms_scale(k, q, sums, n, width, eps, after):
    a = q.dve.do(lambda e: e.tensor_scalar(sums[:, 0:n], sums[:, 0:n], 1.0 / width, eps, ALU.mult, ALU.add), after=[after])
    return q.pool.do(lambda e: e.tensor_tensor(sums[:, 0:n], sums[:, 0:n], k.neg_half[:, 0:n], ALU.pow), after=[a])


def softmax_rows(k, q, bank, step, e_out, scale, tag, free):
    view = bank.tile[:, :].rearrange("p (a b) -> p a b", a=NB)
    q.dve.do(lambda e: e.tensor_reduce(tag[:, 0:2], view, AXX, ALU.max), after=[step])
    neg = q.dve.do(lambda e: e.tensor_scalar(tag[:, 2:4], tag[:, 0:2], -scale, None, ALU.mult))
    for b in range(NB):
        got = q.act.do(lambda e, b=b: e.activation(e_out[:, b, :], view[:, b, :], ACT.Exp, bias=tag[:, 2 + b:3 + b], scale=scale,
                                                   accum_out=tag[:, 4 + b:5 + b]), after=[neg] + free)
    bank.free = [got]
    return got


def rotated(k, q, c0, dst, which, raw, got):
    for pair in range(2):
        bank, step = project(k, q, ("ev_in", c0 + pair), "feat")
        for x in got.raw_free:
            q.act.wait(x)
        for queue in (q.pe, q.dve):
            queue.wait(k.rotary_here[which])
        here = evacuate(k, q, bank, step, raw, bank.tile[:, :].rearrange("p (a b) -> p a b", a=2))
        yield
        done = rotate(k, q, raw, dst[:, 2 * pair:2 * pair + 2, :], k.tab(which + "_cos"), k.tab(which + "_sin"),
                      k.tab(which + "_swap"), [here])
        got.raw_free = [done]
        got.last = done
        yield


def diff_heads(k, q, heads, b, dq, dk, dv, ready, lam_ready, o_banks, o_steps):
    scale = DIFF_D ** -0.5
    for h in heads:
        ex = []
        for m, e_out in enumerate((b.e1, b.e2)):
            r = slice(m * DIFF_D, (m + 1) * DIFF_D)
            bank = k.banks_b.take()
            view = bank.tile[:, :].rearrange("p (a b) -> p a b", a=NB)
            step = product(q, bank, [(view[:, i, :], [(dq[r, h, i * P:(i + 1) * P], dk[r, h, :])]) for i in range(NB)], after=ready)
            ex.append(softmax_rows(k, q, bank, step, e_out, scale, b.tags[:, m, :], b.free))
        yield
        tags = b.tags
        q.dve.do(lambda e, tags=tags: e.reciprocal(tags[:, :, 6:8], tags[:, :, 4:6]), after=ex)
        q.dve.do(lambda e, tags=tags: e.tensor_scalar(tags[:, 1, 6:8], tags[:, 1, 6:8], k.lam[:, 2:3], None, ALU.mult), after=[lam_ready])
        for i in range(NB):
            q.dve.do(lambda e, i=i, tags=tags: e.tensor_scalar(b.e2[:, i, :], b.e2[:, i, :], tags[:, 1, 6 + i:7 + i], None, ALU.mult))
            p = q.dve.do(lambda e, i=i, tags=tags: e.scalar_tensor_tensor(out=b.e1[:, i, :], in0=b.e1[:, i, :], scalar=tags[:, 0, 6 + i:7 + i],
                                                               in1=b.e2[:, i, :], op0=ALU.mult, op1=ALU.add))
        yield
        turned, o_steps[h] = probabilities_times_v(k, q, b.e1, b.pt, p, b.pt_free, dv, h, ready[-1], o_banks)
        b.pt_free = [o_steps[h][1]]
        b.free = [turned, p]
        yield


def retention_heads(k, q, heads, b, rq, rk, rv, ready, rates, o_banks, o_steps):
    for h in heads:
        decay, scores = b.e2, b.e1
        q.dve.do(lambda e, h=h, decay=decay: e.tensor_scalar(decay, k.distance[:, 0, :, :], k.neg_rate[:, h:h + 1], None, ALU.mult),
                 after=[rates, k.distance_here] + b.free)
        arg = q.dve.do(lambda e, h=h, decay=decay: e.scalar_tensor_tensor(out=decay, in0=k.distance[:, 1, :, :], scalar=k.neg_rate[:, HEADS + h:HEADS + h + 1],
                                                             in1=decay, op0=ALU.mult, op1=ALU.add))
        dec = q.act.do(lambda e, decay=decay: e.activation(decay, decay, ACT.Exp), after=[arg])
        yield
        bank = k.banks_b.take()
        view = bank.tile[:, :].rearrange("p (a b) -> p a b", a=NB)
        step = product(q, bank, [(view[:, sb, :], [(rk[:, h, sb * P:(sb + 1) * P], rq[:, h, :])]) for sb in range(NB)], after=ready)
        got = q.dve.do(lambda e, scores=scores, view=view, decay=decay: e.scalar_tensor_tensor(out=scores, in0=view, scalar=HD ** -0.5, in1=decay, op0=ALU.mult, op1=ALU.mult),
                       after=[step, dec])
        bank.free = [got]
        yield
        o_steps[h] = [product(q, o_banks[tb], [(o_banks[tb].tile[:, h * HD:(h + 1) * HD],
                                                [(scores[:, sb, tb * P:(tb + 1) * P], rv[:, sb, h * HD:(h + 1) * HD]) for sb in range(NB)])],
                              after=[got]) for tb in range(NB)]
        b.free = [o_steps[h][1]]
        yield


def retention_diff_mixer(k, q):
    A = k.arena
    A.restart()
    y = k.acc
    raw = A.take(2, T)
    dq, dk, rq, rk = (A.take(HEADS, T) for _ in range(4))
    dv, rv, gate = (A.take(NB, 512) for _ in range(3))
    bufs = []
    for i in range(2):
        b = Tiles()
        b.e1, b.e2, b.pt = A.take(NB, T), A.take(NB, T), k.mixT[:, 4 + 2 * i:6 + 2 * i, :]
        b.tags, b.free, b.pt_free = k.tags[:, 2 * i:2 * i + 2, :], [], []
        bufs.append(b)
    got = Tiles()
    got.raw_free = []
    interleave(rotated(k, q, 8, dq, "dif", raw, got))
    dq_done = got.last
    interleave(rotated(k, q, 10, dk, "dif", raw, got))
    dk_done = got.last
    a = q.act.do(lambda e: e.activation(k.neg_rate[:, :], k.ret_decay[:, :], ACT.Exp), after=[k.params])
    rates = q.dve.do(lambda e: e.tensor_scalar(k.neg_rate[:, :], k.neg_rate[:, :], -1.0, None, ALU.mult), after=[a])
    lam = k.lam
    for i in range(2):
        q.dve.do(lambda e, i=i: e.tensor_tensor(k.lqk[:, 2 * i, :], k.lqk[:, 2 * i, :], k.lqk[:, 2 * i + 1, :], ALU.mult), after=[k.params])
        s = q.dve.do(lambda e, i=i: e.tensor_reduce(lam[:, i:i + 1], k.lqk[:, 2 * i, :], AXX, ALU.add))
    s = q.act.do(lambda e: e.activation(lam[:, 0:2], lam[:, 0:2], ACT.Exp), after=[s])
    q.dve.do(lambda e: e.tensor_tensor(lam[:, 2:3], lam[:, 1:2], lam[:, 0:1], ALU.subtract), after=[s])
    neg_lam = q.dve.do(lambda e: e.tensor_scalar(lam[:, 2:3], lam[:, 2:3], -LAM_INIT, None, ALU.add))
    q.dve.do(lambda e: e.tensor_scalar(k.subln[:, :], k.subln[:, :], 1.0 - LAM_INIT, None, ALU.mult), after=[k.params])
    for c in range(2):
        dv_done = token_major(k, q, ("ev_in", 12 + c), dv[:, :, 256 * c:256 * c + 256])

    def retention_projections():
        yield from rotated(k, q, 0, rq, "ret", raw, got)
        got.rq = got.last
        yield from rotated(k, q, 2, rk, "ret", raw, got)
        got.rk = got.last
        for c in range(2):
            got.rv = token_major(k, q, ("ev_in", 4 + c), rv[:, :, 256 * c:256 * c + 256])
            yield
        for c in range(2):
            got.gate = token_major(k, q, ("ev_in", 6 + c), gate[:, :, 256 * c:256 * c + 256])
            yield

    o_banks, o_steps = [k.banks_o.take() for _ in range(NB)], [None] * HEADS
    ready = [dq_done, dk_done, dv_done]
    interleave(*[diff_heads(k, q, (2 * i, 2 * i + 1), bufs[i], dq, dk, dv, ready, neg_lam, o_banks, o_steps) for i in range(2)],
               retention_projections())
    last = [o_steps[3][tb] for tb in range(NB)]
    mixed = []

    def diff_out(o_banks):
        for tb in range(NB):
            ss = sums_of_squares(k, q, o_banks[tb].tile, last[tb], HEADS, HD, k.hrs[:, HEADS * tb:HEADS * tb + HEADS])
        rs = rms_scale(k, q, k.hrs, 8, HD, RMS_EPS, ss)
        yield
        for tb in range(NB):
            for h in range(HEADS):
                i = tb * HEADS + h
                done = q.dve.do(lambda e, tb=tb, h=h, i=i: e.scalar_tensor_tensor(
                    out=y[:, tb, 512 + h * HD:512 + (h + 1) * HD], in0=o_banks[tb].tile[:, h * HD:(h + 1) * HD], scalar=k.hrs[:, i:i + 1],
                    in1=k.subln[:, :], op0=ALU.mult, op1=ALU.mult), after=[rs], chain=h == 0)
            o_banks[tb].free = [done]
        got.gate = silu_in_place(k, q, gate, got.gate)
        yield
        writes = [mix_transposes(k, q, y[:, :, 512:1024], tb, 4, [done], k.banks_b) for tb in range(NB)]
        mixed.extend(write() for write in writes)

    diff_banks, o_banks, o_steps = o_banks, [k.banks.take() for _ in range(NB)], [None] * HEADS
    ready = [got.rq, got.rk, got.rv]
    interleave(*[retention_heads(k, q, (2 * i, 2 * i + 1), bufs[i], rq, rk, rv, ready, rates, o_banks, o_steps) for i in range(2)],
               diff_out(diff_banks))

    def stats(tb):
        part = slice(HEADS * tb, HEADS * tb + HEADS)
        for h in range(HEADS):
            q.dve.do(lambda e, h=h, o_banks=o_banks: e.bn_stats(k.hbn[:, HEADS * tb + h, :], o_banks[tb].tile[:, h * HD:(h + 1) * HD]), after=[o_steps[3][tb]],
                     chain=False)
        for h in range(HEADS):
            q.dve.do(lambda e, h=h: e.bn_aggr(k.hmv[:, HEADS * tb + h, :], k.hbn[:, HEADS * tb + h, :]), chain=h == 0)
        var = q.dve.do(lambda e: e.tensor_scalar(k.hrs[:, part], k.hmv[:, part, 1], LN_EPS, None, ALU.add))
        got.rs = q.pool.do(lambda e: e.tensor_tensor(k.hrs[:, part], k.hrs[:, part], k.neg_half[:, 0:HEADS], ALU.pow), after=[var])

    def scale(tb):
        for h in range(HEADS):
            i = tb * HEADS + h
            done = q.dve.do(lambda e, i=i, o_banks=o_banks, h=h: e.tensor_scalar(y[:, tb, h * HD:(h + 1) * HD], o_banks[tb].tile[:, h * HD:(h + 1) * HD],
                                                      k.hmv[:, i, 0:1], k.hrs[:, i:i + 1], ALU.subtract, ALU.mult), after=[got.rs], chain=h == 0)
        o_banks[tb].free = [done]
        return y, q.dve.do(lambda e: e.tensor_tensor(y[:, tb, 0:512], y[:, tb, 0:512], gate[:, tb, :], ALU.mult), after=[got.gate])

    meanwhile = load_router(k, q, 0, mixed)
    return out_projection(k, q, "ev_out", *normed_heads(k, q, "ev_out", stats, scale, 0, mixed), meanwhile)


def probabilities_times_v(k, q, p, pt, p_ready, pt_free, v, h, v_ready, o_banks):
    bank = k.banks_b.take()
    view = bank.tile[:, :].rearrange("p (a b) -> p a b", a=NB)
    step = transposes(q, bank, k.ident, [(view[:, kb, b * P:(b + 1) * P], p[:, b, kb * P:(kb + 1) * P])
                                         for kb in range(NB) for b in range(NB)], after=[p_ready])
    for s in pt_free:
        q.act.wait(s)
    got = evacuate(k, q, bank, step, pt, view)
    out = []
    for tb in range(NB):
        out.append(product(q, o_banks[tb], [(o_banks[tb].tile[:, h * HD:(h + 1) * HD],
                                             [(pt[:, kb, tb * P:(tb + 1) * P], v[:, kb, h * HD:(h + 1) * HD]) for kb in range(NB)])],
                           after=[got, v_ready]))
    return step, out


def decayed_scores(k, q, la, qT, kT, heads_on, sides, diag, cross, ready, forward, first, work, refs, got):
    n = la.shape[1]
    b, f, qf, kf = work
    flat = lambda a: a.rearrange("p a b -> p (a b)")
    mask_base = 0 if forward else len(LEVELS)

    def blockwise(lhs, rhs, mask, after):
        steps, copies = [], []
        for side in sides:
            bank = k.banks_b.take()
            view = bank.tile[:, :].rearrange("p (a b) -> p a b", a=4)
            groups = []
            for i in range(2):
                r, j = heads_on(side, i)
                for blk in range(NB):
                    ts = slice(blk * P, (blk + 1) * P)
                    groups.append((view[:, 2 * i + blk, :], [(lhs[r, j, ts], rhs[r, j, ts])]))
            step = product(q, bank, groups, after=after)
            steps.append(step)

            def copy(side=side, bank=bank, view=view, step=step):
                done = q.dve.do(lambda e: e.copy_predicated(diag[:, side, :, :], mid_bcast(mask, 4), view), after=[step] + first)
                bank.free = [done]

            copies.append(copy)
        return steps, copies

    def factor(m, free):
        size = 1 << m
        if m >= 7:
            mid, width = refs[:, m - 7, 0:n, :].rearrange("p a b -> p (a b)"), CHUNK
        else:
            mid, width = flat(b)[:, size // 2 - (1 if forward else 0)::size], size
        bv, fv = (flat(a).rearrange("p (a b) -> p a b", b=width) for a in (b, f))
        d = q.dve.do(lambda e, mid=mid, width=width: e.tensor_tensor(fv, bv, bcast(mid, width), ALU.subtract), after=free)
        if len(sides) == 2:
            d = q.dve.do(lambda e: e.scalar_tensor_tensor(out=flat(f), in0=flat(f), scalar=-1.0, in1=flat(f), op0=ALU.mult, op1=ALU.min))
            return q.act.do(lambda e: e.activation(flat(f), flat(f), ACT.Exp), after=[d])
        q.act.do(lambda e: e.activation(flat(f), flat(f), ACT.Abs), after=[d])
        return q.act.do(lambda e: e.activation(flat(f), flat(f), ACT.Exp, scale=-1.0))

    copies = blockwise(kT, qT, k.masks[:, 2 * len(LEVELS), :], ready[0:2])[1] if forward else []
    if forward:
        q.dve.do(lambda e: e.tensor_tensor_scan(flat(b), k.tab("scan")[:, 0:n * T], flat(la), 0.0, ALU.mult, ALU.add), after=ready)
        tot = b[:, :, CHUNK - 1::CHUNK]
    else:
        q.dve.do(lambda e: e.tensor_tensor(flat(f)[:, 1:n * T], flat(la)[:, 0:n * T - 1], k.tab("scan")[:, 1:n * T], ALU.mult), after=ready)
        q.dve.do(lambda e: e.memset(flat(f)[:, 0:1], 0.0))
        q.dve.do(lambda e: e.tensor_tensor_scan(flat(b), k.tab("scan")[:, 0:n * T], flat(f), 0.0, ALU.mult, ALU.add))
        q.dve.do(lambda e: e.tensor_tensor(refs[:, 2, 0:n, :], b[:, :, CHUNK - 1::CHUNK], la[:, :, CHUNK - 1::CHUNK], ALU.add))
        tot = refs[:, 2, 0:n, :]
    yield
    q.dve.do(lambda e: e.memset(refs[:, 0:2, :, :], 0.0))
    q.dve.do(lambda e, tot=tot: e.tensor_copy(refs[:, 0, 0:n, 0::2], tot[:, :, 0::2]))
    q.dve.do(lambda e, tot=tot: e.tensor_copy(refs[:, 1, 0:n, 1:2], tot[:, :, 1:2]), chain=False)
    q.dve.do(lambda e, tot=tot: e.tensor_tensor(refs[:, 1, 0:n, 0:1], tot[:, :, 0:1], tot[:, :, 1:2], ALU.add), chain=False)
    q.dve.do(lambda e, tot=tot: e.tensor_scalar(refs[:, 1, 0:n, 3:4], tot[:, :, 2:3], -1.0, None, ALU.mult), chain=False)
    levels = (8,) + LEVELS
    ex = factor(levels[0], [])
    factors_free = []
    for m in levels:
        yield
        qd = q.dve.do(lambda e: e.tensor_tensor(flat(qf), flat(f), flat(qT), ALU.mult), after=[ex] + factors_free)
        kd = q.pool.do(lambda e: e.tensor_tensor(flat(kf), flat(f), flat(kT), ALU.mult), after=[ex] + factors_free + ready)
        for copy in copies:
            copy()
        if m == 8:
            sb, tb = (0, 1) if forward else (1, 0)
            factors_free, copies = [], []
            for side in sides:
                bank = k.banks_b.take()
                view = bank.tile[:, 0:2 * P].rearrange("p (a b) -> p a b", a=2)
                groups = []
                for i in range(2):
                    r, j = heads_on(side, i)
                    groups.append((view[:, i, :], [(kf[r, j, sb * P:(sb + 1) * P], qf[r, j, tb * P:(tb + 1) * P])]))
                step = product(q, bank, groups, after=[qd, kd])
                factors_free.append(step)
                copies.append(lambda side=side, bank=bank, view=view, step=step: got.append(evacuate(k, q, bank, step, cross[:, side, :, :], view)))
        else:
            factors_free, copies = blockwise(kf, qf, k.masks[:, mask_base + LEVELS.index(m), :], [qd, kd])
        if m > 1:
            ex = factor(m - 1, [kd])
    yield
    for copy in copies:
        copy()
    got.append(Step(q.dve.sem, q.dve.count))


def decayed_values(k, q, diag, crosses, head_of, v, ready):
    o_banks = [k.banks_o.take() for _ in range(NB)]
    steps = []
    for tb in range(NB):
        groups = []
        for side in range(2):
            for i in range(2):
                h = head_of(side, i)
                vs = slice(h * HD, (h + 1) * HD)
                parts = [(diag[:, side, 2 * i + tb, :], v[:, tb, vs])]
                if crosses[tb] is not None:
                    parts.append((crosses[tb][:, side, i, :], v[:, 1 - tb, vs]))
                groups.append((o_banks[tb].tile[:, vs], parts))
        steps.append(product(q, o_banks[tb], groups, after=ready))
    return o_banks, steps


def silu_in_place(k, q, gate, ready):
    return q.act.do(lambda e: e.activation(gate, gate, ACT.Silu), after=[ready])


def gated_rms(k, q, name, o_banks, steps, gain, gate, gate_ready, y, rest):
    got = Tiles()

    def stats(tb):
        sums = k.hrs[:, HEADS * tb:HEADS * tb + HEADS]
        ss = sums_of_squares(k, q, o_banks[tb].tile, steps[tb], HEADS, HD, sums)
        got.rs = rms_scale(k, q, sums, HEADS, HD, RMS_EPS, ss)

    def scale(tb):
        for h in range(HEADS):
            i = tb * HEADS + h
            done = q.dve.do(lambda e, i=i, h=h: e.scalar_tensor_tensor(
                out=y[:, tb, h * HD:(h + 1) * HD], in0=o_banks[tb].tile[:, h * HD:(h + 1) * HD], scalar=k.hrs[:, i:i + 1],
                in1=gain, op0=ALU.mult, op1=ALU.mult), after=[got.rs, k.params], chain=h == 0)
        o_banks[tb].free = [done]
        return y, q.dve.do(lambda e: e.tensor_tensor(y[:, tb, 0:512], y[:, tb, 0:512], gate[:, tb, :], ALU.mult), after=[gate_ready])

    return normed_heads(k, q, name, stats, scale, 4, rest)


def log_sigmoid(k, q, z, tmp, ready):
    a = q.dve.do(lambda e: e.scalar_tensor_tensor(out=tmp, in0=z, scalar=-1.0, in1=z, op0=ALU.mult, op1=ALU.min), after=ready)
    q.act.do(lambda e: e.activation(tmp, tmp, ACT.Exp), after=[a])
    return q.act.do(lambda e: e.activation(tmp, tmp, ACT.Ln, bias=1.0))


def mla_gla_mixer(k, q):
    A = k.arena
    A.restart()
    y = k.acc
    gla_v, gate = A.take(NB, 512), A.take(NB, 512)
    gq, gk = A.take(2, T), A.take(2, T)
    gla_end = A.at
    cq, ckv = A.take(NB, MLA_QR), A.take(NB, MLA_KVR)
    cqT, ckvT = A.take(2, T), A.take(1, T)
    A.at = gla_end
    bufs = [Tiles(), Tiles()]
    bufs[1].e1, bufs[1].pt = A.take(NB, T), A.take(NB, T)
    A.at = gla_end + 3 * NB * T
    qh, kh = A.take(HEADS, T), A.take(HEADS, T)
    v = A.take(NB, 512)
    bufs[0].e1, bufs[0].pt = A.take(NB, T), A.take(NB, T)
    narrow = k.rot_tmp[:, 0:NB * P].rearrange("p (a b) -> p a b", a=NB)
    mla_end = A.at
    lr_at = A.words - T
    assert mla_end <= lr_at
    A.at = lr_at
    narrow_T = A.take(1, T)
    bank, step = project(k, q, ("od_in", 0), "tok")
    for b in range(NB):
        sq = sums_of_squares(k, q, bank.tile[:, b * 256:(b + 1) * 256], step, 1, MLA_QR, k.hrs[:, b:b + 1])
    bank2, step2 = project(k, q, ("od_in", 1), "tok")
    narrow_in = bank2.tile[:, :].rearrange("p (a b) -> p a b", a=NB)
    for b in range(NB):
        sk = sums_of_squares(k, q, narrow_in[:, b, 0:MLA_KVR], step2, 1, MLA_KVR, k.hrs[:, 8 + b:9 + b])
    rs = rms_scale(k, q, k.hrs, 2, MLA_QR, RMS_EPS, sq)
    rk = rms_scale(k, q, k.hrs[:, 8:10], 2, MLA_KVR, RMS_EPS, sk)
    for b in range(NB):
        a = q.dve.do(lambda e, b=b, bank=bank: e.tensor_scalar(cq[:, b, :], bank.tile[:, b * 256:(b + 1) * 256], k.hrs[:, b:b + 1], None, ALU.mult), after=[rs])
    bank.free = [a]
    for b in range(NB):
        c = q.dve.do(lambda e, b=b: e.tensor_scalar(ckv[:, b, :], narrow_in[:, b, 0:MLA_KVR], k.hrs[:, 8 + b:9 + b], None, ALU.mult), after=[rk])
    G = Tiles()

    def feature_major(c, dst, scale=None):
        bank, step = project(k, q, ("od_in", c), "feat", k.banks_b)
        return evacuate(k, q, bank, step, dst, bank.tile[:, :].rearrange("p (a b) -> p a b", a=2), scale=scale)

    ropes = slice(MLA_NOPE, MLA_QD)
    kr_raw = narrow_T[ropes, 0:1, :]
    q.dve.do(lambda e: e.memset(narrow, 0.0))
    q.dve.do(lambda e: e.tensor_copy(narrow[:, :, ropes], narrow_in[:, :, MLA_KVR:MLA_KVR + MLA_ROPE]))
    for way in range(2):
        at = T - 2 * GATE_RANK + GATE_RANK * way
        got = q.dve.do(lambda e, way=way, at=at: e.tensor_copy(narrow[:, :, 32 * way:32 * way + GATE_RANK], narrow_in[:, :, at:at + GATE_RANK]))
    bank2.free = [got]
    G.q_done = feature_major(2, gq, 64 ** -0.5)
    G.k_done = feature_major(3, gk)
    bank_n = k.banks.take()
    step = transposes(q, bank_n, k.ident, [(bank_n.tile[:, b * P:(b + 1) * P], narrow[:, b, :]) for b in range(NB)], after=[got])
    kr = lr_done = evacuate(k, q, bank_n, step, narrow_T[:, 0, :], bank_n.tile[:, 0:T], engine="dve")
    tb_bank = k.banks.take()
    view = tb_bank.tile[:, :].rearrange("p (a b) -> p a b", a=2)
    step = transposes(q, tb_bank, k.ident, [(view[:, j, b * P:(b + 1) * P], cq[:, b, j * P:(j + 1) * P]) for j in range(2) for b in range(NB)], after=[a])
    for j in range(2):
        cq_done = q.dve.do(lambda e, j=j, view=view: e.tensor_scalar(cqT[:, j, :], view[:, j, :], k.q_norm[:, j:j + 1], None, ALU.mult), after=[step, k.params])
    tb_bank.free = [cq_done]
    tb2 = k.banks.take()
    step = transposes(q, tb2, k.ident, [(tb2.tile[:, b * P:(b + 1) * P], ckv[:, b, :]) for b in range(NB)], after=[c])
    ckv_done = q.dve.do(lambda e: e.tensor_scalar(ckvT[:, 0, :], tb2.tile[:, 0:T], k.kv_norm[:, 0:1], None, ALU.mult), after=[step])
    tb2.free = [ckv_done]
    for pair in range(2):
        bank = k.banks.take()
        groups = [(bank.tile[0:MLA_QD, i * T:(i + 1) * T],
                   [(k.w_uq[:, j, (2 * pair + i) * MLA_QD:(2 * pair + i + 1) * MLA_QD], cqT[:, j, :]) for j in range(2)]) for i in range(2)]
        step = product(q, bank, groups, after=[cq_done, k.params])
        src = bank.tile[0:MLA_QD, :].rearrange("p (a b) -> p a b", a=2)
        q_raw = evacuate(k, q, bank, step, qh[0:MLA_QD, 2 * pair:2 * pair + 2, :], src)
        bank = k.banks.take()
        groups = [(bank.tile[0:MLA_NOPE, i * T:(i + 1) * T], [(k.w_ukv[:, (2 * pair + i) * 192:(2 * pair + i) * 192 + MLA_NOPE], ckvT[:, 0, :])])
                  for i in range(2)]
        step = product(q, bank, groups, after=[ckv_done])
        src = bank.tile[0:MLA_NOPE, :].rearrange("p (a b) -> p a b", a=2)
        k_raw = evacuate(k, q, bank, step, kh[0:MLA_NOPE, 2 * pair:2 * pair + 2, :], src)
        bank = k.banks.take()
        groups = [(bank.tile[:, (b * 2 + i) * HD:(b * 2 + i + 1) * HD],
                   [(ckvT[:, 0, b * P:(b + 1) * P], k.w_ukv[:, (2 * pair + i) * 192 + MLA_NOPE:(2 * pair + i + 1) * 192])])
                  for b in range(NB) for i in range(2)]
        step = product(q, bank, groups, after=[ckv_done])
        v_done = evacuate(k, q, bank, step, v[:, :, 256 * pair:256 * pair + 256], bank.tile[:, :].rearrange("p (a b) -> p a b", a=2), engine="dve")
    cos, sin, swap = (k.tab(n)[ropes, :] for n in ("mla_cos", "mla_sin", "mla_swap"))
    bank = k.banks.take()
    step = product(q, bank, [(bank.tile[ropes, 0:T], [(swap, kr_raw[:, 0, :])])], after=[kr])
    g = q.dve.do(lambda e, bank=bank: e.tensor_tensor(k.rot_tmp[ropes, 0:T], bank.tile[ropes, 0:T], sin, ALU.mult), after=[step])
    bank.free = [g]
    q.dve.do(lambda e: e.tensor_tensor(kr_raw[:, 0, :], kr_raw[:, 0, :], cos, ALU.mult))
    k_done = q.dve.do(lambda e: e.tensor_tensor(kh[ropes, :, :], mid_bcast(kr_raw[:, 0, :], HEADS), mid_bcast(k.rot_tmp[ropes, 0:T], HEADS), ALU.add))
    q_done = []
    for pair in range(2):
        part = qh[ropes, 2 * pair:2 * pair + 2, :]
        bank = k.banks_b.take()
        view = bank.tile[ropes, :].rearrange("p (a b) -> p a b", a=2)
        step = product(q, bank, [(view[:, i, :], [(swap, part[:, i, :])]) for i in range(2)], after=[q_raw])
        t2 = k.rot_tmp[ropes, :].rearrange("p (a b) -> p a b", a=2)
        g = q.dve.do(lambda e, t2=t2, view=view: e.tensor_tensor(t2, view, mid_bcast(sin, 2), ALU.mult), after=[step])
        bank.free = [g]
        q.dve.do(lambda e, part=part: e.tensor_tensor(part, part, mid_bcast(cos, 2), ALU.mult))
        q_done.append(q.dve.do(lambda e, part=part, t2=t2: e.tensor_tensor(part, part, t2, ALU.add)))
    token_major(k, q, ("od_in", 4), gla_v[:, :, 0:256])
    mixed = []

    def attention(pair):
        b, tags, free, pt_free = bufs[pair], k.tags[:, pair, :], [], []
        out_bank = k.banks_o.take()
        for i in range(2):
            h = 2 * pair + i
            bank = k.banks_b.take()
            view = bank.tile[:, :].rearrange("p (a b) -> p a b", a=NB)
            step = product(q, bank, [(view[:, c, :], [(qh[0:MLA_QD, h, c * P:(c + 1) * P], kh[0:MLA_QD, h, :])]) for c in range(NB)],
                           after=[q_done[pair], k_done, k_raw, v_done])
            ex = softmax_rows(k, q, bank, step, b.e1, MLA_QD ** -0.5, tags, free)
            yield
            q.dve.do(lambda e: e.reciprocal(tags[:, 6:8], tags[:, 4:6]), after=[ex])
            for c in range(NB):
                p = q.dve.do(lambda e, c=c: e.tensor_scalar(b.e1[:, c, :], b.e1[:, c, :], tags[:, 6 + c:7 + c], None, ALU.mult), chain=c == 0)
            yield
            bank = k.banks_b.take()
            view = bank.tile[:, :].rearrange("p (a b) -> p a b", a=NB)
            step = transposes(q, bank, k.ident, [(view[:, kb, c * P:(c + 1) * P], b.e1[:, c, kb * P:(kb + 1) * P])
                                                 for kb in range(NB) for c in range(NB)], after=[p])
            free = [step, p]
            for x in pt_free:
                q.act.wait(x)
            turned = evacuate(k, q, bank, step, b.pt, view)
            yield
            step = product(q, out_bank, [(out_bank.tile[:, i * T:(i + 1) * T],
                                          [(v[:, kb, h * HD:(h + 1) * HD], b.pt[:, kb, :]) for kb in range(NB)])], after=[turned])
            pt_free = [step]
            yield
        q.act.wait(k.masks_made)
        mixed.append(evacuate(k, q, out_bank, step, k.mixT[:, 2 * pair:2 * pair + 2, :], out_bank.tile[:, :].rearrange("p (a b) -> p a b", a=2)))

    def gla_projections():
        G.v_done = token_major(k, q, ("od_in", 5), gla_v[:, :, 256:512])
        yield
        G.gate = token_major(k, q, ("od_in", 6), gate[:, :, 0:256])

    la = [k.mixT[:, 4 + 2 * i:6 + 2 * i, :] for i in range(2)]
    la_done = []

    def gate_logs():
        zt = k.rot_tmp[:, :].rearrange("p (a b) -> p a b", a=2)
        for way in range(2):
            rank = slice(32 * way, 32 * way + GATE_RANK)
            bank = k.banks.take()
            view = bank.tile[:, :].rearrange("p (a b) -> p a b", a=2)
            step = product(q, bank, [(view[:, j, :], [(k.gla_w2[rank, j * P:(j + 1) * P], narrow_T[rank, 0, :])]) for j in range(2)],
                           after=[lr_done, k.params])
            for x in (q_done[1], k.masks_made):
                q.dve.wait(x)
            for j in range(2):
                z = q.dve.do(lambda e, view=view, j=j, way=way: e.tensor_scalar(zt[:, j, :], view[:, j, :], k.gla_b[:, way, j:j + 1], None, ALU.add), after=[step])
            bank.free = [z]
            ln = log_sigmoid(k, q, zt, la[way], [])
            yield
            q.dve.do(lambda e, way=way: e.scalar_tensor_tensor(out=la[way], in0=zt, scalar=0.0, in1=la[way], op0=ALU.min, op1=ALU.subtract), after=[ln])
            la_done.append(q.dve.do(lambda e, way=way: e.tensor_scalar(la[way], la[way], 1.0 / GLA_TAU, None, ALU.mult)))
            yield

    interleave(attention(0), attention(1), gla_projections(), gate_logs())

    A.at = gla_end
    diag = A.take(2, 4, P)
    crosses = [A.take(2, 2, P) for _ in range(2)]
    work = [[A.take(2, T) for _ in range(4)] for _ in range(2)]
    assert A.at <= lr_at
    for x in mixed + [Step(q.pe.sem, q.pe.count)]:
        for queue in (q.act, q.dve, q.pool):
            queue.wait(x)
    q.act.wait(Step(q.dve.sem, q.dve.count))
    q.dve.wait(Step(q.act.sem, q.act.count))
    q.dve.wait(k.masks_made)
    clear = q.dve.do(lambda e: e.memset(diag.rearrange("p a b c -> p (a b c)"), 0.0))
    rows_of = lambda side, i: (slice(64 * side, 64 * side + 64), i)
    G.gate = token_major(k, q, ("od_in", 7), gate[:, :, 256:512])
    done = []
    interleave(*[decayed_scores(k, q, la[way], gq, gk, rows_of, (0, 1), diag, crosses[way], [G.q_done, G.k_done, la_done[way]], way == 0,
                                [clear], work[way], k.refs[way], done) for way in range(2)])
    gate_done = silu_in_place(k, q, gate, G.gate)
    q.act.wait(Step(q.pe.sem, q.pe.count))
    parts = mix_parts(k, q, k.mixT[:, 0:4, :], (slice(0, P), slice(0, 4), slice(0, T)), mixed[-1])
    o_banks, o_steps = decayed_values(k, q, diag, (crosses[1], crosses[0]), lambda side, i: 2 * i + side, gla_v, done + [G.v_done])
    router = load_router(k, q, 1, [parts])
    begun_and_ready = gated_rms(k, q, "od_out", o_banks, o_steps, k.gla_norm[:, :], gate, gate_done, y, [parts])
    return out_projection(k, q, "od_out", *begun_and_ready, router)


def pool_hgrn_mixer(k, q, layer):
    A = k.arena
    A.restart()
    y = k.acc
    gate, v = A.take(NB, 512), A.take(NB, 512)
    qT, kT, la = A.take(HEADS, T), A.take(HEADS, T), A.take(HEADS, T)
    diag, cross = A.take(2, 4, P), A.take(2, 2, P)
    work = [A.take(HEADS, T) for _ in range(3)] + [k.mixT[:, 4:8, :]]
    f = work[0]
    u = work[2].rearrange("p a b -> p (a b)").rearrange("p (a b) -> p a b", a=NB)
    for c in range(2):
        bank, step = project(k, q, ("in2", 4 + c), "feat")
        f_done = evacuate(k, q, bank, step, f[:, 2 * c:2 * c + 2, :], bank.tile[:, :].rearrange("p (a b) -> p a b", a=2))
    G, mixed = Tiles(), []

    def forget_gates():
        ln = log_sigmoid(k, q, f, la, [f_done])
        yield
        a = q.dve.do(lambda e: e.tensor_scalar(kT, f, -1.0, 0.0, ALU.mult, ALU.min), after=[ln])
        a = q.dve.do(lambda e: e.tensor_tensor(kT, kT, la, ALU.subtract))
        kk = q.act.do(lambda e: e.activation(kT, kT, ACT.Exp), after=[a])
        yield
        la_done = q.dve.do(lambda e: e.scalar_tensor_tensor(out=la, in0=f, scalar=0.0, in1=la, op0=ALU.min, op1=ALU.subtract))
        if layer == 1:
            lbp, lbd = k.lb_param, k.lb_work
            q.dve.do(lambda e: e.tensor_tensor(lbd[:, 0, :], lbp[:, 1, :], lbp[:, 0, :], ALU.subtract), after=[k.params])
            d = log_sigmoid(k, q, lbd[:, 0, :], lbd[:, 1, :], [])
            yield
            q.dve.do(lambda e: e.scalar_tensor_tensor(out=lbd[:, 2, :], in0=lbd[:, 0, :], scalar=0.0, in1=lbd[:, 1, :], op0=ALU.min, op1=ALU.subtract), after=[d])
            q.dve.do(lambda e: e.tensor_scalar(lbd[:, 3, :], lbd[:, 0, :], -1.0, 0.0, ALU.mult, ALU.min))
            d = q.dve.do(lambda e: e.tensor_tensor(lbd[:, 3, :], lbd[:, 3, :], lbd[:, 1, :], ALU.subtract))
            one = q.act.do(lambda e: e.activation(lbd[:, 0, :], lbd[:, 3, :], ACT.Exp), after=[d])
            yield
            kk = q.dve.do(lambda e: e.tensor_tensor(kT, kT, bcast(lbd[:, 0, :], T), ALU.mult), after=[one, kk])
            q.dve.do(lambda e: e.tensor_tensor(la, la, bcast(lbd[:, 3, :], T), ALU.add))
            q.dve.do(lambda e: e.tensor_tensor(f, la, bcast(lbd[:, 2, :], T), ALU.subtract))
            d = log_sigmoid(k, q, f, work[1], [])
            yield
            q.dve.do(lambda e: e.tensor_tensor(la, la, bcast(lbd[:, 2, :], T), ALU.max))
            la_done = q.dve.do(lambda e: e.tensor_tensor(la, la, work[1], ALU.add), after=[d])
        G.kk, G.la = kk, la_done

    def pooling():
        for c in range(2):
            bank, step = project(k, q, ("in2", c), "tok")
            yield
            G.u_done = evacuate(k, q, bank, step, u[:, :, 256 * c:256 * c + 256], bank.tile[:, :].rearrange("p (a b) -> p a b", a=NB))
        for c in range(2):
            bank, step = project(k, q, ("in2", 2 + c), "feat")
            yield
            G.q_done = evacuate(k, q, bank, step, qT[:, 2 * c:2 * c + 2, :], bank.tile[:, :].rearrange("p (a b) -> p a b", a=2), scale=HD ** -0.5)
        pooled = work[3]
        for half in range(2):
            bank = k.banks.take()
            groups = [(bank.tile[:, i * T:(i + 1) * T],
                       [(u[:, sb, (2 * half + i) * P:(2 * half + i + 1) * P], k.pool_mat[:, sb, 2 * half + i, :]) for sb in range(NB)]) for i in range(2)]
            step = product(q, bank, groups, after=[G.u_done, k.pool_here])
            p_done = evacuate(k, q, bank, step, pooled[:, 2 * half:2 * half + 2, :], bank.tile[:, :].rearrange("p (a b) -> p a b", a=2))
            yield
            bank = k.banks.take()
            groups = [(bank.tile[:, i * T:(i + 1) * T], [(k.pool_w[:, layer, 2 * half + i, :], pooled[:, 2 * half + i, :])]) for i in range(2)]
            step = product(q, bank, groups, after=[p_done])
            for i in range(2):
                g = 2 * half + i
                got = q.act.do(lambda e, g=g, i=i, bank=bank: e.activation(k.mixT[:, g, :], bank.tile[:, i * T:(i + 1) * T], ACT.Copy,
                                                                scale=k.pool_scale[:, layer, g:g + 1]), after=[step])
            bank.free = [got]
            mixed.append(got)

    interleave(pooling(), forget_gates())
    clear = q.dve.do(lambda e: e.memset(diag.rearrange("p a b c -> p (a b c)"), 0.0))
    for queue in (q.dve, q.pool, q.act):
        queue.wait(mixed[-1])

    def value_projections():
        for c in range(2):
            G.v_done = token_major(k, q, ("in2", 6 + c), v[:, :, 256 * c:256 * c + 256])
            for _ in range(2):
                yield
        for c in range(2):
            G.gate = token_major(k, q, ("in2", 8 + c), gate[:, :, 256 * c:256 * c + 256])
            for _ in range(2):
                yield

    done = []
    heads = [slice(2 * s, 2 * s + 2) for s in range(2)]
    interleave(*[decayed_scores(k, q, la[:, hs, :], qT[:, hs, :], kT[:, hs, :], lambda side, i: (slice(0, P), i), (s,), diag, cross,
                                [G.q_done, G.kk, G.la], True, [clear], [w[:, hs, :] for w in work], k.refs[s], done)
                 for s, hs in enumerate(heads)], value_projections())
    gate_done = silu_in_place(k, q, gate, G.gate)
    q.act.wait(Step(q.pe.sem, q.pe.count))
    parts = mix_parts(k, q, k.mixT[:, 0:4, :], (slice(0, P), slice(0, 4), slice(0, T)), mixed[-1])
    o_banks, o_steps = decayed_values(k, q, diag, (None, cross), lambda side, i: 2 * side + i, v, done + [G.v_done])
    return out_projection(k, q, "out2", *gated_rms(k, q, "out2", o_banks, o_steps, k.hgrn_g[:, layer, :], gate, gate_done, y, [parts]))


class FfnWeights:

    def __init__(self, k, q):
        self.k, self.q, self.chunk, self.ready = k, q, {}, []
        self.order = [part for f in range(FT + FFN_LAG)
                      for part in [("gate", f), ("up", f)] * (f < FT) + [("down", f - FFN_LAG)] * (f >= FFN_LAG)]

    def fill(self, wanted=PARTS):
        k, q = self.k, self.q
        while self.order and len(self.ready) < wanted:
            name, tile = self.order.pop(0)
            if tile % 2 == 0 and name != "up":
                for part in ("gate", "up") if name == "gate" else ("down",):
                    self.chunk[part] = k.ring.next((part, tile // 2))
            n, w, here = self.chunk[name]
            src = w[:, :, (tile % 2) * P:(tile % 2 + 1) * P] if name != "down" else w[:, tile % 2:tile % 2 + 1, :]
            parts = k.split.split(q, src, here)
            self.ready.append(((name, tile), parts))
            if tile % 2 == 1:
                k.ring.release(n, parts[3])

    def take(self, name, tile):
        assert self.ready[0][0] == (name, tile)
        return self.ready[0][1]

    def used(self, buffer, step):
        self.k.split.free[buffer] = [step]
        self.ready.pop(0)
        self.fill()


def ffn(k, q, weights):
    A = k.arena
    silu, hidden = k.ffn_tmp[0], k.ffn_tmp[1]
    out_banks, work_banks = k.all_banks[0:4], Banks(k.all_banks[4:8])
    for x in after_everything(q):
        q.act.wait(x)
        q.dve.wait(x)
    for tb in range(NB):
        scaled = q.dve.do(lambda e, tb=tb: e.tensor_scalar(k.acc[:, tb, :], k.x_tok[:, tb, :], ALPHA, None, ALU.mult), after=k.x_ready)

    def down(e, blocks, halves, tiles):
        for tb in blocks:
            ts = slice(tb * P, (tb + 1) * P)
            for n in halves:
                for g, hi, lo in tiles:
                    hh, hl = k.hid_high[:, g % HIDDEN, ts], k.hid_low[:, g % HIDDEN, ts]
                    cols = slice(BANK * n, BANK * n + BANK)
                    for i, (lhs, rhs) in enumerate(((hh, hi), (hh, lo), (hl, hi))):
                        ins = e.matmul(out_banks[2 * tb + n].tile[:, :], lhs, rhs[:, 0, cols], start=g == 0 and i == 0, stop=g == FT - 1 and i == 2)
        return ins

    h_done = [None] * FT
    silu_free, slot_free = [[], []], [[] for _ in range(HIDDEN)]
    for f in range(FT + FFN_LAG):
        if f < FT:
            bank = work_banks.take()
            for i, name in enumerate(("gate", "up")):
                b, hi, lo, here = weights.take(name, f)
                step = product(q, bank, [three_passes(bank.tile[:, i * T:(i + 1) * T],
                                                      [((hi[:, j, :], lo[:, j, :]), (k.xh[:, j, :], k.xl[:, j, :])) for j in range(KT)])],
                               after=[here] + k.xT_ready)
                weights.used(b, step)
                if i == 0:
                    gate_step = step
            s, h, u = silu[:, f % 2, :], hidden[:, f % 2, :], bank.tile[:, T:2 * T]
            hh, hl = k.hid_high[:, f % HIDDEN, :], k.hid_low[:, f % HIDDEN, :]
            a = q.act.do(lambda e, s=s, bank=bank: e.activation(s, bank.tile[:, 0:T], ACT.Silu), after=[gate_step, step] + silu_free[f % 2], chain=False)
            h0 = q.dve.do(lambda e, h=h, s=s, u=u: e.tensor_tensor(h, s, u, ALU.mult), after=[a], chain=True)
            bank.free = [h0]
            h1 = q.act.do(lambda e, hh=hh, h=h: e.activation(hh, h, ACT.Copy), after=[h0] + slot_free[f % HIDDEN], chain=False)
            h_done[f] = q.dve.do(lambda e, hl=hl, h=h, hh=hh: e.tensor_tensor(hl, h, hh.bitcast(F32), ALU.subtract), after=[h1], chain=False)
            silu_free[f % 2] = [h_done[f]]
        if FFN_LAG <= f < FT:
            g = f - FFN_LAG
            b, hi, lo, here = weights.take("down", g)
            step = q.pe.do(lambda e, g=g, hi=hi, lo=lo: down(e, (0, 1), (0, 1), [(g, hi, lo)]), after=[here, h_done[g]] + ([s for b in out_banks for s in b.free] if g == 0 else []), chain=False)
            weights.used(b, step)
            slot_free[g % HIDDEN] = [step]
    parts = [weights.ready[i][1] for i in range(FFN_LAG)]
    last = [(FT - FFN_LAG + i, hi, lo) for i, (b, hi, lo, here) in enumerate(parts)]
    steps = [[q.pe.do(lambda e, tb=tb, n=n: down(e, (tb,), (n,), last), after=[part[3] for part in parts] + h_done[-FFN_LAG:], chain=False)
              for n in range(2)] for tb in range(NB)]
    for part in parts:
        weights.used(part[0], steps[-1][-1])

    def finish(tb):
        done = []
        for n in range(2):
            bank = out_banks[2 * tb + n]
            cols = slice(BANK * n, BANK * n + BANK)
            done.append(q.dve.do(lambda e, cols=cols, bank=bank: e.scalar_tensor_tensor(
                out=k.acc[:, tb, cols], in0=bank.tile[:, :], scalar=0.5, in1=k.acc[:, tb, cols], op0=ALU.mult, op1=ALU.add),
                after=[steps[tb][n], scaled], chain=False))
            bank.free = [done[-1]]
        return [[step] for step in done]

    return [lambda: finish(0), lambda: finish(1)]


def after_everything(q):
    return [Step(e.sem, e.count) for e in (q.pe, q.act, q.dve)]


def route(k, q, layer):
    R = k.route
    n_logits = N_GROUPS + N_EXPERTS
    buffer, hi, lo, here = k.router_parts
    bank = k.banks.take()
    step = product(q, bank, [three_passes(bank.tile[:, 0:T], [((hi[:, j, :], lo[:, j, :]), (k.xh[:, j, :], k.xl[:, j, :])) for j in range(KT)])],
                   after=k.xT_ready + [here])
    k.split.free[buffer] = [step]
    logits = k.rot_tmp[0:n_logits, 0:T]
    got = evacuate(k, q, bank, step, logits, bank.tile[0:n_logits, 0:T], engine="dve")
    bank = k.banks.take()
    view = bank.tile[:, 0:NB * n_logits].rearrange("p (a b) -> p a b", a=NB)
    step = transposes(q, bank, k.ident[0:n_logits, 0:n_logits], [(view[:, b, :], logits[:, b * P:(b + 1) * P]) for b in range(NB)], after=[got])
    lg, le = view[:, :, 0:N_GROUPS], view[:, :, N_GROUPS:n_logits]
    do = q.dve.do
    tt, ts, red = (lambda *a: lambda e: e.tensor_tensor(*a)), (lambda *a: lambda e: e.tensor_scalar(*a)), (lambda *a: lambda e: e.tensor_reduce(*a))
    do(tt(R.gl, lg, mid_bcast(k.b_grp[:, layer, :], NB), ALU.add), after=[step])
    bank.free = [do(tt(R.el, le, mid_bcast(k.b_exp[:, layer, :], NB), ALU.add))]

    def first_of(values, best, onehot, order, n):
        do(red(best, values, AXX, ALU.max))
        do(tt(onehot, values, bcast(best, n), ALU.is_equal))
        do(tt(onehot, onehot, mid_bcast(order, NB), ALU.mult))
        do(red(R.top, onehot, AXX, ALU.max))
        return do(tt(onehot, onehot, bcast(R.top, n), ALU.is_equal))

    first_of(R.gl, R.gmax, R.goh, k.tab("desc_grp"), N_GROUPS)
    d = do(tt(R.gl, R.gl, bcast(R.gmax, N_GROUPS), ALU.subtract))
    ex = q.act.do(lambda e: e.activation(R.gl, R.gl, ACT.Exp), after=[d])
    do(ts(R.goh, R.goh, 1.0, BIG, ALU.subtract, ALU.mult))
    el8 = R.el.rearrange("p a (g e) -> p (a g) e", e=PER_GROUP)
    do(tt(el8, el8, bcast(R.goh.rearrange("p a g -> p (a g)"), PER_GROUP), ALU.add))
    first_of(R.el, R.m1, R.oh1, k.tab("desc_exp"), N_EXPERTS)
    do(lambda e: e.scalar_tensor_tensor(out=R.el, in0=R.oh1, scalar=-BIG, in1=R.el, op0=ALU.mult, op1=ALU.add))
    first_of(R.el, R.m2, R.oh2, k.tab("desc_exp"), N_EXPERTS)
    d = do(tt(R.m2, R.m2, R.m1, ALU.subtract))
    ex2 = q.act.do(lambda e: e.activation(R.m2, R.m2, ACT.Exp), after=[d])
    chosen = do(tt(R.hot, R.oh1, R.oh2, ALU.add))
    bank = k.banks.take()
    view = bank.tile[:, 0:3 * N_EXPERTS].rearrange("p (a b) -> p a b", a=3)
    earlier, ones = k.tab("earlier"), k.tab("ones")
    step = product(q, bank, [(view[:, 0, :], [(earlier, R.hot[:, 0, :])]),
                             (view[:, 1, :], [(earlier, R.hot[:, 1, :]), (ones, R.hot[:, 0, :])]),
                             (view[:, 2, :], [(ones, R.hot[:, 0, :]), (ones, R.hot[:, 1, :])])], after=[chosen])
    do(red(R.top[:, 0:1], view[:, 2, :], AXX, ALU.max), after=[step])
    most = do(lambda e: e.tensor_copy(k.most[0:1, 0:1], R.top[0:1, 0:1]))
    do(lambda e, view=view: e.scalar_tensor_tensor(out=k.rank, in0=view[:, 0:2, :], scalar=1.0, in1=R.hot, op0=ALU.add, op1=ALU.mult))
    bank.free = [do(ts(k.rank, k.rank, -1.0, None, ALU.add))]

    def weigh():
        do(red(R.gmax, R.gl, AXX, ALU.add), after=[ex])
        do(ts(R.m1, R.m2, 1.0, None, ALU.add), after=[ex2])
        do(tt(R.gmax, R.gmax, R.m1, ALU.mult))
        do(lambda e: e.reciprocal(R.m1, R.gmax))
        do(tt(R.m2, R.m2, R.m1, ALU.mult))
        do(tt(R.oh1, R.oh1, bcast(R.m1, N_EXPERTS), ALU.mult))
        do(tt(R.oh2, R.oh2, bcast(R.m2, N_EXPERTS), ALU.mult))
        do(tt(k.gate_w, R.oh1, R.oh2, ALU.add))

    return Step(q.dve.sem, q.dve.count), most, weigh


def expert_buffers(k):
    A = k.arena
    A.restart()
    b = Tiles()
    b.sel = [A.take(NB, P) for _ in range(2)]
    b.sel_w = [A.take(NB, P) for _ in range(2)]
    b.sel_wT = [A.take(T) for _ in range(3)]
    b.xg = [A.take(KT, P) for _ in range(2)]
    b.silu, b.h, b.hT = A.take(BANK), A.take(BANK), A.take(FT_E, P)
    b.y = [A.take(D) for _ in range(2)]
    b.spill = [k.mixT[:, :, :].rearrange("p k t -> p (k t)"), k.pool_or_distance[:, :]]
    return b


def experts(k, q, buf, ring, ready, weigh=None):
    n_pairs = N_EXPERTS // PAIR
    gate_bank, up_bank, y_banks = k.all_banks[0], k.all_banks[1], k.all_banks[2:4]
    work = Banks(k.all_banks[4:8])
    none = []
    sel_step, sel_w_step, xg_step, wT_step, y_step, comb = {}, {}, {}, {}, {}, {}
    gate_step, h_step = {}, {}

    def select(g):
        i = g % 2
        e0 = slice(PAIR * g, PAIR * g + PAIR)
        after = [xg_step[g - 2][1]] if g >= 2 else list(ready)
        for tb in range(NB):
            out = buf.sel[i][:, tb, :].rearrange("p (a b) -> p a b", a=PAIR)
            q.dve.do(lambda e, out=out, tb=tb: e.tensor_tensor(out, mid_bcast(k.tab("slot_no"), PAIR), bcast(k.rank[:, tb, e0], CAP), ALU.is_equal),
                     after=after, chain=False)
        sel_step[g] = Step(q.dve.sem, q.dve.count)
        if g == 0 and weigh:
            weigh()
        for tb in range(NB):
            out = buf.sel_w[i][:, tb, :].rearrange("p (a b) -> p a b", a=PAIR)
            src = buf.sel[i][:, tb, :].rearrange("p (a b) -> p a b", a=PAIR)
            sel_w_step[g] = q.dve.do(lambda e, out=out, src=src, tb=tb: e.tensor_tensor(out, src, bcast(k.gate_w[:, tb, e0], CAP), ALU.mult),
                                     after=[wT_step[g - 2][0]] if g >= 2 else [])

    def gather(g):
        i = g % 2
        got = []
        for half in range(2):
            bank = work.take()
            view = bank.tile[:, :].rearrange("p (a b) -> p a b", a=4)
            groups = [(view[:, kk, :], [(k.x_tok[:, tb, (4 * half + kk)::KT], buf.sel[i][:, tb, :]) for tb in range(NB)]) for kk in range(4)]
            step = product(q, bank, groups, after=[sel_step[g]] + k.x_ready)
            if g >= 2:
                (q.act if half == 0 else q.dve).wait(gate_step[g - 2])
            got.append(evacuate(k, q, bank, step, buf.xg[i][:, 4 * half:4 * half + 4, :], view, engine="act" if half == 0 else "dve"))
        xg_step[g] = (got, step)
        bank = work.take()
        step = transposes(q, bank, k.ident, [(bank.tile[:, tb * P:(tb + 1) * P], buf.sel_w[i][:, tb, :]) for tb in range(NB)], after=[sel_w_step[g]])
        if g >= 3:
            q.act.wait(comb[g - 3])
        wT_step[g] = (step, evacuate(k, q, bank, step, buf.sel_wT[g % 3], bank.tile[:, 0:T]))

    def paired(bank_of, name, g, halves, per, lhs, n_cols, after):
        for half in range(halves):
            chunks = [ring.next((name, g, half, j)) for j in range(PAIR)]

            def emit(e, half=half, chunks=chunks):
                for kk in range(per):
                    for n in range(n_cols):
                        for j in range(PAIR):
                            r = slice(CAP * j, CAP * j + CAP)
                            ins = e.matmul(bank_of[n].tile[r, :], lhs[:, half * per + kk, r], chunks[j][1][:, kk, BANK * n:BANK * n + BANK],
                                           start=half == 0 and kk == 0, stop=half == halves - 1 and kk == per - 1)
                return ins

            free = [s for b in bank_of for s in b.free] if half == 0 else []
            step = q.pe.do(emit, after=[c[2] for c in chunks] + free + after, chain=False)
            for c in chunks:
                ring.release(c[0], step)
        return step

    def combine(g):
        i = g % 2
        for tb in range(NB):
            for n in range(2):
                bank = work.take()
                cols = slice(BANK * n, BANK * n + BANK)
                step = product(q, bank, [(bank.tile[:, :], [(buf.sel_wT[g % 3][:, tb * P:(tb + 1) * P], buf.y[i][:, cols])])],
                               after=[wT_step[g][1]] + y_step[g])
                got = q.dve.do(lambda e, tb=tb, cols=cols, bank=bank: e.tensor_tensor(k.acc[:, tb, cols], k.acc[:, tb, cols], bank.tile[:, :], ALU.add),
                               after=[step], chain=True)
                bank.free = [got]
        comb[g] = step
        return got

    select(0)
    gather(0)
    for g in range(n_pairs):
        i = g % 2
        gate_s = paired([gate_bank], "gate", g, 2, KT // 2, buf.xg[i], 1, xg_step[g][0])
        up_s = paired([up_bank], "up", g, 2, KT // 2, buf.xg[i], 1, [])
        gate_step[g] = up_s
        if g + 1 < n_pairs:
            select(g + 1)
        a = q.act.do(lambda e: e.activation(buf.silu, gate_bank.tile[:, :], ACT.Silu), after=[gate_s] + ([h_step[g - 1]] if g else none), chain=False)
        gate_bank.free = [a]
        if g:
            q.dve.wait(comb_hT)
        h_step[g] = q.dve.do(lambda e: e.tensor_tensor(buf.h, buf.silu, up_bank.tile[:, :], ALU.mult), after=[a, up_s], chain=False)
        up_bank.free = [h_step[g]]
        if g + 1 < n_pairs:
            gather(g + 1)
        bank = work.take()
        view = bank.tile[:, :].rearrange("p (a b) -> p a b", a=FT_E)
        step = transposes(q, bank, k.ident, [(view[:, f, :], buf.h[:, f::FT_E]) for f in range(FT_E)], after=[h_step[g]])
        comb_hT = step
        if g:
            q.act.wait(down_step)
        hT = evacuate(k, q, bank, step, buf.hT, view)
        if g:
            combine(g - 1)
        down_step = paired(y_banks, "down", g, 2, FT_E // 2, buf.hT, 2, [hT])
        y_step[g] = []
        for n in range(2):
            eng = q.act if n == 0 else q.dve
            if g >= 2:
                eng.wait(comb[g - 2])
            y_step[g].append(evacuate(k, q, y_banks[n], down_step, buf.y[i][:, BANK * n:BANK * n + BANK], engine="act" if n == 0 else "dve"))
    return combine(n_pairs - 1)


def moe(k, q, layer, nc, new_sem, A, mixer_done):
    for tb in range(NB):
        base = q.act.do(lambda e, tb=tb: e.activation(k.acc[:, tb, :], k.x_tok[:, tb, :], ACT.Copy, scale=ALPHA), after=k.x_ready)
    ranked, most, weigh = route(k, q, layer)
    buf = expert_buffers(k)
    k.ring.lend([k.split.free[i] for i in EXTRA_ORDER] + [mixer_done])
    last = experts(k, q, buf, k.ring, [ranked, base], weigh)
    for i, step in zip(EXTRA_ORDER, k.ring.last_reads()):
        k.split.free[i] = [step]
    q.play(nc, [k.ring])
    most_value = nc.values_load(k.most[0:1, 0:1], min_val=0, max_val=T)
    with nc.If(most_value > CAP):
        with nc.Fori(1, (most_value + (CAP - 1)) // CAP):
            over = Engines(new_sem, f"over{layer}")
            ring_sems = [over.sem("slot0"), over.sem("slot1")]
            ring = Ring([t for t in buf.spill], ring_sems, moe_plan(A, layer), over.sp)
            saved = [list(b.free) for b in k.all_banks]
            ready, k.x_ready = k.x_ready, []
            for b in k.all_banks:
                b.free = []
            down = over.dve.do(lambda e: e.tensor_scalar(k.rank, k.rank, -float(CAP), None, ALU.add))
            experts(k, over, buf, ring, [down])
            over.play(nc, [ring])
            nums = sorted(s.num for s in over.sems)
            nc.all_engine_barrier(sems_to_clear=range(nums[0], nums[-1] + 1))
            for b, free in zip(k.all_banks, saved):
                b.free = free
            k.x_ready = ready
    return [lambda: [[last], [last]]] * NB


def build(nc, A, out):
    table, cols = constant_tables()
    with ExitStack() as ctx:
        ctx.enter_context(nc.allow_non_contiguous_dma("small parameters"))

        def sb(name, shape, dt=F32):
            return ctx.enter_context(nc.sbuf_tensor(name, shape, dt))

        def new_sem(name):
            return ctx.enter_context(nc.semaphore(name))

        k = Tiles()
        tables = sb("tables", [P, table.shape[1]])
        k.tab = lambda name: tables[:, cols[name][0]:cols[name][0] + cols[name][1]]
        k.ident = k.tab("ident")
        k.neg_half = k.tab("neg_half")
        k.masks = sb("level_masks", [P, 2 * len(LEVELS) + 1, P], U8)
        k.x_tok, k.acc = sb("x_tok", [P, NB, D]), sb("acc", [P, NB, D])
        k.mixT = sb("mixT", [P, KT, T])
        k.xh, k.xl = (sb(name, [P, KT, T], F32R) for name in ("xT_high", "xT_low"))
        extra_slots = [sb(f"w_parts{i}", [P, SLOT]) for i in range(PARTS)]
        parts_at = nc.sbuf_base - 4 * SLOT * PARTS
        k.split = Splitter(*[[nc.alloc_sbuf_tensor_at(f"w_{x}{i}", [P, PART], F32R, offset=parts_at + 4 * (SLOT * i + PART * j))
                              for i in range(PARTS)] for j, x in enumerate(("high", "low"))])
        k.norm_gb = sb("norm_gb", [P, 2, D])
        k.bn, k.mv = sb("bn", [P, NB, 12]), sb("mv", [P, NB, 2])
        k.ve, k.rstd = (sb(name, [P, NB]) for name in ("var_eps", "rstd"))
        k.hbn, k.hmv, k.hrs = sb("head_bn", [P, 8, 6]), sb("head_mv", [P, 8, 2]), sb("head_rs", [P, 16])
        k.tags = sb("softmax_stats", [P, 4, 8])
        k.rot_tmp = sb("rot_tmp", [P, 2 * T])
        k.junk = k.acc[:, 0, 512:512 + T]
        k.refs = [sb(f"level_refs{i}", [P, 3, 2, 4])[:, :, :, :] for i in range(2)]
        k.rank, k.gate_w = (sb(name, [P, NB, N_EXPERTS])[:, :, :] for name in ("rank", "gate_w"))
        k.most = sb("most", [1, 1], I32)
        R = k.route = Tiles()
        R.gl, R.goh = (sb(name, [P, NB, N_GROUPS])[:, :, :] for name in ("group_logits", "group_hot"))
        R.el, R.oh1, R.oh2, R.hot = (sb(name, [P, NB, N_EXPERTS])[:, :, :] for name in ("expert_logits", "first_hot", "second_hot", "chosen_hot"))
        R.gmax, R.m1, R.m2, R.top = (sb(name, [P, NB])[:, :] for name in ("group_max", "first_max", "second_max", "place"))
        k.ret_decay, k.neg_rate = sb("ret_decay", [P, 2 * HEADS]), sb("neg_rate", [P, 2 * HEADS])
        k.lqk, k.lam = sb("lqk", [P, 4, DIFF_D]), sb("lam", [P, 4])
        k.subln, k.gla_norm, k.hgrn_g = sb("subln", [P, HD]), sb("gla_norm", [P, HD]), sb("hgrn_g", [P, DEPTH, HD])
        k.q_norm, k.kv_norm = sb("q_norm", [P, 2]), sb("kv_norm", [P, 1])
        k.gla_b = sb("gla_b", [P, 2, 2])
        k.pool_scale = sb("pool_scale", [P, DEPTH, 4])
        at = cols["dif_cos"][0]
        k.pool_w = tables[:, at:at + DEPTH * 4 * P].rearrange("p (l g n) -> p l g n", l=DEPTH, g=4)
        k.lb_param, k.lb_work = sb("lb_param", [P, DEPTH, 4]), sb("lb_work", [P, 4, 4])
        k.b_grp, k.b_exp = sb("b_grp", [P, DEPTH, N_GROUPS]), sb("b_exp", [P, DEPTH, N_EXPERTS])
        slots = [sb(f"ring{i}", [P, SLOT]) for i in range(RING)]
        k.pool_or_distance = sb("wide_tables", [P, NB * 4 * T])
        k.distance = k.pool_or_distance[:, 0:2 * NB * T].rearrange("p (w s t) -> p w s t", w=2, s=NB)
        k.pool_mat = k.pool_or_distance[:, :].rearrange("p (s g t) -> p s g t", s=NB, g=4)
        k.w_uq = k.pool_or_distance[:, 0:768].rearrange("p (j n) -> p j n", j=2)
        k.w_ukv = k.pool_or_distance[:, 768:1536]
        k.gla_w2 = k.pool_or_distance[:, 1536:1792]
        words = nc.sbuf_bytes_remaining // 4 // 8 * 8 - 8
        arena = sb("arena", [P, words])
        arena_at = nc.sbuf_base - 4 * words
        k.arena = Arena(arena, words)
        k.ffn_tmp = [arena[:, 2 * T * i:2 * T * (i + 1)].rearrange("p (a b) -> p a b", a=2) for i in range(2)]
        k.hid_high, k.hid_low = (nc.alloc_sbuf_tensor_at(f"hidden_{x}", [P, HIDDEN, T], F32R, offset=arena_at + 4 * T * (4 + HIDDEN * i))
                                 for i, x in enumerate(("high", "low")))
        k.all_banks = [Bank(ctx.enter_context(nc.psum_tensor(f"bank{i}", [P, BANK], F32))) for i in range(8)]
        k.banks, k.banks_o, k.banks_b = Banks(k.all_banks[0:2]), Banks(k.all_banks[2:4]), Banks(k.all_banks[4:8])

        q = Engines(new_sem, "main")
        extra_slots = [extra_slots[i] for i in EXTRA_ORDER] + [arena[:, words - SLOT:words]]
        slots += extra_slots
        k.ring = Ring(slots, [new_sem(f"slot{i}_loaded") for i in range(len(slots))], weight_plan(A), q.sp, extra=len(extra_slots))
        par_sem, wide_sem, mask_sem, out_sem = (new_sem(n) for n in ("params_loaded", "wide_loaded", "masks_loaded", "out_stored"))
        x_sem, tab_sem = [new_sem(f"x_block{b}_loaded") for b in range(NB)], [new_sem(f"tables{i}_loaded") for i in range(4)]
        k.norm_sem, k.router_sem = new_sem("norm_loaded"), new_sem("router_loaded")
        k.router = [(A["moe_w_grp"][i], A["moe_w_exp"][i]) for i in range(DEPTH)]
        k.norm_free, k.norm_no = [], 0
        k.norm_rows = []
        for layer in range(DEPTH):
            k.norm_rows += [(A["ln1_g"][layer], A["ln1_b"][layer]), (A["ln2_g"][layer], A["ln2_b"][layer])]
        for layer in range(DEPTH):
            k.norm_rows += [(A["ln_g_2"][layer, i], A["ln_b_2"][layer, i]) for i in range(3)]

        x_here = [q.sp.dma(k.x_tok[:, b, :], A["x"][0, b * P:(b + 1) * P, :], x_sem[b], 16) for b in range(NB)]
        first, middle, second = (cols[name][0] for name in ("dif_cos", "ret_cos", "ones"))
        ident_here = q.act.dma(tables[:, 0:first], A["tables"][:, 0:first], tab_sem[0], 16)
        k.rotary_here = {"dif": q.act.dma(tables[:, first:middle], A["tables"][:, first:middle], tab_sem[1], 16)}
        k.ring.load()
        k.rotary_here["ret"] = q.sp.dma(tables[:, middle:second], A["tables"][:, middle:second], tab_sem[2], 16)
        small = [
            (k.ret_decay[:, 0:HEADS], A["ev_ret_decay_f"][0].partition_broadcast(P)),
            (k.ret_decay[:, HEADS:2 * HEADS], A["ev_ret_decay_b"][0].partition_broadcast(P)),
            (k.subln[:, :], A["ev_subln"][0].partition_broadcast(P)),
            (k.gla_norm[:, :], A["od_gla_norm"][0].partition_broadcast(P)),
            (k.q_norm[:, :], A["od_q_norm"][0].rearrange("(j p) -> p j", p=P)),
            (k.kv_norm[:, :], A["od_kv_norm"].rearrange("a p -> p a")),
            (k.gla_b[:, 0, :], A["od_gla_b_f"][0].rearrange("(j p) -> p j", p=P)),
            (k.gla_b[:, 1, :], A["od_gla_b_b"][0].rearrange("(j p) -> p j", p=P)),
        ]
        for i, name in enumerate(("ev_lq1", "ev_lk1", "ev_lq2", "ev_lk2")):
            small.append((k.lqk[:, i, :], A[name][0].partition_broadcast(P)))
        for i in range(DEPTH):
            small += [
                (k.hgrn_g[:, i, :], A["hgrn_norm_g_2"][i].partition_broadcast(P)),
                (k.pool_scale[:, i, :], A["pool_scale_2"][i].rearrange("(g p) -> p g", p=P)),
                (k.lb_param[:, i, :], A["lb_param_2"][i].rearrange("(g p) -> p g", p=P)),
                (k.b_grp[:, i, :], A["moe_b_grp"][i].partition_broadcast(P)),
                (k.b_exp[:, i, :], A["moe_b_exp"][i].partition_broadcast(P)),
            ]
        for dst, src in small:
            q.sp.dma(dst, src, par_sem, 16 * len(small))
        params = k.params = Step(par_sem, 16 * len(small))
        k.distance_here = q.sp.dma(k.pool_or_distance[:, 0:2 * NB * T], A["distance"], wide_sem, 16)
        k.tables_here = q.sp.dma(tables[:, second:], A["tables"][:, second:], tab_sem[3], 16)
        load_norm(k, q, 0)

        q.pe.wait(ident_here)
        q.pool.wait(ident_here)
        k.x_ready = x_here
        to_feature_major(k, q, k.x_ready)

        k.split.prefetch(k, q)
        prefetch = lambda: k.split.prefetch(k, q)
        layer_norm(k, q, retention_diff_mixer(k, q), halves=(1,))
        for queue in (q.pe, q.dve, q.act, q.pool):
            queue.wait(k.tables_here)
        layer_norm(k, q, moe(k, q, 0, nc, new_sem, A, after_everything(q)), between=prefetch)
        for dst, src in ((k.w_uq, A["od_w_uq"][0].rearrange("(j p) n -> p j n", p=P)), (k.w_ukv, A["od_w_ukv"][0]),
                         (k.gla_w2[0:GATE_RANK, :], A["od_gla_w2_f"][0]), (k.gla_w2[32:32 + GATE_RANK, :], A["od_gla_w2_b"][0])):
            q.act.dma(dst, src, wide_sem, 16 * 5)
        k.params = Step(wide_sem, 16 * 5)
        n_masks = 2 * len(LEVELS) + 1
        wide_masks = k.mixT[:, :, :].rearrange("p k t -> p (k t)")[:, 0:n_masks * P].rearrange("p (a b) -> p a b", a=n_masks)
        masks_here = q.act.dma(wide_masks, A["masks"], mask_sem, 16)
        k.masks_made = q.pool.do(lambda e: e.tensor_copy(k.masks[:, :, :], wide_masks), after=[masks_here])
        layer_norm(k, q, mla_gla_mixer(k, q), halves=(1,))
        k.params = params
        mixed = moe(k, q, 1, nc, new_sem, A, after_everything(q))
        weights = FfnWeights(k, q)
        layer_norm(k, q, mixed, between=lambda: weights.fill(2), after=weights.fill)
        k.pool_here = q.act.dma(k.pool_or_distance[:, :], A["pool_mat"], wide_sem, 16 * 8, after=[Step(q.dve.sem, q.dve.count)])
        for i in range(DEPTH):
            q.act.dma(k.pool_w[:, i, :, :], A["pool_w_2"][i].rearrange("g c d -> c g d"), wide_sem, 16 * 8)
        for layer in range(DEPTH):
            layer_norm(k, q, ffn(k, q, weights), before=prefetch)
            mixed = pool_hgrn_mixer(k, q, layer)
            weights = FfnWeights(k, q)
            layer_norm(k, q, mixed, halves=(1,), before=lambda: weights.fill(2), after=weights.fill)
            mixed = ffn(k, q, weights)
            if layer + 1 < DEPTH:
                weights = FfnWeights(k, q)
                layer_norm(k, q, mixed, before=lambda: weights.fill(2), after=weights.fill)
            else:
                layer_norm(k, q, mixed)
        rows_out = out.rearrange("a (b p) d -> p (a b) d", p=P)
        for tb in range(NB):
            stored = q.act.dma(rows_out[:, tb, :], k.x_tok[:, tb, :], out_sem, 16 * NB, after=[k.x_ready[tb]])
        q.act.wait(stored)
        q.play(nc, [k.ring])
        assert k.ring.asked == k.ring.loaded == len(k.ring.plan)


_INS = ['x', 'ev_w_in', 'ev_ret_decay_f', 'ev_ret_decay_b', 'ev_lq1', 'ev_lk1', 'ev_lq2', 'ev_lk2', 'ev_subln', 'ev_w_out',
        'od_w_in', 'od_q_norm', 'od_w_uq', 'od_kv_norm', 'od_w_ukv', 'od_gla_w2_f', 'od_gla_b_f', 'od_gla_w2_b', 'od_gla_b_b',
        'od_gla_norm', 'od_w_out', 'ln1_g', 'ln1_b', 'ln2_g', 'ln2_b', 'moe_w_grp', 'moe_b_grp', 'moe_w_exp', 'moe_b_exp',
        'moe_w_gate', 'moe_w_up', 'moe_w_down', 'w_in_2', 'pool_w_2', 'pool_scale_2', 'lb_param_2', 'hgrn_norm_g_2', 'w_out_2',
        'ffn1_gate_2', 'ffn1_up_2', 'ffn1_down_2', 'ffn2_gate_2', 'ffn2_up_2', 'ffn2_down_2', 'ln_g_2', 'ln_b_2']


def kernel(**inputs):
    import concourse.bacc as bacc
    from concourse.bass_utils import run_bass_kernel_spmd

    arrays = {name: np.ascontiguousarray(inputs[name]) for name in _INS}
    arrays["tables"] = constant_tables()[0]
    arrays["masks"] = level_masks()
    arrays["distance"] = distance_tables().reshape(P, -1)
    arrays["pool_mat"] = pool_tables().reshape(P, -1)
    nc = bacc.Bacc("TRN2", target_bir_lowering=False, num_devices=1)
    feed, A = {}, {}
    for name, a in arrays.items():
        feed[f"in_{name}"] = a
        A[name] = nc.dram_tensor(f"in_{name}", a.shape, mybir.dt.from_np(a.dtype), kind="ExternalInput").ap()
    out = nc.dram_tensor("out_0", (1, T, D), F32, kind="ExternalOutput").ap()
    build(nc, A, out)
    r = run_bass_kernel_spmd(nc, [feed], core_ids=[0])
    return r.results[0]["out_0"]
```
